# Optimizing a Trainium2 kernel written in Bass

```python
import math
import jax, jax.numpy as jnp
from jax import lax
import numpy as np

D_MODEL = 1024
BATCH = 1
SEQ = 256
DEPTH = 2

GRID_W = 64
CTX_LEN = 256
MIX_WIDTH = D_MODEL
RWKV_WIDTH = MIX_WIDTH // 2
CONV_WIDTH = MIX_WIDTH - RWKV_WIDTH
HEAD_SIZE = 64
RWKV_HEADS = RWKV_WIDTH // HEAD_SIZE
DECAY_LORA = 64
ICLR_LORA = 64
GATE_LORA = 128
CONV_K = 3
D_FF = 7 * D_MODEL // 2
N_EXPERTS = 8
TOP_K = 2
N_DENSE = (DEPTH + 1) // 2
N_MOE = DEPTH // 2
DN_ALPHA = (2 * DEPTH) ** 0.25
DN_BETA = (8 * DEPTH) ** -0.25
LN_EPS = 1e-5
GN_EPS = 64e-5
NORM_EPS = 1e-12
PROJ_SIZES = (RWKV_WIDTH, RWKV_WIDTH, RWKV_WIDTH, 2 * DECAY_LORA, 2 * ICLR_LORA, GATE_LORA, CONV_WIDTH, CONV_WIDTH, CONV_WIDTH)
PROJ_COLS = sum(PROJ_SIZES)
SPLIT_IDX = tuple(sum(PROJ_SIZES[:i + 1]) for i in range(len(PROJ_SIZES) - 1))
VALUE_GROUPS = (2, 8)

kernel_name = "hybrid_rwkv7_shortconv_moe_deepnorm_dit"

def layer_norm(x, g, b):
    xf = x.astype(jnp.float32)
    mu = jnp.mean(xf, -1, keepdims=True)
    var = jnp.mean(jnp.square(xf - mu), -1, keepdims=True)
    return ((xf - mu) * lax.rsqrt(var + LN_EPS)).astype(x.dtype) * g + b

def heads(t):
    return t.reshape(t.shape[:-1] + (RWKV_HEADS, HEAD_SIZE))

def rwkv_prep(r, k, v, wd, ad, w0, w2, a0, a2, k_k, k_a):
    nb, n = r.shape[:2]
    wd = wd.reshape(nb, n, 2, DECAY_LORA)
    ad = ad.reshape(nb, n, 2, ICLR_LORA)
    w_log = -jax.nn.softplus(-(w0 + jnp.einsum("bldr,drc->bldc", jnp.tanh(wd), w2))) - 0.5
    decay = jnp.exp(-jnp.exp(w_log.astype(jnp.float32)))
    a = jax.nn.sigmoid(a0 + jnp.einsum("bldr,drc->bldc", ad, a2))
    kk = heads(k * k_k).astype(jnp.float32)
    kk = kk / jnp.maximum(jnp.sqrt(jnp.sum(kk * kk, -1, keepdims=True)), NORM_EPS)
    k_dir = heads(k[:, :, None, :] * (1 + (a - 1) * k_a))
    b_vec = kk[:, :, None] * heads(a)
    return (heads(r), k_dir, heads(v), heads(decay), kk, b_vec)

def wkv_scan(s0, terms, d, reverse, readout):
    r, k, v, w, kk, b = terms
    tm = lambda t: jnp.moveaxis(t.astype(jnp.float32), 1, 0)
    xs = (tm(w[:, :, d]), tm(k[:, :, d]), tm(v), tm(kk), tm(b[:, :, d]))
    if readout:
        xs = xs + (tm(r),)

    def step(s, inp):
        w_t, k_t, v_t, kk_t, b_t = inp[:5]
        sa = jnp.einsum("bhvk,bhk->bhv", s, -kk_t)
        s = s * w_t[:, :, None, :] + sa[..., None] * b_t[:, :, None, :] + v_t[..., None] * k_t[:, :, None, :]
        y = jnp.einsum("bhvk,bhk->bhv", s, inp[5]) if readout else None
        return s, y

    s_fin, ys = lax.scan(step, s0, xs, reverse=reverse)
    return s_fin, (jnp.moveaxis(ys, 0, 1) if readout else None)

def rwkv_readout(y, terms, gd, r_k, g2, lnx_g, lnx_b):
    r, k, v = terms[:3]
    mu = jnp.mean(y, -1, keepdims=True)
    var = jnp.mean(jnp.square(y - mu), -1, keepdims=True)
    yn = (y - mu) * lax.rsqrt(var + GN_EPS)
    bonus = jnp.sum(jnp.sum(r[:, :, None] * k * r_k, -1, keepdims=True) * v[:, :, None], axis=2)
    out = yn.reshape(y.shape[:2] + (RWKV_WIDTH,)) * lnx_g + lnx_b + bonus.reshape(y.shape[:2] + (RWKV_WIDTH,))
    g = jax.nn.sigmoid(gd) @ g2
    return (out * g).astype(gd.dtype)

def short_conv(u, w):
    pad = CONV_K // 2
    n = u.shape[-2]
    up = jnp.pad(u, [(0, 0)] * (u.ndim - 2) + [(pad, pad), (0, 0)])
    out = up[..., 0:n, :] * w[0]
    for j in range(1, CONV_K):
        out = out + up[..., j:j + n, :] * w[j]
    return out

def conv_branch(cb, cc, ch, conv_w, rows):
    u = cc * ch
    if rows is not None:
        u = u.reshape(u.shape[0], rows, GRID_W, u.shape[-1])
    return cb * short_conv(u, conv_w).reshape(cb.shape)

def token_mixer(hl, hc, rows, w_in, w0, w2, a0, a2, k_k, k_a, r_k, g2, lnx_g, lnx_b, conv_w, w_out, ctx_out):
    pl = jnp.split(hl @ w_in, SPLIT_IDX, axis=-1)
    pc = jnp.split(hc @ w_in, SPLIT_IDX, axis=-1)
    lat = rwkv_prep(pl[0], pl[1], pl[2], pl[3], pl[4], w0, w2, a0, a2, k_k, k_a)
    cx = rwkv_prep(pc[0], pc[1], pc[2], pc[3], pc[4], w0, w2, a0, a2, k_k, k_a)
    s0 = jnp.zeros((hl.shape[0], RWKV_HEADS, HEAD_SIZE, HEAD_SIZE), jnp.float32)
    y_lat, y_ctx = 0.0, 0.0
    for d in range(2):
        s_ctx, yc = wkv_scan(s0, cx, d, d == 1, ctx_out)
        _, yl = wkv_scan(s_ctx, lat, d, d == 1, True)
        y_lat = y_lat + yl
        if ctx_out:
            y_ctx = y_ctx + yc
    out_l = jnp.concatenate([rwkv_readout(y_lat, lat, pl[5], r_k, g2, lnx_g, lnx_b),
                             conv_branch(pl[6], pl[7], pl[8], conv_w, rows)], axis=-1) @ w_out
    if not ctx_out:
        return out_l, None
    out_c = jnp.concatenate([rwkv_readout(y_ctx, cx, pc[5], r_k, g2, lnx_g, lnx_b),
                             conv_branch(pc[6], pc[7], pc[8], conv_w, None)], axis=-1) @ w_out
    return out_l, out_c

def swiglu(x, w1, w3, w2):
    return (jax.nn.silu(x @ w1) * (x @ w3)) @ w2

def moe_ffn(x, w_router, b_router, w1, w3, w2):
    logits = (x @ w_router + b_router).astype(jnp.float32)
    top_v, top_i = lax.top_k(logits, TOP_K)
    top_w = jax.nn.softmax(top_v, axis=-1)
    gate = jnp.sum(jax.nn.one_hot(top_i, N_EXPERTS, dtype=jnp.float32) * top_w[..., None], axis=-2).astype(x.dtype)
    out = gate[..., 0:1] * swiglu(x, w1[0], w3[0], w2[0])
    for e in range(1, N_EXPERTS):
        out = out + gate[..., e:e + 1] * swiglu(x, w1[e], w3[e], w2[e])
    return out

def channel_mixer(h, l, ffn_w1, ffn_w3, ffn_w2, router_w, router_b, moe_w1, moe_w3, moe_w2):
    i = l // 2
    if l % 2 == 0:
        return swiglu(h, ffn_w1[i], ffn_w3[i], ffn_w2[i])
    return moe_ffn(h, router_w[i], router_b[i], moe_w1[i], moe_w3[i], moe_w2[i])

def setup_inputs(seed: int = 0) -> dict:
    key = jax.random.key(seed)
    ks = iter(jax.random.split(key, 40))
    D = D_MODEL
    L = DEPTH
    nrm = lambda shape, s: jax.random.normal(next(ks), shape, jnp.float32) * s
    col_scale = jnp.concatenate([jnp.full((n,), DN_BETA if i in VALUE_GROUPS else 1.0, jnp.float32)
                                 for i, n in enumerate(PROJ_SIZES)])
    return {
        "x": nrm((BATCH, SEQ, D), 1.0),
        "c": nrm((BATCH, D), 1.0),
        "ctx": nrm((BATCH, CTX_LEN, D), 1.0),
        "c_ctx": nrm((D,), 1.0),
        "w_mod": nrm((L, D, 6 * D), 0.5 * D ** -0.5),
        "b_mod": nrm((L, 6 * D), 0.02),
        "w_in": nrm((L, D, PROJ_COLS), D ** -0.5) * col_scale,
        "rk_w0": -6.0 + 5.0 * jax.random.uniform(next(ks), (L, 2, RWKV_WIDTH), jnp.float32),
        "rk_w2": nrm((L, 2, DECAY_LORA, RWKV_WIDTH), 0.1 * DECAY_LORA ** -0.5),
        "rk_a0": nrm((L, 2, RWKV_WIDTH), 0.1),
        "rk_a2": nrm((L, 2, ICLR_LORA, RWKV_WIDTH), 0.1 * ICLR_LORA ** -0.5),
        "rk_kk": 0.85 + nrm((L, RWKV_WIDTH), 0.02),
        "rk_ka": 1.0 + nrm((L, RWKV_WIDTH), 0.02),
        "rk_rk": nrm((L, RWKV_HEADS, HEAD_SIZE), 0.1),
        "rk_g2": nrm((L, GATE_LORA, RWKV_WIDTH), GATE_LORA ** -0.5),
        "rk_lnx_g": 1.0 + nrm((L, RWKV_WIDTH), 0.02),
        "rk_lnx_b": nrm((L, RWKV_WIDTH), 0.02),
        "conv_w": nrm((L, CONV_K, CONV_WIDTH), CONV_K ** -0.5),
        "w_out": nrm((L, MIX_WIDTH, D), MIX_WIDTH ** -0.5 * DN_BETA),
        "ln1_g": 1.0 + nrm((L, D), 0.02),
        "ln1_b": nrm((L, D), 0.02),
        "ln2_g": 1.0 + nrm((L, D), 0.02),
        "ln2_b": nrm((L, D), 0.02),
        "ffn_w1": nrm((N_DENSE, D, D_FF), D ** -0.5),
        "ffn_w3": nrm((N_DENSE, D, D_FF), D ** -0.5),
        "ffn_w2": nrm((N_DENSE, D_FF, D), D_FF ** -0.5 * DN_BETA),
        "router_w": nrm((N_MOE, D, N_EXPERTS), D ** -0.5),
        "router_b": nrm((N_MOE, N_EXPERTS), 0.01),
        "moe_w1": nrm((N_MOE, N_EXPERTS, D, D_FF), D ** -0.5),
        "moe_w3": nrm((N_MOE, N_EXPERTS, D, D_FF), D ** -0.5),
        "moe_w2": nrm((N_MOE, N_EXPERTS, D_FF, D), D_FF ** -0.5 * DN_BETA),
    }

def reference(x, c, ctx, c_ctx, w_mod, b_mod, w_in, rk_w0, rk_w2, rk_a0, rk_a2, rk_kk, rk_ka, rk_rk, rk_g2,
              rk_lnx_g, rk_lnx_b, conv_w, w_out, ln1_g, ln1_b, ln2_g, ln2_b, ffn_w1, ffn_w3, ffn_w2,
              router_w, router_b, moe_w1, moe_w3, moe_w2):
    rows = x.shape[1] // GRID_W
    n_ctx = ctx.shape[1]
    xl, xc = x, ctx
    for l in range(DEPTH):
        last = l == DEPTH - 1
        ml = jnp.split((jax.nn.silu(c) @ w_mod[l] + b_mod[l])[:, None, :], 6, axis=-1)
        mc = jnp.split(jax.nn.silu(c_ctx) @ w_mod[l] + b_mod[l], 6, axis=-1)
        mix_l, mix_c = token_mixer(xl * (1 + ml[1]) + ml[0], xc * (1 + mc[1]) + mc[0], rows,
                                   w_in[l], rk_w0[l], rk_w2[l], rk_a0[l], rk_a2[l], rk_kk[l], rk_ka[l],
                                   rk_rk[l], rk_g2[l], rk_lnx_g[l], rk_lnx_b[l], conv_w[l], w_out[l], not last)
        xl = layer_norm(DN_ALPHA * xl + ml[2] * mix_l, ln1_g[l], ln1_b[l])
        if last:
            f_l = channel_mixer(xl * (1 + ml[4]) + ml[3], l, ffn_w1, ffn_w3, ffn_w2,
                                router_w, router_b, moe_w1, moe_w3, moe_w2)
        else:
            xc = layer_norm(DN_ALPHA * xc + mc[2] * mix_c, ln1_g[l], ln1_b[l])
            h = jnp.concatenate([xc * (1 + mc[4]) + mc[3], xl * (1 + ml[4]) + ml[3]], axis=1)
            f = channel_mixer(h, l, ffn_w1, ffn_w3, ffn_w2, router_w, router_b, moe_w1, moe_w3, moe_w2)
            xc = layer_norm(DN_ALPHA * xc + mc[5] * f[:, :n_ctx], ln2_g[l], ln2_b[l])
            f_l = f[:, n_ctx:]
        xl = layer_norm(DN_ALPHA * xl + ml[5] * f_l, ln2_g[l], ln2_b[l])
    return xl


_drawn_inputs = setup_inputs


def setup_inputs(seed=0):
    import zlib

    import numpy as np

    out = dict(_drawn_inputs(seed))
    spreads = {}
    factors = {'ctx': 2.701,
     'c_ctx': 4.372,
     'b_mod': 4.439,
     'rk_w2': 8.0,
     'rk_a0': 8.0,
     'rk_a2': 8.0,
     'rk_kk': 8.0,
     'rk_ka': 8.0,
     'rk_lnx_g': 40.772,
     'rk_lnx_b': 42.703,
     'router_b': 38.407}
    for name, (base, spread) in spreads.items():
        noise = np.random.default_rng([zlib.crc32(name.encode()), seed]).standard_normal(out[name].shape)
        drawn = base * np.exp(spread * noise) if base else spread * noise
        out[name] = __import__('jax').numpy.asarray(drawn.astype(out[name].dtype))
    for name, factor in factors.items():
        out[name] = (out[name] * factor).astype(out[name].dtype)
    return out
```

```python
import concourse.bass as bass
from concourse import mybir
from contextlib import ExitStack


def hybrid_kernel(nc, x, c, ctx, c_ctx, w_mod, b_mod, w_in, rk_w0, rk_w2, rk_a0, rk_a2, rk_kk, rk_ka, rk_rk, rk_g2,
                  rk_lnx_g, rk_lnx_b, conv_w, w_out, ln1_g, ln1_b, ln2_g, ln2_b, ffn_w1, ffn_w3, ffn_w2,
                  router_w, router_b, moe_w1, moe_w3, moe_w2, out):
    fp32 = mybir.dt.float32
    i32 = mybir.dt.int32
    f32r = mybir.dt.float32r
    ALU = mybir.AluOpType
    ACT = mybir.ActivationFunctionType
    AX = mybir.AxisListType

    P = 128
    L = w_mod.shape[0]
    D = x.shape[2]
    KD = D // P
    TC, TL = ctx.shape[1], x.shape[1]
    T = TC + TL
    W = rk_kk.shape[1]
    NP = W // P
    HS = 64
    NH = W // HS
    NT = T // P
    GRID = 64
    FF = ffn_w1.shape[2]
    NE = moe_w1.shape[1]
    DECAY = 0.6065306597126334
    ALPHA = float((2 * L) ** 0.25)
    LN_EPS, GN_EPS = 1e-5, 64e-5
    RING = 4
    UNIT = 2048
    MRING = 7
    MSPLIT = 3
    SLOTS = P
    NITEM = NE + TL * 2 // SLOTS
    BIG = 1.0e6

    es = ExitStack()
    with es:
        def sb(name, shape, dt=fp32):
            return es.enter_context(nc.sbuf_tensor(name, shape, dt))

        sems = {}

        def sem(name):
            if name not in sems:
                sems[name] = es.enter_context(nc.semaphore(name))
            return sems[name]

        def wait(eng, name, value):
            if isinstance(value, int) and value <= 0:
                return
            eng.wait_ge(sem(name), value)

        mean_w = sb("mean_w", [P, P])
        keep = sb("keep", [P, 3, P])
        ident, heads, ones_t = keep[:, 0, :], keep[:, 1, :], keep[:, 2, :]
        tri = sb("tri", [P, 4, P])
        level = sb("level", [P, 7, P])
        par = sb("par", [P, L, P])
        ccol = sb("ccol", [P, 2 * KD])
        csig = sb("csig", [P, 2 * KD])
        cs = sb("cs", [P, 2 * KD + 62])
        one = 2 * KD + 30
        mc = sb("mc", [P, L, 2, 6 * KD])
        one_ka = sb("one_ka", [P, L, NP])
        qm = sb("qm", [P, 2 * NP * NT])
        qt = sb("qt", [P, 2 * NP * NT])
        e1 = sb("e1", [P, 2, NP, NT])
        e2 = sb("e2", [P, 2, NP, NT])
        fac = sb("fac", [P, 2, NP, 4])
        COLS = {}
        at = 0
        for nm, n in (("b_mod", 6 * KD), ("w0", 2 * NP), ("a0", 2 * NP), ("kk", NP), ("ka", NP), ("rk", NP),
                      ("lnxg", NP), ("lnxb", NP), ("conv", 3 * NP), ("ln1g", KD), ("ln1b", KD), ("ln2g", KD),
                      ("ln2b", KD)):
            COLS[nm] = at
            at += n
        assert at == P

        def pcol(l, nm, i=0):
            return par[:, l, COLS[nm] + i:COLS[nm] + i + 1]

        o_x = 0
        o_hb = o_x + KD * T
        o_mix = o_hb + 2 * NP * NT * (P + 1)
        o_ring = o_mix + KD * T
        o_rest = o_ring + 6 * UNIT
        SIZE = 49968
        arena = sb("arena", [P, SIZE])

        arena_at = nc.sbuf_base - 4 * SIZE

        def cut(name, off, *dims):
            t = nc.alloc_sbuf_tensor_at(name, [P] + list(dims), f32r, offset=arena_at + 4 * off)
            return t[:]

        def area(off, *dims):
            n = 1
            for d in dims:
                n *= d
            assert off + n <= SIZE, (off, n)
            v = arena[:, off:off + n]
            if len(dims) == 1:
                return v
            names = "abcdef"[:len(dims)]
            return v.rearrange(f"p ({' '.join(names)}) -> p {' '.join(names)}", **dict(zip(names, dims)))

        same = area(o_rest + 8192, 8, P)
        X = area(o_x, KD, T)
        HB = area(o_hb, KD, T)
        Q = area(o_hb, 2, NP, NT, P + 1)
        Qflat = area(o_hb, 2 * NP * NT, P + 1)
        MIX = area(o_mix, KD, T)
        xrows = area(o_mix, NT, D)
        w2z = area(o_mix, 2, 2, W)
        g2 = area(o_mix, W)
        rt = area(o_mix + 512, 2, NP, P)
        o = o_rest
        R = area(o, NP, T)
        K = area(o + 2048, NP, T)
        VTK = area(o + 2048, NT, NP, P)
        V = area(o + 4096, NP, T)
        KKN = area(o + 6144, NP, T)
        KDIR = area(o + 8192, 2, NP, T)
        BV = area(o + 12288, 2, NP, T)
        CB = area(o + 16384, NP, T)
        Y = area(o + 16384, NP, T)
        CC = area(o + 18432, NP, T)
        U = area(o + 20480, NP, T)
        GD = area(o + 22528, T)
        WD = area(o + 23040, T)
        AD = area(o + 23552, T)
        o_tmp = o + 24064
        tmp = area(o_tmp, 2, T)
        o_stage = o + 18432
        EX = area(o_stage, 3, NP, P)
        BS = area(o_stage + 1536, NP, P)
        KS = area(o_stage + 2048, NP, P)
        AS = area(o_stage + 2560, NP, P)
        VS = area(o_stage + 3072, NP, P)
        MI = area(o_stage + 3584, NH, HS)
        ZR = area(o + 23040, NP, 4, P)
        MC = area(o + 23040 + 2048, NP, HS)
        mt = area(o_mix + 1536, NP, HS)
        wk = []
        for q in range(2):
            b = o_ring + q * 6144
            names = {}
            for i, nm in enumerate(("LT", "TT", "T", "XS", "XA", "RB", "AK", "RK")):
                names[nm] = area(b + 512 * i, 4, P)
            names["UW"], names["YW"] = names["LT"], names["T"]
            names["LM"] = area(b + 4096, 2, 4, P)
            names["BT"] = area(b + 5120, 2, P)
            names["KT"] = area(b + 5376, 2, P)
            names["GT"] = area(b + 5632, 2, HS)
            wk.append(names)
        o_ln = SIZE - 2048
        SQ = area(o_ln, 2, T)
        RSTD = area(o_ln + 1024, T)
        mrow = sb("mrow", [P, 512])
        par_rows = area(o_rest, P)
        crow = area(o_rest + P, P)[0:2 * KD]
        RSQ = area(o + 12288, NP, T)
        RTB = area(o + 14336, NP, T)
        RRS = area(o + 2048, NP, T)
        FS = area(o + 16384, 2, T)
        FP = area(o + 17408, 2, T)
        FACC = area(o + 18432, KD, T)

        HT = area(o_ln, 2, T)
        HH = [cut(f"h_hi{k}", o_hb + k * T, T) for k in range(KD)]
        HL = [cut(f"h_lo{k}", o + 8192 + k * T, T) for k in range(KD)]
        GH = [cut(f"g_hi{f}", o + f * T, T) for f in range(4)]
        GL = [cut(f"g_lo{f}", o + 2048 + f * T, T) for f in range(4)]
        WH = [cut(f"w_hi{i}", off, UNIT) for i, off in enumerate((o_ring + RING * UNIT, o + 12288))]
        WL = [cut(f"w_lo{i}", off + UNIT, UNIT) for i, off in enumerate((o_ring + RING * UNIT, o + 12288))]

        bank = [es.enter_context(nc.psum_tensor(f"bank{i}", [P, 512], fp32)) for i in range(8)]

        def pk(b, *dims):
            names = "abcdef"[:len(dims)]
            n = 1
            for d in dims:
                n *= d
            return bank[b][:, 0:n].rearrange(f"p ({' '.join(names)}) -> p {' '.join(names)}", **dict(zip(names, dims)))

        units = []
        index = {}

        splits = []

        def unit(key, src, nk, nm, free):
            index[key] = len(units)
            if key[0] != "mod":
                splits.append((key, free))
                free = ("w_lo", len(splits))
            units.append((src, nk, nm, (free,)))

        def acc_unit(m, k):
            l, part = m // 3, m % 3
            index["acc", m, k] = len(units)
            w = w_mod[l][P * k:P * (k + 1), 2 * D * part:2 * D * (part + 1)]
            units.append((w.rearrange("(k p) n -> p k n", p=P), 1, 2 * D,
                          (("mod_acc", acc_count(m, k)),)))

        def acc_count(m, k):
            return (KD + 1) * (m - 1) + k + 2

        NCT = w_in.shape[2] // P
        proj_cts = [list(range(NCT)), list(range(NCT))]
        beside = {}
        for l in range(L):
            if l == 0:
                for g in range(8):
                    unit(("mod", 0, g), w_mod[0][:, 256 * g:256 * (g + 1)].rearrange("(k p) n -> p k n", p=P), KD, 256,
                         ("mod_mm", g + 1))
            for u in range((NCT + 1) // 2):
                n = min(2, NCT - 2 * u)
                unit(("in", l, u), w_in[l][:, 256 * u:256 * u + P * n].rearrange("(k p) n -> p k n", p=P), KD, P * n,
                     ("proj_mm", NCT * l + 2 * u + n))
                if l == 0:
                    ms = [(1, k) for k in range(2 * u - 2, 2 * u)] if 1 <= u <= 4 else [(2, u - 6)] if u >= 6 else []
                    beside["in", l, u] = ms
                    for m, k in ms:
                        acc_unit(m, k)
            for u in range(KD // 2):
                unit(("out", l, u), w_out[l][:, 256 * u:256 * (u + 1)].rearrange("(k p) n -> p k n", p=P), KD, 256,
                     ("out_mm", KD * l + 2 * u + 2))
            if l % 2 == 0:
                NG = FF // 256

                def ffn_h_unit(nm, g):
                    w = ffn_w1 if nm == "w1" else ffn_w3
                    unit((nm, l, g), w[l // 2][:, 256 * g:256 * (g + 1)].rearrange("(k p) n -> p k n", p=P), KD, 256,
                         ("ffn_h" + nm[1], 2 * g + 2))

                def ffn_y_unit(g):
                    unit(("w2", l, g), ffn_w2[l // 2][256 * g:256 * (g + 1), :].rearrange("(k p) n -> p k n", p=P), 2, D,
                         ("ffn_y", KD * (g + 1)))
                names = [(nm, l, g) for s in range(NG + 1) for nm, g in (("w1", s), ("w3", s), ("w2", s - 1))
                         if 0 <= g < NG]
                for j, (nm, _, g) in enumerate(names):
                    if nm == "w2":
                        ffn_y_unit(g)
                    else:
                        ffn_h_unit(nm, g)
                    part, k = divmod(j - 1, 12)
                    beside[nm, l, g] = [(3 + part, k)] if 0 <= part < 3 and k < KD else []
                    for m, k in beside[nm, l, g]:
                        acc_unit(m, k)

        def slot_view(key):
            i = index[key]
            _, nk, nm, _ = units[i]
            return area(o_ring + (i % RING) * UNIT, UNIT)[:, 0:nk * nm].rearrange("p (k n) -> p k n", k=nk)

        split_of = {k: i for i, (k, _) in enumerate(splits)}

        def split_views(key):
            i = split_of[key]
            _, nk, nm, _ = units[index[key]]
            return [w[i % 2][:, 0:nk * nm].rearrange("p (k n) -> p k n", k=nk) for w in (WH, WL)]

        def wait_split(eng, key):
            wait(eng, "w_lo", split_of[key] + 1)

        def split_hi(act, i):
            if i >= len(splits):
                return
            key = splits[i][0]
            wait_unit(act, key)
            if i >= 2:
                wait(act, *splits[i - 2][1])
            act.activation(split_views(key)[0], slot_view(key), ACT.Copy).then_inc(sem("w_hi"), 1)

        def split_lo(eng, i):
            if i >= len(splits):
                return
            hi, lo = split_views(splits[i][0])
            wait(eng, "w_hi", i + 1)
            eng.tensor_tensor(lo, slot_view(splits[i][0]), hi, ALU.subtract).then_inc(sem("w_lo"), 1)

        ACC = area(o_mix, 2, 2 * D)
        reduce_at = {4: 3, 8: 4, 12: 5}

        def mod_sums(dve, key):
            for m, k in beside.get(key, ()):
                if k == 0:
                    if m == 1:
                        wait(dve, "xT", KD)
                    if m == 3:
                        wait(dve, "mix_lo", KD)
                    if m > 1:
                        wait(dve, "mod_mm", 7 + m)
                    nc.vector.memset(ACC[:], 0.0).then_inc(sem("mod_acc"), 1)
                wait(dve, "mod_acc", acc_count(m, k) - 1)
                wait_unit(dve, ("acc", m, k))
                for stream in range(2):
                    ins = nc.vector.scalar_tensor_tensor(out=ACC[:, stream], in0=slot_view(("acc", m, k))[:, 0, :],
                                                         scalar=cs[:, 2 * k + stream:2 * k + stream + 1],
                                                         in1=ACC[:, stream], op0=ALU.mult, op1=ALU.add)
                ins.then_inc(sem("mod_acc"), 1)

        def three(out_, pairs, first=True, last=True):
            n = len(pairs)
            for i, ((ah, al), (bh, bl)) in enumerate(pairs):
                nc.tensor.matmul(out_, ah, bh, start=(first and i == 0), stop=False)
                nc.tensor.matmul(out_, ah, bl, start=False, stop=False)
                ins = nc.tensor.matmul(out_, al, bh, start=False, stop=(last and i == n - 1))
            return ins

        def wait_unit(eng, key):
            i = index[key]
            wait(eng, f"slot{i % RING}", 16 * (i // RING + 1))


        def TILE(st):
            return st if st < 4 else (st - 4) ^ 1

        def reads_out(l, st):
            return l < L - 1 or TILE(st) >= TC // P

        ybefore, yn = {}, 0
        YTOT = []
        for l_ in range(L):
            for st_ in range(8):
                ybefore[l_, st_] = yn
                yn += reads_out(l_, st_)
            YTOT.append(2 * yn)

        def CTOK(l, ct):
            both = l < L - 1 or NP <= ct < 3 * NP + 2
            return slice(0, T) if both else slice(TC, T)

        def LTOK(l):
            return slice(TC, T) if l == L - 1 else slice(0, T)

        def tmp_k(j):
            return tmp[:, j % 2]


        NI = NE + 3
        NGM = FF // 512
        rw = sb("rw", [P, KD, NE])
        rb = sb("rb", [P, NE])
        o_m = o_ring + 14 * UNIT
        table_at = [o_m + 5888]

        def table(*dims):
            n = 1
            for d in dims:
                n *= d
            v = area(table_at[0], *dims)
            table_at[0] += n
            return v

        logit = table(2, NE)
        top_v = table(2, 8)
        top_i = table(2, 8).bitcast(mybir.dt.uint32)
        top_f = table(2, 8)
        one_hot = table(2, 2, NE)
        gw = table(4, 2)
        chosen = table(2, NE)
        gate = table(2, NE)
        rank = table(2, 2, NE)
        io_i = table(P).bitcast(i32)
        io = table(P)
        it_n = table(4, NE)[0:1]
        it_ge = table(2, NI, NE)[0:1]
        it_f = table(4, NI)[0:1]
        it_i = table(3 * NI)[0:1].bitcast(i32)
        XTK = area(o_mix, 2, D)
        FA = area(o_mix + 2048, KD, TL)
        OUTT = area(o_mix, 2, D)
        GSM = area(o_m, 2, 512)
        SGM = area(o_m + 1024, 2, 512)
        YS = area(o_m + 3072, D)
        o_mlow = o_ring + MRING * UNIT + MSPLIT * 2 * UNIT
        XGH, XGL = [cut(nm, at_, KD, P) for nm, at_ in (("x_hi", o_m + 4096), ("x_lo", o_mlow))]
        GTH, GTL = [[cut(f"{nm}{r}", at_ + 4 * P * r, 4, P) for r in range(2)]
                    for nm, at_ in (("gate_hi", o_m + 2048), ("gate_lo", o_mlow + KD * P))]
        MWH, MWL = [[cut(f"{nm}{r}", o_ring + (MRING + 2 * r + part) * UNIT, UNIT) for r in range(MSPLIT)]
                    for part, nm in enumerate(("unit_hi", "unit_lo"))]
        assert o_mlow + 2 * KD * P <= o_m
        SEL = area(o_m + 5120, 2, P)
        SG = area(o_m + 5376, 2, P)
        SGT = area(o_m + 5632, TL)
        assert table_at[0] <= o_ln, (table_at, o_ln)

        order = []
        for s in range(NGM + 2):
            if s < NGM:
                order += [("w1", s, 0), ("w1", s, 1), ("w3", s, 0), ("w3", s, 1)]
            if s >= 2:
                order += [("w2", s - 2, 0), ("w2", s - 2, 1)]
        NU = len(order)
        assert NU % MRING == 0 and NU % MSPLIT == 0
        TURNS = NU // MRING
        place = {u: j for j, u in enumerate(order)}
        turned = {place["w3", g + 1, 1]: g for g in range(NGM - 1)}
        turned[place["w2", NGM - 3, 1]] = NGM - 1

        used = [len(range(r, len(units), RING)) if r < RING else 0 for r in range(MRING)]
        NS = len(splits)

        def moe_slot(j):
            nk = 2 if order[j][0] == "w2" else 4
            return area(o_ring + (j % MRING) * UNIT, UNIT).rearrange("p (k n) -> p k n", k=nk)

        def moe_split(j):
            nk = 2 if order[j][0] == "w2" else 4
            return [w[j % MSPLIT].rearrange("p (k n) -> p k n", k=nk) for w in (MWH, MWL)]

        def moe_hi(act, i, j):
            slot, n = f"slot{j % MRING}", used[j % MRING] + j // MRING
            if i is None:
                wait(act, slot, 16 * (n + 1))
            else:
                act.wait_ge(sem(slot), 16 * (TURNS * i + (n + 1)))
                act.wait_ge(sem("m_unit"), NU * i + (j - MSPLIT + 1))
            act.activation(moe_split(j)[0], moe_slot(j), ACT.Copy).then_inc(sem("w_hi"), 1)

        def moe_lo(dve, i, j):
            if i is None:
                wait(dve, "w_hi", NS + j + 1)
            else:
                dve.wait_ge(sem("w_hi"), NU * i + (NS + j + 1))
            hi, lo = moe_split(j)
            nc.vector.tensor_tensor(lo, moe_slot(j), hi, ALU.subtract).then_inc(sem("w_lo"), 1)

        def split_ahead(split, eng, i, j, more):
            if j + MSPLIT < NU:
                split(eng, i, j + MSPLIT)
            elif more:
                split(eng, i + 1, j + MSPLIT - NU)

        def moe_sp(sp):
            def load(e, i, j):
                kind, g, part = order[j]
                if kind == "w2":
                    r0 = 512 * g + 256 * part
                    src = moe_w2[0][bass.ds(e, 1)][0, r0:r0 + 256, :] if e is not None else moe_w2[0, 0, r0:r0 + 256, :]
                else:
                    w = moe_w1 if kind == "w1" else moe_w3
                    rows, cols = slice(512 * part, 512 * part + 512), slice(512 * g, 512 * g + 512)
                    src = w[0][bass.ds(e, 1)][0, rows, cols] if e is not None else w[0, 0, rows, cols]
                if i is not None:
                    sp.wait_ge(sem("w_lo"), NU * i + (NS + j - MRING + 1))
                    if order[j] == ("w2", 0, 0):
                        sp.sem_inc(sem("m_turn"), 1)
                sp.dma_start(moe_slot(j), src.rearrange("(k p) n -> p k n", p=P)) \
                  .then_inc(sem(f"slot{j % MRING}"), 16)

            wait(sp, "out_mm", KD * L)
            for j in range(MRING):
                load(None, None, j)
            wait(sp, "items", 1)
            last = sp.value_load(it_i[0:1, 2 * NI:2 * NI + 1], min_val=NE - 1, max_val=NI - 1)
            with sp.Fori(0, last) as i:
                e = sp.value_load(it_i[0:1, bass.ds(i, 1)], min_val=0, max_val=NE - 1)
                for j in range(MRING, NU):
                    load(e, i, j)
                e1_ = sp.value_load(it_i[0:1, bass.ds(i + 1, 1)], min_val=0, max_val=NE - 1)
                for j in range(MRING):
                    load(e1_, i + 1, j)
            e = sp.value_load(it_i[0:1, bass.ds(last, 1)], min_val=0, max_val=NE - 1)
            for j in range(MRING, NU):
                load(e, last, j)

        def moe_act(act, ln_act):
            for t in range(2):
                for h in range(2):
                    wait(act, "xtkT", 2 * t + h + 1)
                    act.activation(XTK[:, t, 512 * h:512 * h + 512], bank[1 + h][:], ACT.Copy).then_inc(sem("xtk"), 1)
            wait(act, "gate_d", 1)
            act.activation(gw[:, 1, :], gw[:, 0, :], ACT.Exp).then_inc(sem("gate_e"), 1)

            def gather(i):
                for r in range(2):
                    act.wait_ge(sem("m_ga"), 2 * i + r + 1)
                    act.activation(XGH[:, 4 * r:4 * r + 4, :], pk((7, 1)[r], 4, P), ACT.Copy).then_inc(sem("m_xh"), 1)

            def item(i, more):
                for j, (kind, s, part) in enumerate(order):
                    if (kind, part) == ("w1", 1):
                        act.wait_ge(sem("m_unit"), NU * i + j + 1)
                        act.wait_ge(sem("m_s"), NGM * i + max(s - 1, 0) + 1)
                        act.activation(SGM[:, s % 2], bank[s % 2][:], ACT.Sigmoid).then_inc(sem("m_sig"), 1)
                    split_ahead(moe_hi, act, i, j, more)
                    if (kind, part) == ("w3", 1) and s == 3:
                        act.wait_ge(sem("m_sgT"), i + 1 + 1)
                        act.activation(SGT, bank[7][:, 0:TL], ACT.Copy).then_inc(sem("m_sgt"), 1)
                    if (kind, s, part) == ("w2", NGM - 3, 1) and more:
                        gather(i + 1)
                    g = turned.get(j)
                    if g is not None:
                        act.wait_ge(sem("m_tr"), NGM * i + g + 1)
                        act.activation(GTH[g % 2], pk(4, 4, P), ACT.Copy).then_inc(sem("m_gh"), 1)
                act.wait_ge(sem("m_unit"), NU * i + NU)
                act.activation(YS[:, 0:512], bank[5][:], ACT.Copy)
                act.activation(YS[:, 512:1024], bank[6][:], ACT.Copy).then_inc(sem("m_ys"), 1)

            gather(0)
            for j in range(MSPLIT):
                moe_hi(act, None, j)
            last = act.value_load(it_i[0:1, 2 * NI:2 * NI + 1], min_val=NE - 1, max_val=NI - 1)
            with act.Fori(0, last) as i:
                item(i, True)
            item(last, False)
            ln_act(3, slice(TC, T), 1, "ln2g", "ln2b")
            for t in range(2):
                for h in range(2):
                    n = 2 * t + h
                    wait(act, "outT", n + 1)
                    ins = act.activation(OUTT[:, t, 512 * h:512 * h + 512], bank[n][:], ACT.Copy)
            ins.then_inc(sem("fin"), 1)

        def moe_dve(dve, ln_dve, modulate, link):
            modulate(1, 3, 3, 4, (1,), ("ln_x", 2 * KD), False)
            tt, ts = nc.vector.tensor_tensor, nc.vector.tensor_scalar
            wait(dve, "iota", 1)
            link(nc.vector.tensor_copy(io, io_i))
            wait(dve, "router_mm", 1)
            wait(dve, "router_load", 32)
            link(tt(logit, pk(0, 2, NE), rb[:, None, :].to_broadcast([P, 2, NE]), ALU.add))
            for t in range(2):
                link(nc.vector.max(top_v[:, t], logit[:, t]))
                link(nc.vector.max_index(top_i[:, t], top_v[:, t], logit[:, t]))
            link(nc.vector.tensor_copy(top_f, top_i))
            tt(gw[:, 0, :], top_v[:, :, 1], top_v[:, :, 0], ALU.subtract).then_inc(sem("gate_d"), 1)
            for n in range(2):
                for t in range(2):
                    link(ts(one_hot[:, n, t], io[:, 0:NE], top_f[:, t, n:n + 1], None, ALU.is_equal))
            tt(chosen, one_hot[:, 0], one_hot[:, 1], ALU.add).then_inc(sem("chosen"), 1)
            wait(dve, "gate_e", 1)
            link(ts(gw[:, 2, :], gw[:, 1, :], 1.0, None, ALU.add))
            link(nc.vector.reciprocal(gw[:, 2, :], gw[:, 2, :]))
            link(tt(gw[:, 3, :], gw[:, 1, :], gw[:, 2, :], ALU.mult))
            link(tt(gate, one_hot[:, 0], gw[:, 2, :].unsqueeze(2).to_broadcast([P, 2, NE]), ALU.mult))
            link(tt(one_hot[:, 1], one_hot[:, 1], gw[:, 3, :].unsqueeze(2).to_broadcast([P, 2, NE]), ALU.mult))
            link(tt(gate, gate, one_hot[:, 1], ALU.add))
            wait(dve, "rank_mm", 1)
            wait(dve, "chosen", 1)
            stt = nc.vector.scalar_tensor_tensor
            ps = pk(3, 3, NE)
            link(stt(out=rank[:, 0], in0=ps[:, 0:2], scalar=1.0, in1=chosen, op0=ALU.add, op1=ALU.mult))
            link(ts(rank[:, 1], rank[:, 0], -1.0 - SLOTS, None, ALU.add))
            link(ts(rank[:, 0], rank[:, 0], -1.0, None, ALU.add))
            link(ts(it_n[:, 0], ps[0:1, 2], float(SLOTS), 1.0, ALU.is_gt, ALU.add))
            link(nc.vector.tensor_tensor_scan(it_n[:, 1], ones_t[0:1, 0:NE], it_n[:, 0], 0.0, ALU.mult, ALU.add))
            link(tt(it_ge[:, 0], io[0:1, 0:NI].unsqueeze(2).to_broadcast([1, NI, NE]),
                    it_n[:, 1:2, :].to_broadcast([1, NI, NE]), ALU.is_ge))
            link(tt(it_ge[:, 1], it_ge[:, 0], it_n[:, 0:1, :].to_broadcast([1, NI, NE]), ALU.mult))
            link(nc.vector.tensor_reduce(out=it_f[:, 0], in_=it_ge[:, 0], axis=AX.X, op=ALU.add))
            link(nc.vector.tensor_reduce(out=it_f[:, 1], in_=it_ge[:, 1], axis=AX.X, op=ALU.add))
            link(ts(it_f[:, 0], it_f[:, 0], float(NE - 1), None, ALU.min))
            link(tt(it_f[:, 1], io[0:1, 0:NI], it_f[:, 1], ALU.subtract))
            link(ts(it_f[:, 1], it_f[:, 1], 1.0, None, ALU.min))
            link(stt(out=it_f[:, 2], in0=it_f[:, 1], scalar=float(2 * NE), in1=it_f[:, 0], op0=ALU.mult, op1=ALU.add))
            link(ts(it_f[:, 3], it_n[:, 1, NE - 1:NE].to_broadcast([1, NI]), -1.0, None, ALU.add))
            link(nc.vector.tensor_copy(it_i[:, 0:NI], it_f[:, 0]))
            link(nc.vector.tensor_copy(it_i[:, NI:2 * NI], it_f[:, 2]))
            nc.vector.tensor_copy(it_i[:, 2 * NI:3 * NI], it_f[:, 3]).then_inc(sem("items"), 1)
            wait(dve, "items", 1)
            wait(dve, "xtk", 4)
            nc.vector.memset(FA[:], 0.0).then_inc(sem("m_fa"), 1)
            nc.vector.memset(YS, 0.0).then_inc(sem("m_ys"), 1)
            nc.vector.memset(SGT, 0.0).then_inc(sem("m_sgt"), 1)
            dve.sem_inc(sem("m_s"), 1)
            dve.sem_inc(sem("m_g"), 1)
            dve.sem_inc(sem("m_gt"), 1)
            rank_f = rank.rearrange("p b t e -> p (b t e)")
            gate_f = gate.rearrange("p t e -> p (t e)")

            def select(i):
                col = dve.value_load(it_i[0:1, bass.ds(i + NI, 1)], min_val=0, max_val=3 * NE - 1)
                for t in range(2):
                    ins = ts(SEL[:, t], io, rank_f[:, bass.ds(col + NE * t, 1)], None, ALU.is_equal)
                ins.then_inc(sem("m_sel"), 1)

            def weigh(i):
                e = dve.value_load(it_i[0:1, bass.ds(i, 1)], min_val=0, max_val=NE - 1)
                dve.wait_ge(sem("m_sel"), i + 1)
                for t in range(2):
                    ins = ts(SG[:, t], SEL[:, t], gate_f[:, bass.ds(e + NE * t, 1)], None, ALU.mult)
                ins.then_inc(sem("m_sg"), 1)

            def scatter_add(i):
                for r in range(4):
                    dve.wait_ge(sem("m_sc"), 4 * i + r + 1)
                    tt(FA[:, 2 * r:2 * r + 2], FA[:, 2 * r:2 * r + 2], pk((7, 4)[r % 2], 2, TL), ALU.add) \
                        .then_inc(sem("m_fa"), 1)

            def gather(i):
                for r in range(2):
                    dve.wait_ge(sem("m_xh"), 2 * i + r + 1)
                    tt(XGL[:, 4 * r:4 * r + 4, :], pk((7, 1)[r], 4, P), XGH[:, 4 * r:4 * r + 4, :], ALU.subtract) \
                        .then_inc(sem("m_xg"), 1)

            def item(i, more):
                dve.wait_ge(sem("m_sgT"), i + 1)
                weigh(i)
                for j, (kind, s, part) in enumerate(order):
                    if (kind, part) == ("w1", 1):
                        dve.wait_ge(sem("m_sig"), NGM * i + s + 1)
                        if s >= 2:
                            dve.wait_ge(sem("m_tr"), NGM * i + s - 1)
                        tt(GSM[:, s % 2], SGM[:, s % 2], bank[s % 2][:], ALU.mult).then_inc(sem("m_s"), 1)
                    if (kind, part) == ("w3", 1):
                        dve.wait_ge(sem("m_unit"), NU * i + j + 1)
                        dve.wait_ge(sem("m_s"), NGM * i + s + 1 + 1)
                        tt(GSM[:, s % 2], GSM[:, s % 2], bank[2 + s % 2][:], ALU.mult).then_inc(sem("m_g"), 1)
                    split_ahead(moe_lo, dve, i, j, more)
                    if (kind, s, part) == ("w3", 0, 1):
                        dve.wait_ge(sem("m_fa"), 4 * i + 1)
                        scatter_add(i)
                    if (kind, s, part) == ("w3", 4, 1) and more:
                        select(i + 1)
                    if (kind, s, part) == ("w2", NGM - 3, 1) and more:
                        gather(i + 1)
                    g = turned.get(j)
                    if g is not None:
                        dve.wait_ge(sem("m_gh"), NGM * i + g + 1)
                        tt(GTL[g % 2], pk(4, 4, P), GTH[g % 2], ALU.subtract).then_inc(sem("m_gt"), 1)

            select(0)
            gather(0)
            for j in range(MSPLIT):
                moe_lo(dve, None, j)
            last = dve.value_load(it_i[0:1, 2 * NI:2 * NI + 1], min_val=NE - 1, max_val=NI - 1)
            with dve.Fori(0, last) as i:
                item(i, True)
            item(last, False)
            scatter_add(last + 1)
            dve.wait_ge(sem("m_fa"), 4 * last + 8 + 1)
            for m in range(KD):
                stt(out=X[:, m, TC:T], in0=FA[:, m], scalar=mc[:, 1, 1, 5 * KD + m:5 * KD + m + 1],
                    in1=X[:, m, TC:T], op0=ALU.mult, op1=ALU.add).then_inc(sem("z"), 1)
            ln_dve(3, slice(TC, T))

        def moe_pe(pe, ln_pe):
            mm = nc.tensor.matmul
            wait(pe, "router_load", 32)
            wait(pe, "h_ready", 4 * KD)
            for t in range(2):
                for k in range(KD):
                    ins = mm(pk(0, 2, NE)[:, t], HB[:, k, TC + P * t:TC + P * (t + 1)], rw[:, k, :], start=(k == 0),
                             stop=(k == KD - 1))
            ins.then_inc(sem("router_mm"), 1)
            for t in range(2):
                for h in range(2):
                    wait(pe, "xtk", 2 * t + h - 1)
                    for k in range(4):
                        ins = nc.tensor.transpose(bank[1 + h][:, k * P:(k + 1) * P],
                                                  HB[:, 4 * h + k, TC + P * t:TC + P * (t + 1)], ident)
                    ins.then_inc(sem("xtkT"), 1)
            wait(pe, "chosen", 1)
            ps = pk(3, 3, NE)
            mm(ps[:, 0], tri[:, 0, :], chosen[:, 0], start=True, stop=True)
            mm(ps[:, 1], tri[:, 0, :], chosen[:, 1], start=True, stop=False)
            mm(ps[:, 1], ones_t, chosen[:, 0], start=False, stop=True)
            mm(ps[:, 2], ones_t, chosen[:, 0], start=True, stop=False)
            mm(ps[:, 2], ones_t, chosen[:, 1], start=False, stop=True).then_inc(sem("rank_mm"), 1)
            wait(pe, "xtk", 4)
            pe.sem_inc(sem("m_sgT"), 1)

            def gather(i):
                pe.wait_ge(sem("m_sel"), i + 1)
                for r in range(2):
                    for k in range(4):
                        for t in range(2):
                            ins = mm(pk((7, 1)[r], 4, P)[:, k], XTK[:, t, (4 * r + k) * P:(4 * r + k + 1) * P],
                                     SEL[:, t], start=(t == 0), stop=(t == 1))
                    ins.then_inc(sem("m_ga"), 1)

            def scatter(i):
                pe.wait_ge(sem("m_ys"), i + 1)
                pe.wait_ge(sem("m_sgt"), i + 1)
                pe.wait_ge(sem("m_gt"), NGM * i + 1)
                for r in range(4):
                    if r >= 2:
                        pe.wait_ge(sem("m_fa"), 4 * i + r - 1 + 1)
                    for k in range(2):
                        ins = mm(pk((7, 4)[r % 2], 2, TL)[:, k], YS[:, (2 * r + k) * P:(2 * r + k + 1) * P], SGT,
                                 start=True, stop=True)
                    ins.then_inc(sem("m_sc"), 1)

            def hidden(i, g):
                if g < 2:
                    pe.wait_ge(sem("m_g"), NGM * i + 1)
                else:
                    pe.wait_ge(sem("m_g"), NGM * i + g - 1 + 1)
                for b, kind in ((0, "w1"), (2, "w3")):
                    for part in range(2):
                        j = place[kind, g, part]
                        pe.wait_ge(sem("w_lo"), NU * i + (NS + j + 1))
                        wh, wl = moe_split(j)
                        three(bank[b + g % 2][:], [((XGH[:, 4 * part + k, :], XGL[:, 4 * part + k, :]),
                                                    (wh[:, k, :], wl[:, k, :])) for k in range(4)],
                              part == 0, part == 1).then_inc(sem("m_unit"), 1)

            def turn(i, g):
                pe.wait_ge(sem("m_g"), NGM * i + g + 1 + 1)
                if g:
                    pe.wait_ge(sem("m_gt"), NGM * i + g + 1)
                else:
                    pe.wait_ge(sem("m_fa"), 4 * i + 4 + 1)
                for f in range(4):
                    ins = nc.tensor.transpose(pk(4, 4, P)[:, f], GSM[:, g % 2, f * P:(f + 1) * P], ident)
                ins.then_inc(sem("m_tr"), 1)

            def down(i, g):
                pe.wait_ge(sem("m_gt"), NGM * i + g + 1 + 1)
                if g == 0:
                    pe.wait_ge(sem("m_ys"), i + 1)
                for part in range(2):
                    j = place["w2", g, part]
                    pe.wait_ge(sem("w_lo"), NU * i + (NS + j + 1))
                    wh, wl = moe_split(j)
                    for h in range(2):
                        cols = slice(512 * h, 512 * h + 512)
                        ins = three(bank[5 + h][:], [((GTH[g % 2][:, 2 * part + f], GTL[g % 2][:, 2 * part + f]),
                                                      (wh[:, f, cols], wl[:, f, cols])) for f in range(2)],
                                    g + part == 0, g == NGM - 1 and part == 1)
                    ins.then_inc(sem("m_unit"), 1)

            def item(i, more):
                pe.wait_ge(sem("m_xg"), 2 * i + 2)
                for s in range(NGM + 2):
                    if s < NGM:
                        hidden(i, s)
                    if s == 0:
                        scatter(i)
                    if s == 3:
                        pe.wait_ge(sem("m_sg"), i + 1)
                        for t in range(2):
                            ins = nc.tensor.transpose(bank[7][:, t * P:(t + 1) * P], SG[:, t], ident)
                        ins.then_inc(sem("m_sgT"), 1)
                    if s == NGM and more:
                        pe.wait_ge(sem("m_g"), NGM * i + NGM - 1 + 1)
                        pe.wait_ge(sem("m_sgt"), i + 1 + 1)
                        gather(i + 1)
                    if 1 <= s <= NGM:
                        turn(i, s - 1)
                    if s >= 2:
                        down(i, s - 2)

            gather(0)
            wait(pe, "items", 1)
            last = pe.value_load(it_i[0:1, 2 * NI:2 * NI + 1], min_val=NE - 1, max_val=NI - 1)
            with pe.Fori(0, last) as i:
                item(i, True)
            item(last, False)
            scatter(last + 1)
            ln_pe(3, slice(TC, T))
            for t in range(2):
                for h in range(2):
                    n = 2 * t + h
                    for k in range(4):
                        if t == 0:
                            wait(pe, "ln_x", 3 * KD + 4 * h + k + 1)
                        ins = nc.tensor.transpose(bank[n][:, k * P:(k + 1) * P], X[:, 4 * h + k, TC + P * t:TC + P * (t + 1)],
                                                  ident)
                    ins.then_inc(sem("outT"), 1)

        block = es.enter_context(nc.Block())

        @block.sync
        def _(sp):
            for i, (src, nk, nm, _) in enumerate(units):
                if i >= RING:
                    for free in units[i - RING][3]:
                        wait(sp, *free)
                for l in range(L):
                    if i == index[("out", l, 0)]:
                        wait(sp, "y_done", YTOT[l])
                        wait(sp, "state_done", 16 * (l + 1))
                key = [k for k, v in index.items() if v == i][0]
                sp.dma_start(slot_view(key), src).then_inc(sem(f"slot{i % RING}"), 16)
            moe_sp(sp)
            wait(sp, "fin", 1)
            sp.dma_start(out[0].rearrange("(t p) d -> p t d", p=P), area(o_mix, 2, D)).then_inc(sem("out_dma"), 16)
            wait(sp, "out_dma", 16)

        @block.gpsimd
        def _(pool):
            pc = [0]

            def link(ins):
                pc[0] += 1
                ins.then_inc(sem("pool_chain"), 1)
                pool.wait_ge(sem("pool_chain"), pc[0])

            def blocks(b):
                n, w = P >> b, 1 << b
                v = same[:, b, :].rearrange("p (n w) -> p n w", w=w)
                link(nc.gpsimd.memset(same[:, b, :], 1.0))
                link(nc.gpsimd.affine_select(out=v, in_=v, compare_op=ALU.is_ge, fill=0.0, base=0,
                                             pattern=[[-w, n], [0, w]], channel_multiplier=1))
                link(nc.gpsimd.affine_select(out=v, in_=v, compare_op=ALU.is_ge, fill=0.0, base=w - 1,
                                             pattern=[[w, n], [0, w]], channel_multiplier=-1))

            blocks(0)
            link(nc.gpsimd.tensor_copy(keep[:, 0], same[:, 0, :]))
            link(nc.gpsimd.memset(cs[:], 0.0))
            nc.gpsimd.memset(cs[:, one:one + 1], 1.0).then_inc(sem("consts"), 1)
            link(nc.gpsimd.memset(mean_w[:], 1.0 / D))
            link(nc.gpsimd.memset(same[:, 7, :], 1.0))
            for b in range(1, 7):
                blocks(b)
            for b in range(7):
                link(nc.gpsimd.tensor_tensor(level[:, b, :], same[:, b + 1, :], same[:, b, :], ALU.subtract))
            for i, b in ((1, 6), (2, 7)):
                link(nc.gpsimd.tensor_copy(keep[:, i], same[:, b, :]))
            for i, (base, cm, st) in enumerate(((-1, -1, 1), (-1, 1, -1), (0, -1, 1), (0, 1, -1))):
                v = tri[:, i, :]
                link(nc.gpsimd.memset(v, 1.0))
                ins = nc.gpsimd.affine_select(out=v, in_=v, compare_op=ALU.is_ge, fill=0.0, base=base,
                                              pattern=[[st, P]], channel_multiplier=cm)
                if i < 3:
                    link(ins)
            ins.then_inc(sem("masks"), 1)

            for l in range(L):
                for u in range((NCT + 1) // 2):
                    split_lo(pool, split_of["in", l, u])
                wait(pool, "mod_mm", (8 + 2, 8 + 5)[l])
                wait(pool, *(("xT", KD) if l == 0 else ("mix_lo", KD * l)))
                nc.gpsimd.memset(w2z, 0.0).then_inc(sem("w2z_zero"), 1)
                wait(pool, "q_in", l + 1)
                nc.gpsimd.tensor_tensor(Qflat, Qflat, qm[:].unsqueeze(2).to_broadcast([P, 2 * NP * NT, P + 1]),
                                        ALU.subtract).then_inc(sem("q_done"), 1)
                for i in range(2 * NP):
                    k_ = KDIR[:, i // NP, i % NP]
                    wait(pool, "kdir_f", 2 * NP * l + i + 1)
                    nc.gpsimd.tensor_tensor(k_, k_, K[:, i % NP], ALU.mult).then_inc(sem("kdir"), 1)
                wait(pool, "prep_done", l + 1)
                nc.gpsimd.memset(ZR[:], 0.0).then_inc(sem("zr_zero"), 1)
                def values(cn, tj):
                    wait(pool, "pe_m", 2 * cn)
                    wait(pool, "vtok", NT * (l + 1))
                    nc.gpsimd.tensor_copy(VS[:], VTK[:, tj]).then_inc(sem("vs"), 1)

                for st in range(8):
                    d, tj, cn = st // 4, TILE(st), 8 * l + st
                    values(cn, tj)
                    for k in range(6):
                        for q in range(2):
                            w = wk[q]
                            if k == 0:
                                wait(pool, "dve_lt", 2 * cn + q + 1)
                            if k >= 2:
                                wait(pool, "pe_x", (6 * cn + k - 2) * 2 + q + 1)
                            nc.gpsimd.tensor_tensor(w["LM"][:, k % 2], w["LT"],
                                                    level[:, k + 1:k + 2, :].to_broadcast([P, 4, P]), ALU.mult) \
                                .then_inc(sem("pool_lm"), 1)
                if l == 0:
                    for i in range(split_of["w1", 0, 0], split_of["w1", 0, 0] + 3 * (FF // 256)):
                        split_lo(pool, i)
            wait(pool, "mix", NP * L)
            nc.gpsimd.iota(io_i, [[1, P]], base=0, channel_multiplier=0).then_inc(sem("iota"), 1)



        @block.scalar
        def _(act):
            def load_params(l):
                if l:
                    wait(act, "par_T", l)
                srcs = [(b_mod[l], "b_mod"), (rk_w0[l], "w0"), (rk_a0[l], "a0"), (rk_kk[l], "kk"), (rk_ka[l], "ka"),
                        (rk_rk[l], "rk"), (rk_lnx_g[l], "lnxg"), (rk_lnx_b[l], "lnxb"), (conv_w[l], "conv"),
                        (ln1_g[l], "ln1g"), (ln1_b[l], "ln1b"), (ln2_g[l], "ln2g"), (ln2_b[l], "ln2b")]
                for s, nm in srcs:
                    if len(s.shape) == 2:
                        s = s.rearrange("a b -> (a b)")
                    n = s.shape[0] // P
                    act.dma_start(par_rows[COLS[nm]:COLS[nm] + n, :], s.rearrange("(n p) -> n p", p=P)) \
                       .then_inc(sem("par_load"), 16)

            act.dma_start(crow[0:KD, :], c_ctx.rearrange("(n p) -> n p", p=P)).then_inc(sem("c_load"), 16)
            act.dma_start(crow[KD:2 * KD, :], c[0].rearrange("(n p) -> n p", p=P)).then_inc(sem("c_load"), 16)
            load_params(0)
            act.dma_start(rw[:], router_w[0].rearrange("(k p) e -> p k e", p=P)).then_inc(sem("router_load"), 16)
            act.dma_start(rb[:], router_b[0].partition_broadcast(P)).then_inc(sem("router_load"), 16)
            act.dma_start(xrows[:, 0:TC // P, :], ctx[0].rearrange("(t p) d -> p t d", p=P)).then_inc(sem("x_load"), 16)
            act.dma_start(xrows[:, TC // P:NT, :], x[0].rearrange("(t p) d -> p t d", p=P)).then_inc(sem("x_load"), 16)
            load_params(1)
            wait(act, "c_col", 1)
            act.activation(csig[:], ccol[:], ACT.Sigmoid).then_inc(sem("c_sig"), 1)
            for k in range(KD):
                wait(act, "xT", k + 1)
                act.activation(X[:, k, :], bank[k % 4][:], ACT.Copy).then_inc(sem("xT_act"), 1)

            def mod_rows(m):
                wait(act, "mod_mm", 8 + m)
                wait(act, "mod_T", m)
                act.activation(mrow[:], bank[6][:], ACT.Copy).then_inc(sem("mod_rows"), 1)

            def ln_act(n, tok, l, g, b):
                for k in range(KD):
                    wait(act, "ln_d", KD * n + k + 1)
                    if k >= 2 or n:
                        wait(act, "ln_vmm", KD * n + k - 1)
                    act.activation(SQ[:, k % 2, tok], X[:, k, tok], ACT.Square).then_inc(sem("ln_sq"), 1)
                wait(act, "ln_ve", n + 1)
                act.activation(RSTD[:, tok], RSTD[:, tok], ACT.Sqrt).then_inc(sem("ln_std"), 1)
                for k in range(KD):
                    wait(act, "ln_norm", KD * n + k + 1)
                    act.activation(X[:, k, tok], X[:, k, tok], ACT.Identity, bias=pcol(l, b, k), scale=pcol(l, g, k)) \
                       .then_inc(sem("ln_x"), 1)

            def hi_parts(n):
                for k in range(KD):
                    wait(act, "h_ready", KD * n + k + 1)
                    act.activation(HH[k][:, :], HT[:, k % 2], ACT.Copy).then_inc(sem("h_hi"), 1)

            mod_rows(0)
            for l in range(L):
                dst = [R[:, i] for i in range(NP)] + [K[:, i] for i in range(NP)] + [V[:, i] for i in range(NP)] + \
                      [WD, AD, GD] + [CB[:, i] for i in range(NP)] + [CC[:, i] for i in range(NP)]
                hi_parts(2 * l)
                s0 = split_of[("in", l, 0)]
                split_hi(act, s0)
                split_hi(act, s0 + 1)
                for ct in range(NCT):
                    if ct < len(dst):
                        wait(act, "proj_mm", NCT * l + ct + 1)
                        f = {3 * NP: ACT.Tanh, 3 * NP + 2: ACT.Sigmoid}.get(ct, ACT.Copy)
                        tok = CTOK(l, ct)
                        act.activation(dst[ct][:, tok], bank[ct % 4][:, tok], f).then_inc(sem("proj_act"), 1)
                    if ct % 2 and s0 + ct // 2 + 2 <= split_of[("in", l, NCT // 2)]:
                        split_hi(act, s0 + ct // 2 + 2)
                    if l == 0 and ct == 11:
                        mod_rows(1)
                    if (ct - 9) % 3 == 0 and 0 <= (ct - 9) // 3 < NP:
                        j = (ct - 9) // 3
                        wait(act, "kk_raw", NP * l + j + 1)
                        wait(act, "kk_done", NP * l + j - 1)
                        act.activation(tmp_k(j), KKN[:, j], ACT.Square).then_inc(sem("kk_sq"), 1)
                    if (ct - 12) % 3 == 0 and 0 <= (ct - 12) // 3 < NP:
                        j = (ct - 12) // 3
                        wait(act, "kk_ss", NP * l + j + 1)
                        act.activation(tmp_k(j), tmp_k(j), ACT.Sqrt).then_inc(sem("kk_norm"), 1)
                if l == 0:
                    mod_rows(2)
                wait(act, "w2z_zero", l + 1)
                for kind, w in enumerate((rk_w2, rk_a2)):
                    for d in range(2):
                        act.dma_start(w2z[64 * d:64 * (d + 1), kind, d, :], w[l, d]).then_inc(sem("lora_load"), 16)
                wait(act, "kk_done", NP * (l + 1))
                for i in range(4 * NP):
                    n = 4 * NP * l + i
                    wait(act, "lora_mm", n + 1)
                    wait(act, "lora_use", n - 1)
                    kind, d, j = i // (2 * NP), i // NP % 2, i % NP
                    act.activation(tmp[:, i % 2], bank[i % 4][:], ACT.Sigmoid,
                                   bias=pcol(l, ("w0", "a0")[kind], d * NP + j)).then_inc(sem("lora_sig"), 1)
                wait(act, "q_in", l + 1)
                act.activation(e1[:].rearrange("p d j t -> p (d j t)"), qm[:], ACT.Exp, scale=-DECAY)
                act.activation(e2[:].rearrange("p d j t -> p (d j t)"), qt[:], ACT.Exp, scale=-DECAY) \
                   .then_inc(sem("e12"), 1)
                for t in range(NT):
                    wait(act, "vT", NT * l + t + 1)
                    if t == 0:
                        wait(act, "kdir", 2 * NP * (l + 1))
                    act.activation(VTK[:, t], pk(2 + t % 2, NP, P), ACT.Copy).then_inc(sem("vtok"), 1)
                wait(act, "prep_done", l + 1)
                act.dma_start(g2, rk_g2[l]).then_inc(sem("g2_load"), 16)

                def stage(cn, st):
                    d, tj = st // 4, TILE(st)
                    wait(act, "staged", cn)
                    incl, excl = (slice(1, P + 1), slice(0, P)) if d == 0 else (slice(0, P), slice(1, P + 1))
                    s = -DECAY if d == 0 else DECAY
                    act.activation(EX[:, 0], Q[:, d, :, tj, incl], ACT.Exp, scale=s)
                    act.activation(EX[:, 1], Q[:, d, :, tj, incl], ACT.Exp, scale=-s)
                    act.activation(EX[:, 2], Q[:, d, :, tj, excl], ACT.Exp, scale=s).then_inc(sem("ex"), 1)

                def masked(cn, st):
                    wait(act, "staged", cn + 1)
                    wait(act, "zr_zero", l + 1)
                    wait(act, "pe_s2", 2 * cn)
                    for i, src in ((0, AS), (2, rt[:, st % 2])):
                        if i == 0 or reads_out(l, st):
                            act.activation(ZR[0:64, :, i, :], src[0:64], ACT.Copy)
                            ins = act.activation(ZR[64:128, :, i + 1, :], src[64:128], ACT.Copy)
                    ins.then_inc(sem("zr"), 1)

                wait(act, "q_done", l + 1)
                stage(8 * l, 0)
                masked(8 * l, 0)
                for st in range(8):
                    cn = 8 * l + st
                    for q in range(2):
                        w, b = wk[q], 4 * q
                        n = 2 * cn + q + 1
                        xa = w["XA"].rearrange("p (a h) n -> p a h n", h=2)
                        wait(act, "pe_tab", n)
                        src = pk(b, 4, P)
                        act.activation(xa[:, :, 0, 0:64], src[:, 0:2, 0:64], ACT.Copy)
                        act.activation(xa[:, :, 1, 64:128], src[:, 0:2, 64:128], ACT.Copy)
                        act.activation(w["BT"], src[:, 2:4, :], ACT.Copy).then_inc(sem("act_tab"), 1)
                        wait(act, "pe_tk", n)
                        act.activation(w["KT"], pk(b + 1, 2, P), ACT.Copy).then_inc(sem("act_tk"), 1)
                    for q in range(2):
                        w, b = wk[q], 4 * q
                        n = 2 * cn + q + 1
                        wait(act, "pe_t1", n)
                        act.activation(w["T"], pk(b + 2, 4, P), ACT.Copy).then_inc(sem("act_t1"), 1)
                    for q in range(2):
                        w, b = wk[q], 4 * q
                        n = 2 * cn + q + 1
                        xa = w["XA"].rearrange("p (a h) n -> p a h n", h=2)
                        wait(act, "pe_ax", n)
                        src = pk(b + 3, 2, 2, P)
                        act.activation(xa[:, :, 0, 64:128], src[:, :, 0, 0:64], ACT.Copy)
                        act.activation(xa[:, :, 1, 0:64], src[:, :, 1, 64:128], ACT.Copy).then_inc(sem("act_ax"), 1)
                    for k in range(6):
                        for q in range(2):
                            w, b = wk[q], 4 * q
                            wait(act, "pe_x", (6 * cn + k) * 2 + q + 1)
                            act.activation(w["XS"], pk(b, 4, P), ACT.Copy).then_inc(sem("act_xs"), 1)
                        if k == 1 and st < 7:
                            stage(cn + 1, st + 1)
                        if k == 3 and st < 7:
                            masked(cn + 1, st + 1)
                    for q in range(2):
                        w, b = wk[q], 4 * q
                        wait(act, "pe_uw", 2 * cn + q + 1)
                        act.activation(w["UW"], pk(b + 3, 4, P), ACT.Copy).then_inc(sem("act_uw"), 1)
                    for q in range(2):
                        w, b = wk[q], 4 * q
                        n = 2 * cn + q + 1
                        wait(act, "pe_gt", n)
                        act.activation(w["GT"], pk(b + 1, 2, HS), ACT.Copy).then_inc(sem("act_gt"), 1)
                        if not reads_out(l, st):
                            continue
                        wait(act, "dve_yw", 2 * ybefore[l, st] + q + 1)
                        yw = w["YW"].rearrange("p (a h) n -> p a h n", h=2)
                        src = pk(b, 2, 2, P)
                        act.activation(yw[64:128, :, 0, :], src[64:128, :, 0, :], ACT.Copy)
                        act.activation(yw[0:64, :, 1, :], src[0:64, :, 1, :], ACT.Copy).then_inc(sem("act_yw"), 1)
                rtok = LTOK(l)
                for j in range(NP):
                    wait(act, "gn_d", NP * l + j + 1)
                    act.activation(RSQ[:, j, rtok], Y[:, j, rtok], ACT.Square).then_inc(sem("gn_sq"), 1)
                for j in range(NP):
                    wait(act, "gn_ve", NP * l + j + 1)
                    act.activation(RRS[:, j, rtok], RRS[:, j, rtok], ACT.Sqrt).then_inc(sem("gn_std"), 1)
                for j in range(NP):
                    wait(act, "gn_norm", NP * l + j + 1)
                    act.activation(Y[:, j, rtok], Y[:, j, rtok], ACT.Identity, bias=pcol(l, "lnxb", j),
                                   scale=pcol(l, "lnxg", j)).then_inc(sem("gn_aff"), 1)
                wait(act, "mix", NP * (l + 1))
                for k in range(KD):
                    act.activation(HH[k][:, rtok], MIX[:, k, rtok], ACT.Copy).then_inc(sem("mix_hi"), 1)
                s0 = split_of[("out", l, 0)]
                for u in range(KD // 2):
                    split_hi(act, s0 + u)
                ln_act(2 * l, LTOK(l), l, "ln1g", "ln1b")
                if l == 0:
                    hi_parts(1)
                    s0 = split_of[("w1", 0, 0)]
                    split_hi(act, s0)
                    split_hi(act, s0 + 1)
                    NG = FF // 256

                    for j, ((kind, _, g), _) in enumerate(splits[s0:s0 + 3 * NG]):
                        if kind == "w1":
                            for f in (2 * g, 2 * g + 1):
                                wait(act, "ffn_h1", f + 1)
                                wait(act, "ffn_s", f - 1)
                                act.activation(FS[:, f % 2], bank[f % 2][:], ACT.Sigmoid).then_inc(sem("ffn_sig"), 1)
                            if g in reduce_at:
                                mod_rows(reduce_at[g])
                        elif kind == "w3":
                            for f in (2 * g, 2 * g + 1):
                                wait(act, "ffn_g", f + 1)
                                wait(act, "ffn_y", KD * (g - 1))
                                act.activation(GH[f % 4], FP[:, f % 2], ACT.Copy).then_inc(sem("ffn_ghi"), 1)
                        if j + 2 < 3 * NG:
                            split_hi(act, s0 + j + 2)
                    ln_act(1, slice(0, T), 0, "ln2g", "ln2b")
            moe_act(act, ln_act)

        @block.vector
        def _(dve):
            ch = [0]

            def link(ins):
                ch[0] += 1
                ins.then_inc(sem("dve_chain"), 1)
                dve.wait_ge(sem("dve_chain"), ch[0])

            wait(dve, "c_T", 1)
            nc.vector.tensor_copy(ccol[:], bank[5][:, 0:2 * KD]).then_inc(sem("c_col"), 1)
            wait(dve, "c_sig", 1)
            wait(dve, "consts", 1)
            nc.vector.tensor_tensor(cs[:, 0:2 * KD].rearrange("p (k s) -> p k s", s=2), ccol[:].rearrange("p (s k) -> p k s", s=2),
                                    csig[:].rearrange("p (s k) -> p k s", s=2), ALU.mult).then_inc(sem("c_silu"), 1)

            def params(l):
                wait(dve, "par_T", l + 1)
                link(nc.vector.tensor_copy(par[:, l, :], bank[4][:, 0:P]))
                nc.vector.tensor_scalar(one_ka[:, l, :], par[:, l, COLS["ka"]:COLS["ka"] + NP], -1.0, 1.0,
                                        ALU.mult, ALU.add).then_inc(sem("par"), 1)
                wait(dve, "par", l + 1)

            params(0)
            params(1)

            def mod_cols(m):
                l, part = m // 3, m % 3
                wait(dve, "mod_T", m + 1)
                b = (7, 7, 5)[part]
                for i in range(4):
                    c0 = 16 * part + 8 * (i // 2) + i % 2
                    src = bank[b][:, i * P:(i + 1) * P].rearrange("p (q s) -> p q s", s=32)[:, :, 0:2]
                    bias = par[:, l, c0:c0 + 7:2].unsqueeze(2).to_broadcast([P, 4, 2])
                    dst = mc[:, l, :, c0:c0 + 7:2].rearrange("p s q -> p q s")
                    ins = nc.vector.tensor_tensor(dst, src, bias, ALU.add)
                    if part != 1 and i == 3:
                        link(ins)
                if part == 1:
                    ins.then_inc(sem("mod_cols"), 1)
                else:
                    c1 = KD if part == 0 else 4 * KD
                    nc.vector.tensor_scalar(mc[:, l, :, c1:c1 + KD], mc[:, l, :, c1:c1 + KD], 1.0, None, ALU.add) \
                      .then_inc(sem("mod_cols"), 1)

            def h_lo(n, k):
                wait(dve, "h_hi", KD * n + k + 1)
                nc.vector.tensor_tensor(HL[k][:, :], HT[:, k % 2], HH[k][:, :], ALU.subtract).then_inc(sem("h_lo"), 1)

            def modulate(l, n, shift, scale, streams, first, cut_):
                for k in range(KD):
                    dst = HT[:, k % 2] if cut_ else HB[:, k]
                    if cut_ and k >= 2:
                        wait(dve, "h_lo", KD * n + k - 1)
                    for s in streams:
                        tok = slice(TC, T) if s else slice(0, TC)
                        wait(dve, first[0], first[1] + k + 1)
                        ins = nc.vector.tensor_scalar(dst[:, tok], X[:, k, tok],
                                                      mc[:, l, s, scale * KD + k:scale * KD + k + 1],
                                                      mc[:, l, s, shift * KD + k:shift * KD + k + 1], ALU.mult, ALU.add)
                    ins.then_inc(sem("h_ready"), 1)
                    if cut_ and k:
                        h_lo(n, k - 1)
                if cut_:
                    h_lo(n, KD - 1)
                wait(dve, "h_ready", KD * (n + 1))
                tok = slice(TC if streams == (1,) else 0, T)
                nc.vector.tensor_scalar(X[:, :, tok], X[:, :, tok], ALPHA, None, ALU.mult).then_inc(sem("xa"), 1)

            def ln_dve(n, tok):
                wait(dve, "ln_mean", n + 1)
                for k in range(KD):
                    nc.vector.tensor_tensor(X[:, k, tok], X[:, k, tok], bank[4][:, tok], ALU.subtract) \
                      .then_inc(sem("ln_d"), 1)
                wait(dve, "ln_vmm", KD * (n + 1))
                nc.vector.tensor_scalar(RSTD[:, tok], bank[5][:, tok], LN_EPS, None, ALU.add).then_inc(sem("ln_ve"), 1)
                wait(dve, "ln_std", n + 1)
                link(nc.vector.reciprocal(RSTD[:, tok], RSTD[:, tok]))
                wait(dve, "ln_sq", KD * (n + 1))
                for k in range(KD):
                    nc.vector.tensor_tensor(X[:, k, tok], X[:, k, tok], RSTD[:, tok], ALU.mult).then_inc(sem("ln_norm"), 1)

            mod_cols(0)
            wait(dve, "masks", 1)
            for l in range(L):
                wait(dve, "mod_cols", 3 * l + 1)
                modulate(l, 2 * l, 0, 1, (0, 1), ("xT_act", 0) if l == 0 else ("ln_x", KD * (2 * l - 1)), True)
                s0 = split_of[("in", l, 0)]
                for u in range(2):
                    mod_sums(dve, ("in", l, u))
                for ct in range(NCT):
                    j = ct - (5 * NP + 3)
                    if j >= 0:
                        wait(dve, "proj_mm", NCT * l + ct + 1)
                        wait(dve, "proj_act", (5 * NP + 3) * l + 4 * NP + 3 + j + 1)
                        tok = CTOK(l, ct)
                        nc.vector.tensor_tensor(U[:, j, tok], CC[:, j, tok], bank[ct % 4][:, tok], ALU.mult) \
                          .then_inc(sem("proj_u"), 1)
                    if ct % 2 and s0 + ct // 2 + 2 <= split_of[("in", l, NCT // 2)]:
                        mod_sums(dve, ("in", l, ct // 2 + 2))
                    if l == 0 and ct == 17:
                        mod_cols(1)
                    if (ct - 8) % 3 == 0 and 0 <= (ct - 8) // 3 < NP:
                        j = (ct - 8) // 3
                        wait(dve, "proj_act", (5 * NP + 3) * l + NP + j + 1)
                        nc.vector.tensor_scalar(KKN[:, j], K[:, j], pcol(l, "kk", j), None, ALU.mult) \
                          .then_inc(sem("kk_raw"), 1)
                    if (ct - 11) % 3 == 0 and 0 <= (ct - 11) // 3 < NP:
                        j = (ct - 11) // 3
                        wait(dve, "kk_mm", NP * l + j + 1)
                        nc.vector.tensor_scalar(tmp_k(j), bank[4 + j % 2][:], 1e-24, None, ALU.max) \
                          .then_inc(sem("kk_ss"), 1)
                    if (ct - 13) % 3 == 0 and 0 <= (ct - 13) // 3 < NP:
                        j = (ct - 13) // 3
                        wait(dve, "kk_norm", NP * l + j + 1)
                        link(nc.vector.reciprocal(tmp_k(j), tmp_k(j)))
                        nc.vector.tensor_tensor(KKN[:, j], KKN[:, j], tmp_k(j), ALU.mult).then_inc(sem("kk_done"), 1)
                if l == 0:
                    wait(dve, "mod_mm", 8 + 2)
                wait(dve, "proj_u", NP * (l + 1))
                stt = nc.vector.scalar_tensor_tensor
                for j in range(NP):
                    m, ctok = MIX[:, NP + j], LTOK(l)
                    link(nc.vector.tensor_scalar(m[:, ctok], U[:, j, ctok], pcol(l, "conv", NP + j), None, ALU.mult))
                    rows = [(m[:, TC:T].rearrange("p (r w) -> p r w", w=GRID),
                             U[:, j, TC:T].rearrange("p (r w) -> p r w", w=GRID), GRID)]
                    if l < L - 1:
                        rows.append((m[:, None, 0:TC], U[:, j, None, 0:TC], TC))
                    for tap, dst, src in ((0, 1, 0), (2, 0, 1)):
                        for mr, ur, n in rows:
                            link(stt(out=mr[:, :, dst:n - 1 + dst], in0=ur[:, :, src:n - 1 + src],
                                     scalar=pcol(l, "conv", tap * NP + j), in1=mr[:, :, dst:n - 1 + dst],
                                     op0=ALU.mult, op1=ALU.add))
                    link(nc.vector.tensor_tensor(m[:, ctok], m[:, ctok], CB[:, j, ctok], ALU.mult))
                for i in range(2 * NP):
                    n = 4 * NP * l + i
                    d, j = i // NP, i % NP
                    wait(dve, "lora_sig", n + 1)
                    for t in range(NT):
                        ins = nc.vector.tensor_tensor_scan(Q[:, d, j, t, 1:P + 1], ones_t,
                                                           tmp[:, i % 2, t * P:(t + 1) * P], 0.0, ALU.mult, ALU.add)
                    ins.then_inc(sem("lora_use"), 1)
                link(nc.vector.memset(Qflat[:, :, 0:1], 0.0))
                wait(dve, "lora_use", 4 * NP * l + 2 * NP)
                link(nc.vector.tensor_copy(qm[:], Qflat[:, :, P // 2]))
                nc.vector.tensor_tensor(qt[:], Qflat[:, :, P], qm[:], ALU.subtract).then_inc(sem("q_in"), 1)
                for i in range(2 * NP):
                    n = 4 * NP * l + 2 * NP + i
                    d, j = i // NP, i % NP
                    wait(dve, "lora_sig", n + 1)
                    nc.vector.tensor_scalar(KDIR[:, d, j], tmp[:, i % 2], pcol(l, "ka", j), one_ka[:, l, j:j + 1],
                                            ALU.mult, ALU.add).then_inc(sem("kdir_f"), 1)
                    nc.vector.scalar_tensor_tensor(out=BV[:, d, j], in0=KKN[:, j], scalar=-1.0, in1=tmp[:, i % 2],
                                                   op0=ALU.mult, op1=ALU.mult).then_inc(sem("lora_use"), 1)
                wait(dve, "lora_use", 4 * NP * (l + 1))
                wait(dve, "e12", l + 1)
                for d in range(2):
                    for j in range(3):
                        a, b = TILE(4 * d + j), TILE(4 * d + j + 1)
                        post, pre = (e2, e1) if d == 0 else (e1, e2)
                        link(nc.vector.tensor_tensor(fac[:, d, :, j], post[:, d, :, a], pre[:, d, :, b], ALU.mult))
                link(nc.vector.memset(MC[:], 0.0))
                link(nc.vector.memset(MI[:], 0.0))
                mi = MI.rearrange("p (a h) n -> p a h n", h=2)
                link(nc.vector.tensor_copy(mi[64:128, :, 0, :], ident[64:128, None, 64:128].to_broadcast([64, NP, HS])))
                nc.vector.tensor_copy(mi[0:64, :, 1, :], ident[0:64, None, 0:64].to_broadcast([64, NP, HS])) \
                  .then_inc(sem("prep_done"), 1)
                if l == 0:
                    mod_cols(2)

                def stage(cn, st):
                    d, tj = st // 4, TILE(st)
                    tok = slice(tj * P, (tj + 1) * P)
                    wait(dve, "ex", cn + 1)
                    wait(dve, "pe_tk", 2 * cn)
                    wait(dve, "zr", cn)
                    nc.vector.tensor_tensor(BS, BV[:, d, :, tok], EX[:, 1], ALU.mult)
                    nc.vector.tensor_tensor(KS, KDIR[:, d, :, tok], EX[:, 1], ALU.mult)
                    ins = nc.vector.tensor_tensor(AS, KKN[:, :, tok], EX[:, 2], ALU.mult)
                    if reads_out(l, st):
                        ins = nc.vector.tensor_tensor(rt[:, st % 2], R[:, :, tok], EX[:, 0], ALU.mult)
                    ins.then_inc(sem("staged"), 1)

                wait(dve, "prep_done", l + 1)
                wait(dve, "kdir", 2 * NP * (l + 1))
                stage(8 * l, 0)
                for st in range(8):
                    d, tj, cn = st // 4, TILE(st), 8 * l + st
                    tok = slice(tj * P, (tj + 1) * P)
                    strict = tri[:, d:d + 1, :].to_broadcast([P, 2, P])
                    incl = tri[:, 2 + d:3 + d, :].to_broadcast([P, 2, P])
                    for q in range(2):
                        w, b = wk[q], 4 * q
                        n = 2 * cn + q + 1
                        wait(dve, "pe_s1", n)
                        for p in range(2):
                            ins = nc.vector.tensor_tensor(w["LT"][:, 2 * p:2 * p + 2], pk(b + p, 4, P)[:, 0:2], strict,
                                                          ALU.mult)
                        ins.then_inc(sem("dve_lt"), 1)
                        wait(dve, "dve_lt", n)
                        link(nc.vector.tensor_tensor(w["TT"], w["LT"], level[:, 0:1, :].to_broadcast([P, 4, P]),
                                                     ALU.mult))
                        nc.vector.tensor_tensor(w["TT"], w["TT"], ident[:, None, :].to_broadcast([P, 4, P]), ALU.add) \
                            .then_inc(sem("t0_done"), 1)
                        if reads_out(l, st):
                            for p in range(2):
                                ins = nc.vector.tensor_tensor(w["RB"][:, 2 * p:2 * p + 2], pk(b + p, 4, P)[:, 2:4],
                                                              incl, ALU.mult)
                            ins.then_inc(sem("dve_rb"), 1)
                    for q in range(2):
                        w, b = wk[q], 4 * q
                        n = 2 * cn + q + 1
                        wait(dve, "pe_s2", n)
                        for p in range(2):
                            ins = nc.vector.tensor_tensor(w["AK"][:, 2 * p:2 * p + 2], pk(b + 2 + p, 4, P)[:, 0:2],
                                                          strict, ALU.mult)
                            if reads_out(l, st):
                                ins = nc.vector.tensor_tensor(w["RK"][:, 2 * p:2 * p + 2], pk(b + 2 + p, 4, P)[:, 2:4],
                                                              incl, ALU.mult)
                        ins.then_inc(sem("dve_ak"), 1)
                    for k in range(6):
                        for q in range(2):
                            w, b = wk[q], 4 * q
                            if k < 5:
                                wait(dve, "pe_u1", (5 * cn + k) * 2 + q + 1)
                                wait(dve, "act_t1", 2 * cn + q + 1)
                                if k:
                                    wait(dve, "dve_t", (5 * cn + k - 1) * 2 + q + 1)
                                nc.vector.tensor_tensor(w["T"], w["T"], pk(b + 1, 4, P), ALU.add).then_inc(sem("dve_t"), 1)
                            wait(dve, "pe_u2", (6 * cn + k) * 2 + q + 1)
                            nc.vector.tensor_tensor(w["TT"], w["TT"], pk(b + 2, 4, P), ALU.add).then_inc(sem("dve_tt"), 1)
                        if k == 2 and st < 7:
                            stage(cn + 1, st + 1)
                    for q in range(2 if reads_out(l, st) else 0):
                        w, b = wk[q], 4 * q
                        n = 2 * ybefore[l, st] + q + 1
                        yw = w["YW"].rearrange("p (a h) n -> p a h n", h=2)
                        src = pk(b, 2, 2, P)
                        wait(dve, "pe_yw", n)
                        r_ = rt[:, st % 2, 2 * q:2 * q + 2]
                        nc.vector.tensor_tensor(yw[0:64, :, 0, :], src[0:64, :, 0, :], r_[0:64], ALU.add)
                        nc.vector.tensor_tensor(yw[64:128, :, 1, :], src[64:128, :, 1, :], r_[64:128], ALU.add) \
                          .then_inc(sem("dve_yw"), 1)
                    for q in range(2):
                        w, b = wk[q], 4 * q
                        n = 2 * cn + q + 1
                        dst = Y[:, 2 * q:2 * q + 2, tok]
                        if reads_out(l, st):
                            wait(dve, "pe_y", 2 * ybefore[l, st] + q + 1)
                        if not reads_out(l, st):
                            pass
                        elif d == 0:
                            nc.vector.tensor_copy(dst, pk(b + 2, 2, P)).then_inc(sem("y_done"), 1)
                        else:
                            nc.vector.tensor_tensor(dst, dst, pk(b + 2, 2, P), ALU.add).then_inc(sem("y_done"), 1)
                        mcq, mtq = MC[:, 2 * q:2 * q + 2], mt[:, 2 * q:2 * q + 2]
                        miq = MI.rearrange("p (a h) n -> p a h n", h=2)[:, 2 * q:2 * q + 2]
                        wait(dve, "pe_m", n)
                        if st % 4 == 3:
                            nc.vector.memset(mcq, 0.0)
                            nc.vector.memset(miq[0:64, :, 0, :], 0.0)
                            nc.vector.memset(miq[64:128, :, 1, :], 0.0).then_inc(sem("state_done"), 1)
                        else:
                            link(nc.vector.tensor_tensor(mtq, mcq, pk(b + 3, 2, HS), ALU.add))
                            link(nc.vector.tensor_tensor(mcq, mtq, fac[:, d, 2 * q:2 * q + 2, st % 4].unsqueeze(2)
                                                         .to_broadcast([P, 2, HS]), ALU.mult))
                            nc.vector.tensor_copy(miq[0:64, :, 0, :], mcq[0:64])
                            nc.vector.tensor_copy(miq[64:128, :, 1, :], mcq[64:128]).then_inc(sem("state_done"), 1)
                rtok = LTOK(l)
                wait(dve, "y_done", YTOT[l])
                for j in range(NP):
                    wait(dve, "gn_mm", NP * l + j + 1)
                    nc.vector.scalar_tensor_tensor(out=Y[:, j, rtok], in0=bank[j % 2][:, rtok], scalar=-1.0 / HS,
                                                   in1=Y[:, j, rtok], op0=ALU.mult, op1=ALU.add).then_inc(sem("gn_d"), 1)
                for j in range(NP):
                    link(nc.vector.tensor_tensor(RTB[:, j, rtok], KDIR[:, 0, j, rtok], KDIR[:, 1, j, rtok], ALU.add))
                    nc.vector.scalar_tensor_tensor(out=RTB[:, j, rtok], in0=R[:, j, rtok], scalar=pcol(l, "rk", j),
                                                   in1=RTB[:, j, rtok], op0=ALU.mult, op1=ALU.mult) \
                      .then_inc(sem("bonus_in"), 1)
                for j in range(NP):
                    wait(dve, "gn_vmm", NP * l + j + 1)
                    nc.vector.tensor_scalar(RRS[:, j, rtok], bank[2 + j % 2][:, rtok], 1.0 / HS, GN_EPS, ALU.mult, ALU.add) \
                      .then_inc(sem("gn_ve"), 1)
                for j in range(NP):
                    wait(dve, "gn_std", NP * l + j + 1)
                    link(nc.vector.reciprocal(RRS[:, j, rtok], RRS[:, j, rtok]))
                    wait(dve, "gn_sq", NP * l + j + 1)
                    nc.vector.tensor_tensor(Y[:, j, rtok], Y[:, j, rtok], RRS[:, j, rtok], ALU.mult) \
                      .then_inc(sem("gn_norm"), 1)
                for j in range(NP):
                    wait(dve, "bonus_mm", NP * l + j + 1)
                    link(nc.vector.tensor_tensor(RTB[:, j, rtok], V[:, j, rtok], bank[4 + j % 2][:, rtok], ALU.mult))
                    wait(dve, "gn_aff", NP * l + j + 1)
                    link(nc.vector.tensor_tensor(Y[:, j, rtok], Y[:, j, rtok], RTB[:, j, rtok], ALU.add))
                    wait(dve, "gate_mm", NP * (l + 1))
                    nc.vector.tensor_tensor(MIX[:, j, rtok], Y[:, j, rtok], bank[(6, 7, 0, 1)[j]][:, rtok], ALU.mult) \
                      .then_inc(sem("mix"), 1)
                for k in range(KD):
                    wait(dve, "mix_hi", KD * l + k + 1)
                    nc.vector.tensor_tensor(HL[k][:, rtok], MIX[:, k, rtok], HH[k][:, rtok], ALU.subtract) \
                      .then_inc(sem("mix_lo"), 1)
                s0 = split_of[("out", l, 0)]
                split_lo(dve, s0)
                split_lo(dve, s0 + 1)
                wait(dve, "mod_cols", 3 * l + 3)
                for ct in range(KD):
                    if ct % 2 == 0 and ct >= 2 and ct // 2 + 1 < KD // 2:
                        split_lo(dve, s0 + ct // 2 + 1)
                    wait(dve, "out_mm", KD * l + ct + 1)
                    for s in ((0, 1) if l < L - 1 else (1,)):
                        tok = slice(TC, T) if s else slice(0, TC)
                        ins = nc.vector.scalar_tensor_tensor(out=X[:, ct, tok], in0=bank[ct % 4][:, tok],
                                                             scalar=mc[:, l, s, 2 * KD + ct:2 * KD + ct + 1],
                                                             in1=X[:, ct, tok], op0=ALU.mult, op1=ALU.add)
                    ins.then_inc(sem("z"), 1)
                ln_dve(2 * l, LTOK(l))
                if l == 0:
                    modulate(0, 1, 3, 4, (0, 1), ("ln_x", 0), True)
                    def acc(g):
                        for m in range(KD):
                            wait(dve, "ffn_y", KD * g + m + 1)
                            src = bank[4 + m % 4][:]
                            if g == 0:
                                nc.vector.tensor_copy(FACC[:, m], src).then_inc(sem("ffn_acc"), 1)
                            else:
                                if m == 0:
                                    wait(dve, "ffn_acc", KD * g)
                                nc.vector.tensor_tensor(FACC[:, m], FACC[:, m], src, ALU.add).then_inc(sem("ffn_acc"), 1)
                    NG = FF // 256
                    s0 = split_of[("w1", 0, 0)]
                    for key, _ in splits[s0:s0 + 2]:
                        mod_sums(dve, key)
                    for j, ((kind, _, g), _) in enumerate(splits[s0:s0 + 3 * NG]):
                        if kind == "w1":
                            for f in (2 * g, 2 * g + 1):
                                wait(dve, "ffn_sig", f + 1)
                                wait(dve, "ffn_glo", f - 1)
                                nc.vector.tensor_tensor(FP[:, f % 2], FS[:, f % 2], bank[f % 2][:], ALU.mult) \
                                  .then_inc(sem("ffn_s"), 1)
                        elif kind == "w3":
                            for f in (2 * g, 2 * g + 1):
                                wait(dve, "ffn_h3", f + 1)
                                wait(dve, "ffn_s", f + 1)
                                nc.vector.tensor_tensor(FP[:, f % 2], FP[:, f % 2], bank[2 + f % 2][:], ALU.mult) \
                                  .then_inc(sem("ffn_g"), 1)
                            for f in (2 * g, 2 * g + 1):
                                wait(dve, "ffn_ghi", f + 1)
                                nc.vector.tensor_tensor(GL[f % 4], FP[:, f % 2], GH[f % 4], ALU.subtract) \
                                  .then_inc(sem("ffn_glo"), 1)
                            if g in reduce_at:
                                mod_cols(reduce_at[g])
                        else:
                            acc(g)
                        if j + 2 < 3 * NG:
                            mod_sums(dve, splits[s0 + j + 2][0])
                    wait(dve, "ffn_acc", KD * (FF // 256))
                    for m in range(KD):
                        for s in (0, 1):
                            tok = slice(TC, T) if s else slice(0, TC)
                            ins = nc.vector.scalar_tensor_tensor(out=X[:, m, tok], in0=FACC[:, m, tok],
                                                                 scalar=mc[:, 0, s, 5 * KD + m:5 * KD + m + 1],
                                                                 in1=X[:, m, tok], op0=ALU.mult, op1=ALU.add)
                        ins.then_inc(sem("z"), 1)
                    ln_dve(1, slice(0, T))
            moe_dve(dve, ln_dve, modulate, link)

        @block.tensor
        def _(pe):
            mm = nc.tensor.matmul
            wait(pe, "consts", 1)
            wait(pe, "c_load", 32)
            nc.tensor.transpose(bank[5][:, 0:2 * KD], crow, ident[0:2 * KD, 0:2 * KD]).then_inc(sem("c_T"), 1)
            wait(pe, "par_load", 13 * 16)
            nc.tensor.transpose(bank[4][:, 0:P], par_rows, ident).then_inc(sem("par_T"), 1)
            wait(pe, "x_load", 32)
            for k in range(KD):
                wait(pe, "xT_act", k - 3)
                for t in range(NT):
                    ins = nc.tensor.transpose(bank[k % 4][:, t * P:(t + 1) * P], xrows[:, t, k * P:(k + 1) * P], ident)
                ins.then_inc(sem("xT"), 1)
            wait(pe, "par", 1)
            wait(pe, "par_load", 2 * 13 * 16)
            nc.tensor.transpose(bank[4][:, 0:P], par_rows, ident).then_inc(sem("par_T"), 1)

            def mod_first():
                wait(pe, "c_silu", 1)
                for u in range(8):
                    key = ("mod", 0, u)
                    wait_unit(pe, key)
                    wv = slot_view(key)
                    q, half = u % 4, u // 4
                    for k in range(KD):
                        ins = mm(bank[6][32 * q:32 * q + 32, 256 * half:256 * half + 256], cs[:, 2 * k:2 * k + 32], wv[:, k, :],
                                 start=(k == 0), stop=(k == KD - 1))
                    ins.then_inc(sem("mod_mm"), 1)

            def mod_reduce(m):
                wait(pe, "mod_acc", acc_count(m, KD - 1))
                wait(pe, "mod_rows", m)
                for u in range(8):
                    q, half = u % 4, u // 4
                    for s in range(2):
                        ins = mm(bank[6][32 * q:32 * q + 32, 256 * half:256 * half + 256], cs[:, one - s:one - s + 32],
                                 ACC[:, s, 256 * u:256 * (u + 1)], start=(s == 0), stop=(s == 1))
                ins.then_inc(sem("mod_mm"), 1)

            def mod_turn(m):
                wait(pe, "mod_rows", m + 1)
                wait(pe, "par", 2)
                for i in range(4):
                    ins = nc.tensor.transpose(bank[(7, 7, 5)[m % 3]][:, i * P:(i + 1) * P], mrow[:, i * P:(i + 1) * P],
                                              ident)
                ins.then_inc(sem("mod_T"), 1)

            def ln_pe(n, tok):
                for k in range(KD):
                    wait(pe, "z", KD * n + k + 1)
                    ins = mm(bank[4][:, tok], mean_w[:], X[:, k, tok], start=(k == 0), stop=(k == KD - 1))
                ins.then_inc(sem("ln_mean"), 1)
                for k in range(KD):
                    wait(pe, "ln_sq", KD * n + k + 1)
                    mm(bank[5][:, tok], mean_w[:], SQ[:, k % 2, tok], start=(k == 0), stop=(k == KD - 1)) \
                        .then_inc(sem("ln_vmm"), 1)

            mod_first()
            mod_turn(0)
            wait(pe, "masks", 1)
            for l in range(L):
                n_act = 5 * NP + 3
                for ct in range(NCT):
                    key = ("in", l, ct // 2)
                    wait_split(pe, key)
                    wh, wl = split_views(key)
                    tok, col = CTOK(l, ct), slice((ct % 2) * P, (ct % 2 + 1) * P)
                    if ct >= 4:
                        if ct - 4 < n_act:
                            wait(pe, "proj_act", n_act * l + ct - 3)
                        else:
                            wait(pe, "proj_u", NP * l + ct - 3 - n_act)
                    if ct == 0:
                        wait(pe, "h_lo", KD * (2 * l + 1))
                    three(bank[ct % 4][:, tok], [((wh[:, k, col], wl[:, k, col]), (HH[k][:, tok], HL[k][:, tok]))
                                                 for k in range(KD)]).then_inc(sem("proj_mm"), 1)
                    if (ct - 10) % 3 == 0 and 0 <= (ct - 10) // 3 < NP:
                        j = (ct - 10) // 3
                        wait(pe, "kk_sq", NP * l + j + 1)
                        if j >= 2:
                            wait(pe, "kk_ss", NP * l + j - 1)
                        mm(bank[4 + j % 2][:], heads, tmp_k(j), start=True, stop=True).then_inc(sem("kk_mm"), 1)
                    if l == 0 and ct == 7:
                        mod_reduce(1)
                    if l == 0 and ct == 13:
                        wait(pe, "mod_cols", 1)
                        mod_turn(1)
                if l == 0:
                    mod_reduce(2)
                    wait(pe, "mod_rows", 3)
                wait(pe, "lora_load", 64 * (l + 1))
                wait(pe, "proj_u", NP * (l + 1))
                for i in range(4 * NP):
                    n = 4 * NP * l + i
                    kind, d, j = i // (2 * NP), i // NP % 2, i % NP
                    if i >= 4:
                        wait(pe, "lora_sig", n - 3)
                    mm(bank[i % 4][:], w2z[:, kind, d, j * P:(j + 1) * P], (WD, AD)[kind], start=True, stop=True) \
                        .then_inc(sem("lora_mm"), 1)
                wait(pe, "kk_ss", NP * (l + 1))
                if l == 0:
                    mod_turn(2)
                wait(pe, "lora_sig", 4 * NP * (l + 1))
                for t in range(NT):
                    wait(pe, "vtok", NT * l + t - 1)
                    wait(pe, "proj_act", n_act * l + 3 * NP)
                    for j in range(NP):
                        ins = nc.tensor.transpose(bank[2 + t % 2][:, j * P:(j + 1) * P], V[:, j, t * P:(t + 1) * P],
                                                  ident)
                    ins.then_inc(sem("vT"), 1)
                for st in range(8):
                    d, tj, cn = st // 4, TILE(st), 8 * l + st
                    tok = slice(tj * P, (tj + 1) * P)
                    wait(pe, "staged", cn + 1)
                    wait(pe, "zr", cn + 1)
                    if st == 0:
                        wait(pe, "mod_cols", 3 * l + 3)
                        wait(pe, "vtok", NT * (l + 1))
                    for q in range(2):
                        w, b = wk[q], 4 * q
                        n = 2 * cn + q + 1
                        ny = 2 * ybefore[l, st] + q - 1
                        cols = 4 * P if reads_out(l, st) else 2 * P
                        wait(pe, "dve_yw", ny)
                        wait(pe, "act_yw", ny)
                        wait(pe, "act_gt", n - 2)
                        for p in range(2):
                            ins = mm(bank[b + p][:, 0:cols], BS[:, 2 * q + p],
                                     ZR[:, 2 * q + p].rearrange("p a n -> p (a n)")[:, 0:cols], start=True, stop=True)
                        ins.then_inc(sem("pe_s1"), 1)
                        wait(pe, "y_done", ny)
                        wait(pe, "state_done", n - 2)
                        for p in range(2):
                            ins = mm(bank[b + 2 + p][:, 0:cols], KS[:, 2 * q + p],
                                     ZR[:, 2 * q + p].rearrange("p a n -> p (a n)")[:, 0:cols], start=True, stop=True)
                        ins.then_inc(sem("pe_s2"), 1)
                    for q in range(2):
                        w, b = wk[q], 4 * q
                        n = 2 * cn + q + 1
                        wait(pe, "dve_lt", n)
                        if reads_out(l, st):
                            wait(pe, "dve_rb", 2 * ybefore[l, st] + q + 1)
                        for i, s in enumerate((AS, AS, BS, BS)):
                            ins = nc.tensor.transpose(pk(b, 4, P)[:, i], s[:, 2 * q + i % 2], ident)
                        ins.then_inc(sem("pe_tab"), 1)
                        for i in range(2):
                            ins = nc.tensor.transpose(pk(b + 1, 4, P)[:, i], KS[:, 2 * q + i], ident)
                        ins.then_inc(sem("pe_tk"), 1)
                    for q in range(2):
                        w, b = wk[q], 4 * q
                        n = 2 * cn + q + 1
                        wait(pe, "dve_ak", n)
                        wait(pe, "t0_done", n)
                        for i in range(4):
                            ins = nc.tensor.transpose(pk(b + 2, 4, P)[:, i], w["TT"][:, i], ident)
                        ins.then_inc(sem("pe_t1"), 1)
                    for q in range(2):
                        w, b = wk[q], 4 * q
                        n = 2 * cn + q + 1
                        wait(pe, "vs", cn + 1)
                        for i in range(4):
                            ins = mm(pk(b + 3, 4, P)[:, i], w["AK"][:, i], VS[:, 2 * q + i // 2], start=True, stop=True)
                        ins.then_inc(sem("pe_ax"), 1)
                    for k in range(6):
                        for q in range(2):
                            w, b = wk[q], 4 * q
                            n = 2 * cn + q + 1
                            wait(pe, "pool_lm", (6 * cn + k) * 2 + q + 1)
                            if k == 0:
                                wait(pe, "act_tab", n)
                                wait(pe, "act_t1", n)
                            else:
                                wait(pe, "dve_t", (5 * cn + k - 1) * 2 + q + 1)
                            for i in range(4):
                                ins = mm(pk(b, 4, P)[:, i], w["LM"][:, k % 2, i], w["T"][:, i], start=True, stop=True)
                            ins.then_inc(sem("pe_x"), 1)
                        for q in range(2):
                            w, b = wk[q], 4 * q
                            n = 2 * cn + q + 1
                            wait(pe, "act_xs", (6 * cn + k) * 2 + q + 1)
                            if k == 0:
                                wait(pe, "act_tk", n)
                            else:
                                wait(pe, "dve_tt", (6 * cn + k - 1) * 2 + q + 1)
                            if k < 5:
                                for i in range(4):
                                    ins = mm(pk(b + 1, 4, P)[:, i], w["TT"][:, i], w["XS"][:, i], start=True, stop=True)
                                ins.then_inc(sem("pe_u1"), 1)
                            for i in range(4):
                                ins = mm(pk(b + 2, 4, P)[:, i], w["XS"][:, i], w["TT"][:, i], start=True, stop=True)
                            ins.then_inc(sem("pe_u2"), 1)
                    for q in range(2):
                        w, b = wk[q], 4 * q
                        n = 2 * cn + q + 1
                        wait(pe, "dve_tt", (6 * cn + 5) * 2 + q + 1)
                        wait(pe, "act_ax", n)
                        for i in range(4):
                            ins = mm(pk(b + 3, 4, P)[:, i], w["TT"][:, i], w["XA"][:, i], start=True, stop=True)
                        ins.then_inc(sem("pe_uw"), 1)
                    for q in range(2):
                        w, b = wk[q], 4 * q
                        n = 2 * cn + q + 1
                        wait(pe, "act_uw", n)
                        wof, uof = (0, 64), (64, 0)
                        for i in range(4):
                            p, h = i // 2, i % 2
                            ins = mm(bank[b + 1][64 * h:64 * h + 64, HS * p:HS * p + HS],
                                     w["UW"][:, i, wof[h]:wof[h] + 64], w["BT"][:, p, 64 * h:64 * h + 64],
                                     start=True, stop=True)
                        ins.then_inc(sem("pe_gt"), 1)
                        for i in range(4 if reads_out(l, st) else 0):
                            p, h = i // 2, i % 2
                            mm(pk(b, 4, P)[:, i], w["UW"][:, i], w["RB"][:, i], start=True, stop=False,
                               skip_group_check=True)
                            ins = mm(pk(b, 4, P)[64 - 64 * h:128 - 64 * h, i], VS[:, 2 * q + p, 64 * h:64 * h + 64],
                                     w["RK"][:, i], start=False, stop=True, skip_group_check=True)
                        if reads_out(l, st):
                            ins.then_inc(sem("pe_yw"), 1)
                    for q in range(2):
                        w, b = wk[q], 4 * q
                        n = 2 * cn + q + 1
                        ny = 2 * ybefore[l, st] + q + 1
                        if reads_out(l, st):
                            wait(pe, "dve_yw", ny)
                            wait(pe, "act_yw", ny)
                        wait(pe, "state_done", n - 2)
                        for i in range(4 if reads_out(l, st) else 0):
                            p, h = i // 2, i % 2
                            ins = mm(bank[b + 2][64 * h:64 * h + 64, P * p:P * (p + 1)], MI[:, 4 * q + i], w["YW"][:, i],
                                     start=True, stop=True)
                        if reads_out(l, st):
                            ins.then_inc(sem("pe_y"), 1)
                        wait(pe, "act_gt", n)
                        for i in range(4):
                            p, h = i // 2, i % 2
                            o_ = bank[b + 3][64 * h:64 * h + 64, HS * p:HS * p + HS]
                            mm(o_, w["BT"][:, p, 64 * h:64 * h + 64], w["UW"][:, i, uof[h]:uof[h] + 64],
                               start=True, stop=False)
                            mm(o_, w["KT"][:, p, 64 * h:64 * h + 64], VS[:, 2 * q + p, 64 * h:64 * h + 64],
                               start=False, stop=False)
                            ins = mm(o_, w["GT"][64 * h:64 * h + 64, p], MC[64 * h:64 * h + 64, 2 * q + p],
                                     start=False, stop=True)
                        ins.then_inc(sem("pe_m"), 1)
                rtok = LTOK(l)
                wait(pe, "y_done", YTOT[l])
                wait(pe, "state_done", 16 * (l + 1))
                for j in range(NP):
                    if j >= 2:
                        wait(pe, "gn_d", NP * l + j - 1)
                    mm(bank[j % 2][:, rtok], heads, Y[:, j, rtok], start=True, stop=True).then_inc(sem("gn_mm"), 1)
                for j in range(NP):
                    wait(pe, "gn_sq", NP * l + j + 1)
                    if j >= 2:
                        wait(pe, "gn_ve", NP * l + j - 1)
                    mm(bank[2 + j % 2][:, rtok], heads, RSQ[:, j, rtok], start=True, stop=True).then_inc(sem("gn_vmm"), 1)
                wait(pe, "g2_load", 16 * (l + 1))
                wait(pe, "gn_d", NP * (l + 1))
                for j in range(NP):
                    mm(bank[(6, 7, 0, 1)[j]][:, rtok], g2[:, j * P:(j + 1) * P], GD[:, rtok], start=True, stop=True) \
                        .then_inc(sem("gate_mm"), 1)
                for j in range(NP):
                    wait(pe, "bonus_in", NP * l + j + 1)
                    if j >= 2:
                        wait(pe, "mix", NP * l + j - 1)
                    mm(bank[4 + j % 2][:, rtok], heads, RTB[:, j, rtok], start=True, stop=True) \
                        .then_inc(sem("bonus_mm"), 1)
                wait(pe, "mix_lo", KD * (l + 1))
                wait(pe, "xa", 2 * l + 1)
                for ct in range(KD):
                    key = ("out", l, ct // 2)
                    wait_split(pe, key)
                    wh, wl = split_views(key)
                    col = slice((ct % 2) * P, (ct % 2 + 1) * P)
                    if ct >= 4:
                        wait(pe, "z", 2 * KD * l + ct - 3)
                    three(bank[ct % 4][:, rtok], [((wh[:, k, col], wl[:, k, col]), (HH[k][:, rtok], HL[k][:, rtok]))
                                                  for k in range(KD)]).then_inc(sem("out_mm"), 1)
                ln_pe(2 * l, LTOK(l))
                if l == 0:
                    NG = FF // 256
                    s0 = split_of[("w1", 0, 0)]
                    wait(pe, "h_lo", 2 * KD)
                    for key, _ in splits[s0:s0 + 3 * NG]:
                        kind, _, g = key
                        wait_split(pe, key)
                        wh, wl = split_views(key)
                        if kind == "w2":
                            wait(pe, "ffn_glo", 2 * g + 2)
                            if g + 1 in reduce_at:
                                wait(pe, "mod_cols", reduce_at[g + 1] + 1)
                            for m in range(KD):
                                wait(pe, "ffn_acc", KD * g + m - 3)
                                col = slice(m * P, (m + 1) * P)
                                three(bank[4 + m % 4][:], [((wh[:, i, col], wl[:, i, col]),
                                                            (GH[(2 * g + i) % 4], GL[(2 * g + i) % 4]))
                                                           for i in range(2)]).then_inc(sem("ffn_y"), 1)
                            continue
                        b, done = (0, "ffn_h1") if kind == "w1" else (2, "ffn_h3")
                        for f in (2 * g, 2 * g + 1):
                            wait(pe, "ffn_s" if kind == "w1" else "ffn_g", f - 1)
                            col = slice((f % 2) * P, (f % 2 + 1) * P)
                            three(bank[b + f % 2][:], [((wh[:, k, col], wl[:, k, col]), (HH[k][:, :], HL[k][:, :]))
                                                       for k in range(KD)]).then_inc(sem(done), 1)
                        if g in reduce_at and kind == "w1":
                            wait(pe, "ffn_acc", KD * (g - 1))
                            mod_reduce(reduce_at[g])
                        elif g in reduce_at:
                            mod_turn(reduce_at[g])
                    ln_pe(1, slice(0, T))
            moe_pe(pe, ln_pe)


_INS = ["x", "c", "ctx", "c_ctx", "w_mod", "b_mod", "w_in", "rk_w0", "rk_w2", "rk_a0", "rk_a2", "rk_kk", "rk_ka", "rk_rk",
        "rk_g2", "rk_lnx_g", "rk_lnx_b", "conv_w", "w_out", "ln1_g", "ln1_b", "ln2_g", "ln2_b", "ffn_w1", "ffn_w3",
        "ffn_w2", "router_w", "router_b", "moe_w1", "moe_w3", "moe_w2"]


def kernel(**inputs):
    import numpy as _np
    import concourse.bacc as _bacc
    from concourse import mybir as _mybir
    from concourse.bass_utils import run_bass_kernel_spmd as _run

    nc = _bacc.Bacc("TRN2", target_bir_lowering=False, num_devices=1)
    arrays, args = {}, []
    for name in _INS:
        a = _np.ascontiguousarray(inputs[name])
        arrays[f"in_{name}_dram"] = a
        args.append(nc.dram_tensor(f"in_{name}_dram", a.shape, _mybir.dt.from_np(a.dtype), kind="ExternalInput").ap())
    shape = inputs["x"].shape
    args.append(nc.dram_tensor("out_dram", shape, _mybir.dt.float32, kind="ExternalOutput").ap())
    hybrid_kernel(nc, *args)
    r = _run(nc, [arrays], core_ids=[0])
    return r.results[0]["out_dram"]
```

```python
import concourse.bass as bass
from concourse import mybir
from contextlib import ExitStack


def hybrid_kernel(nc, x, c, ctx, c_ctx, w_mod, b_mod, w_in, rk_w0, rk_w2, rk_a0, rk_a2, rk_kk, rk_ka, rk_rk, rk_g2,
                  rk_lnx_g, rk_lnx_b, conv_w, w_out, ln1_g, ln1_b, ln2_g, ln2_b, ffn_w1, ffn_w3, ffn_w2,
                  router_w, router_b, moe_w1, moe_w3, moe_w2, out):
    fp32 = mybir.dt.float32
    i32 = mybir.dt.int32
    f32r = mybir.dt.float32r
    ALU = mybir.AluOpType
    ACT = mybir.ActivationFunctionType
    AX = mybir.AxisListType

    P = 128
    L = w_mod.shape[0]
    D = x.shape[2]
    KD = D // P
    TC, TL = ctx.shape[1], x.shape[1]
    T = TC + TL
    W = rk_kk.shape[1]
    NP = W // P
    HS = 64
    NH = W // HS
    NT = T // P
    GRID = 64
    FF = ffn_w1.shape[2]
    NE = moe_w1.shape[1]
    DECAY = 0.6065306597126334
    ALPHA = float((2 * L) ** 0.25)
    LN_EPS, GN_EPS = 1e-5, 64e-5
    RING = 4
    UNIT = 2048
    MRING = 7
    MSPLIT = 3
    SLOTS = P
    NITEM = NE + TL * 2 // SLOTS
    BIG = 1.0e6

    es = ExitStack()
    with es:
        def sb(name, shape, dt=fp32):
            return es.enter_context(nc.sbuf_tensor(name, shape, dt))

        sems = {}

        def sem(name):
            if name not in sems:
                sems[name] = es.enter_context(nc.semaphore(name))
            return sems[name]

        def wait(eng, name, value):
            if isinstance(value, int) and value <= 0:
                return
            eng.wait_ge(sem(name), value)

        mean_w = sb("mean_w", [P, P])
        keep = sb("keep", [P, 3, P])
        ident, heads, ones_t = keep[:, 0, :], keep[:, 1, :], keep[:, 2, :]
        tri = sb("tri", [P, 4, P])
        level = sb("level", [P, 7, P])
        par = sb("par", [P, L, P])
        ccol = sb("ccol", [P, 2 * KD])
        csig = sb("csig", [P, 2 * KD])
        cs = sb("cs", [P, 2 * KD + 62])
        one = 2 * KD + 30
        mc = sb("mc", [P, L, 2, 6 * KD])
        one_ka = sb("one_ka", [P, L, NP])
        qm = sb("qm", [P, 2 * NP * NT])
        qt = sb("qt", [P, 2 * NP * NT])
        e1 = sb("e1", [P, 2, NP, NT])
        e2 = sb("e2", [P, 2, NP, NT])
        fac = sb("fac", [P, 2, NP, 4])
        COLS = {}
        at = 0
        for nm, n in (("b_mod", 6 * KD), ("w0", 2 * NP), ("a0", 2 * NP), ("kk", NP), ("ka", NP), ("rk", NP),
                      ("lnxg", NP), ("lnxb", NP), ("conv", 3 * NP), ("ln1g", KD), ("ln1b", KD), ("ln2g", KD),
                      ("ln2b", KD)):
            COLS[nm] = at
            at += n
        assert at == P

        def pcol(l, nm, i=0):
            return par[:, l, COLS[nm] + i:COLS[nm] + i + 1]

        o_x = 0
        o_hb = o_x + KD * T
        o_mix = o_hb + 2 * NP * NT * (P + 1)
        o_ring = o_mix + KD * T
        o_rest = o_ring + 6 * UNIT
        SIZE = 49968
        arena = sb("arena", [P, SIZE])

        arena_at = nc.sbuf_base - 4 * SIZE

        def cut(name, off, *dims):
            t = nc.alloc_sbuf_tensor_at(name, [P] + list(dims), f32r, offset=arena_at + 4 * off)
            return t[:]

        def area(off, *dims):
            n = 1
            for d in dims:
                n *= d
            assert off + n <= SIZE, (off, n)
            v = arena[:, off:off + n]
            if len(dims) == 1:
                return v
            names = "abcdef"[:len(dims)]
            return v.rearrange(f"p ({' '.join(names)}) -> p {' '.join(names)}", **dict(zip(names, dims)))

        same = area(o_rest + 8192, 8, P)
        X = area(o_x, KD, T)
        HB = area(o_hb, KD, T)
        Q = area(o_hb, 2, NP, NT, P + 1)
        Qflat = area(o_hb, 2 * NP * NT, P + 1)
        MIX = area(o_mix, KD, T)
        xrows = area(o_mix, NT, D)
        w2z = area(o_mix, 2, 2, W)
        g2 = area(o_mix, W)
        rt = area(o_mix + 512, 2, NP, P)
        o = o_rest
        R = area(o, NP, T)
        K = area(o + 2048, NP, T)
        VTK = area(o + 2048, NT, NP, P)
        V = area(o + 4096, NP, T)
        KKN = area(o + 6144, NP, T)
        KDIR = area(o + 8192, 2, NP, T)
        BV = area(o + 12288, 2, NP, T)
        CB = area(o + 16384, NP, T)
        Y = area(o + 16384, NP, T)
        CC = area(o + 18432, NP, T)
        U = area(o + 20480, NP, T)
        GD = area(o + 22528, T)
        WD = area(o + 23040, T)
        AD = area(o + 23552, T)
        o_tmp = o + 24064
        tmp = area(o_tmp, 2, T)
        o_stage = o + 18432
        EX = area(o_stage, 3, NP, P)
        BS = area(o_stage + 1536, NP, P)
        KS = area(o_stage + 2048, NP, P)
        AS = area(o_stage + 2560, NP, P)
        VS = area(o_stage + 3072, NP, P)
        MI = area(o_stage + 3584, NH, HS)
        ZR = area(o + 23040, NP, 4, P)
        MC = area(o + 23040 + 2048, NP, HS)
        mt = area(o_mix + 1536, NP, HS)
        wk = []
        for q in range(2):
            b = o_ring + q * 6144
            names = {}
            for i, nm in enumerate(("LT", "TT", "T", "XS", "XA", "RB", "AK", "RK")):
                names[nm] = area(b + 512 * i, 4, P)
            names["UW"], names["YW"] = names["LT"], names["T"]
            names["LM"] = area(b + 4096, 2, 4, P)
            names["BT"] = area(b + 5120, 2, P)
            names["KT"] = area(b + 5376, 2, P)
            names["GT"] = area(b + 5632, 2, HS)
            wk.append(names)
        o_ln = SIZE - 2048
        SQ = area(o_ln, 2, T)
        RSTD = area(o_ln + 1024, T)
        mrow = sb("mrow", [P, 512])
        par_rows = area(o_rest, P)
        crow = area(o_rest + P, P)[0:2 * KD]
        RTB = area(o + 12288, NP, T)
        RSQ = area(o + 14336, NP, T)
        RRS = area(o + 2048, NP, T)
        FS = area(o + 16384, 2, T)
        FP = area(o + 17408, 2, T)
        FACC = area(o + 18432, KD, T)

        HT = area(o_ln, 2, T)
        HH = [cut(f"h_hi{k}", o_hb + k * T, T) for k in range(KD)]
        HL = [cut(f"h_lo{k}", o + 8192 + k * T, T) for k in range(KD)]
        GH = [cut(f"g_hi{f}", o + f * T, T) for f in range(4)]
        GL = [cut(f"g_lo{f}", o + 2048 + f * T, T) for f in range(4)]
        WH = [cut(f"w_hi{i}", off, UNIT) for i, off in enumerate((o_ring + RING * UNIT, o + 12288))]
        WL = [cut(f"w_lo{i}", off + UNIT, UNIT) for i, off in enumerate((o_ring + RING * UNIT, o + 12288))]

        bank = [es.enter_context(nc.psum_tensor(f"bank{i}", [P, 512], fp32)) for i in range(8)]

        def pk(b, *dims):
            names = "abcdef"[:len(dims)]
            n = 1
            for d in dims:
                n *= d
            return bank[b][:, 0:n].rearrange(f"p ({' '.join(names)}) -> p {' '.join(names)}", **dict(zip(names, dims)))

        units = []
        index = {}

        splits = []

        def unit(key, src, nk, nm, free):
            index[key] = len(units)
            if key[0] != "mod":
                splits.append((key, free))
                free = ("w_lo", len(splits))
            units.append((src, nk, nm, (free,)))

        def acc_unit(m, k):
            l, part = m // 3, m % 3
            index["acc", m, k] = len(units)
            w = w_mod[l][P * k:P * (k + 1), 2 * D * part:2 * D * (part + 1)]
            units.append((w.rearrange("(k p) n -> p k n", p=P), 1, 2 * D,
                          (("mod_acc", acc_count(m, k)),)))

        def acc_count(m, k):
            return (KD + 1) * (m - 1) + k + 2

        NCT = w_in.shape[2] // P
        proj_cts = [list(range(NCT)), list(range(NCT))]
        beside = {}
        for l in range(L):
            if l == 0:
                for g in range(8):
                    unit(("mod", 0, g), w_mod[0][:, 256 * g:256 * (g + 1)].rearrange("(k p) n -> p k n", p=P), KD, 256,
                         ("mod_mm", g + 1))
            for u in range((NCT + 1) // 2):
                n = min(2, NCT - 2 * u)
                unit(("in", l, u), w_in[l][:, 256 * u:256 * u + P * n].rearrange("(k p) n -> p k n", p=P), KD, P * n,
                     ("proj_mm", NCT * l + 2 * u + n))
                if l == 0:
                    ms = [(1, k) for k in range(2 * u - 2, 2 * u)] if 1 <= u <= 4 else [(2, u - 6)] if u >= 6 else []
                    beside["in", l, u] = ms
                    for m, k in ms:
                        acc_unit(m, k)
            for u in range(KD // 2):
                unit(("out", l, u), w_out[l][:, 256 * u:256 * (u + 1)].rearrange("(k p) n -> p k n", p=P), KD, 256,
                     ("out_mm", KD * l + 2 * u + 2))
            if l % 2 == 0:
                NG = FF // 256

                def ffn_h_unit(nm, g):
                    w = ffn_w1 if nm == "w1" else ffn_w3
                    unit((nm, l, g), w[l // 2][:, 256 * g:256 * (g + 1)].rearrange("(k p) n -> p k n", p=P), KD, 256,
                         ("ffn_h" + nm[1], 2 * g + 2))

                def ffn_y_unit(g):
                    unit(("w2", l, g), ffn_w2[l // 2][256 * g:256 * (g + 1), :].rearrange("(k p) n -> p k n", p=P), 2, D,
                         ("ffn_y", KD * (g + 1)))
                names = [(nm, l, g) for s in range(NG + 1) for nm, g in (("w1", s), ("w3", s), ("w2", s - 1))
                         if 0 <= g < NG]
                for j, (nm, _, g) in enumerate(names):
                    if nm == "w2":
                        ffn_y_unit(g)
                    else:
                        ffn_h_unit(nm, g)
                    part, k = divmod(j - 1, 12)
                    beside[nm, l, g] = [(3 + part, k)] if 0 <= part < 3 and k < KD else []
                    for m, k in beside[nm, l, g]:
                        acc_unit(m, k)

        def slot_view(key):
            i = index[key]
            _, nk, nm, _ = units[i]
            return area(o_ring + (i % RING) * UNIT, UNIT)[:, 0:nk * nm].rearrange("p (k n) -> p k n", k=nk)

        split_of = {k: i for i, (k, _) in enumerate(splits)}

        def split_views(key):
            i = split_of[key]
            _, nk, nm, _ = units[index[key]]
            return [w[i % 2][:, 0:nk * nm].rearrange("p (k n) -> p k n", k=nk) for w in (WH, WL)]

        def wait_split(eng, key):
            eng.wait_ge(sem("w_lo"), split_of[key] + 1)

        def split_hi(act, i):
            if i >= len(splits):
                return
            key = splits[i][0]
            wait_unit(act, key)
            if i >= 2:
                wait(act, *splits[i - 2][1])
            act.activation(split_views(key)[0], slot_view(key), ACT.Copy).then_inc(sem("w_hi"), 1)

        def split_lo(pool, i):
            hi, lo = split_views(splits[i][0])
            pool.wait_ge(sem("w_hi"), i + 1)
            pool.tensor_tensor(lo, slot_view(splits[i][0]), hi, ALU.subtract).then_inc(sem("w_lo"), 1)

        ACC = area(o_mix, 2, 2 * D)
        reduce_at = {4: 3, 8: 4, 12: 5}

        def mod_sums(dve, key):
            for m, k in beside.get(key, ()):
                if k == 0:
                    if m == 1:
                        dve.wait_ge(sem("xT"), KD)
                    if m == 3:
                        dve.wait_ge(sem("mix_lo"), KD)
                    if m > 1:
                        wait(dve, "mod_mm", 7 + m)
                    nc.vector.memset(ACC[:], 0.0).then_inc(sem("mod_acc"), 1)
                wait(dve, "mod_acc", acc_count(m, k) - 1)
                wait_unit(dve, ("acc", m, k))
                for stream in range(2):
                    ins = nc.vector.scalar_tensor_tensor(out=ACC[:, stream], in0=slot_view(("acc", m, k))[:, 0, :],
                                                         scalar=cs[:, 2 * k + stream:2 * k + stream + 1],
                                                         in1=ACC[:, stream], op0=ALU.mult, op1=ALU.add)
                ins.then_inc(sem("mod_acc"), 1)

        def three(out_, pairs, first=True, last=True):
            n = len(pairs)
            for i, ((ah, al), (bh, bl)) in enumerate(pairs):
                nc.tensor.matmul(out_, ah, bh, start=(first and i == 0), stop=False)
                nc.tensor.matmul(out_, ah, bl, start=False, stop=False)
                ins = nc.tensor.matmul(out_, al, bh, start=False, stop=(last and i == n - 1))
            return ins

        def wait_unit(eng, key):
            i = index[key]
            wait(eng, f"slot{i % RING}", 16 * (i // RING + 1))


        def TILE(st):
            return st if st < 4 else (st - 4) ^ 1

        def quadrant(d):
            return (slice(HS, P), slice(0, HS)) if d == 0 else (slice(0, HS), slice(HS, P))

        def reads_out(l, st):
            return l < L - 1 or TILE(st) >= TC // P

        ybefore, yn = {}, 0
        YTOT = []
        for l_ in range(L):
            for st_ in range(8):
                ybefore[l_, st_] = yn
                yn += reads_out(l_, st_)
            YTOT.append(2 * yn)

        def CTOK(l, ct):
            both = l < L - 1 or NP <= ct < 3 * NP + 2
            return slice(0, T) if both else slice(TC, T)

        def LTOK(l):
            return slice(TC, T) if l == L - 1 else slice(0, T)

        def tmp_k(j):
            return tmp[:, j % 2]


        NI = NE + 3
        NGM = FF // 512
        rw = sb("rw", [P, KD, NE])
        rb = sb("rb", [P, NE])
        o_m = o_ring + 14 * UNIT
        table_at = [o_m + 5888]

        def table(*dims):
            n = 1
            for d in dims:
                n *= d
            v = area(table_at[0], *dims)
            table_at[0] += n
            return v

        logit = table(2, NE)
        top_v = table(2, 8)
        top_i = table(2, 8).bitcast(mybir.dt.uint32)
        top_f = table(2, 8)
        one_hot = table(2, 2, NE)
        gw = table(4, 2)
        chosen = table(2, NE)
        gate = table(2, NE)
        rank = table(2, 2, NE)
        io_i = table(P).bitcast(i32)
        io = table(P)
        it_n = table(4, NE)[0:1]
        it_ge = table(2, NI, NE)[0:1]
        it_f = table(4, NI)[0:1]
        it_i = table(3 * NI)[0:1].bitcast(i32)
        XTK = area(o_mix, 2, D)
        FA = area(o_mix + 2048, KD, TL)
        OUTT = area(o_mix, 2, D)
        GSM = area(o_m, 2, 512)
        SGM = area(o_m + 1024, 2, 512)
        YS = area(o_m + 3072, D)
        o_mlow = o_ring + MRING * UNIT + MSPLIT * 2 * UNIT
        XGH, XGL = [cut(nm, at_, KD, P) for nm, at_ in (("x_hi", o_m + 4096), ("x_lo", o_mlow))]
        GTH, GTL = [[cut(f"{nm}{r}", at_ + 4 * P * r, 4, P) for r in range(2)]
                    for nm, at_ in (("gate_hi", o_m + 2048), ("gate_lo", o_mlow + KD * P))]
        MWH, MWL = [[cut(f"{nm}{r}", o_ring + (MRING + 2 * r + part) * UNIT, UNIT) for r in range(MSPLIT)]
                    for part, nm in enumerate(("unit_hi", "unit_lo"))]
        assert o_mlow + 2 * KD * P <= o_m
        SEL = area(o_m + 5120, 2, P)
        SG = area(o_m + 5376, 2, P)
        SGT = area(o_m + 5632, TL)
        assert table_at[0] <= o_ln, (table_at, o_ln)

        order = []
        for s in range(NGM + 2):
            if s < NGM:
                order += [("w1", s, 0), ("w1", s, 1), ("w3", s, 0), ("w3", s, 1)]
            if s >= 2:
                order += [("w2", s - 2, 0), ("w2", s - 2, 1)]
        NU = len(order)
        assert NU % MRING == 0 and NU % MSPLIT == 0
        TURNS = NU // MRING
        place = {u: j for j, u in enumerate(order)}
        turned = {place["w3", g + 1, 1]: g for g in range(NGM - 1)}
        turned[place["w2", NGM - 3, 1]] = NGM - 1

        used = [len(range(r, len(units), RING)) if r < RING else 0 for r in range(MRING)]
        NS = len(splits)

        def moe_slot(j):
            nk = 2 if order[j][0] == "w2" else 4
            return area(o_ring + (j % MRING) * UNIT, UNIT).rearrange("p (k n) -> p k n", k=nk)

        def moe_split(j):
            nk = 2 if order[j][0] == "w2" else 4
            return [w[j % MSPLIT].rearrange("p (k n) -> p k n", k=nk) for w in (MWH, MWL)]

        def moe_hi(act, i, j):
            slot, n = f"slot{j % MRING}", used[j % MRING] + j // MRING
            if i is None:
                wait(act, slot, 16 * (n + 1))
            else:
                act.wait_ge(sem(slot), 16 * (TURNS * i + (n + 1)))
                act.wait_ge(sem("m_unit"), NU * i + (j - MSPLIT + 1))
            act.activation(moe_split(j)[0], moe_slot(j), ACT.Copy).then_inc(sem("w_hi"), 1)

        SHARE = UNIT // 4

        def moe_lo(eng, i, j):
            if i is None:
                eng.wait_ge(sem("w_hi"), NS + j + 1)
            else:
                eng.wait_ge(sem("w_hi"), NU * i + (NS + j + 1))
            cols, done = (slice(0, SHARE), "p_lo") if eng is nc.gpsimd else (slice(SHARE, UNIT), "w_lo")
            raw = area(o_ring + (j % MRING) * UNIT, UNIT)[:, cols]
            eng.tensor_tensor(MWL[j % MSPLIT][:, cols], raw, MWH[j % MSPLIT][:, cols], ALU.subtract) \
               .then_inc(sem(done), 1)

        def wait_lo(eng, i, j):
            eng.wait_ge(sem("w_lo"), NU * i + (NS + j + 1))
            if eng is nc.sync:
                eng.sem_inc(sem("m_turn"), 1)
            eng.wait_ge(sem("p_lo"), NU * i + (j + 1))

        def moe_pool(pool):
            def item(i, more):
                for j in range(NU):
                    split_ahead(moe_lo, pool, i, j, more)

            for j in range(MSPLIT):
                moe_lo(pool, None, j)
            pool.wait_ge(sem("items"), 1)
            last = pool.value_load(it_i[0:1, 2 * NI:2 * NI + 1], min_val=NE - 1, max_val=NI - 1)
            with pool.Fori(0, last) as i:
                item(i, True)
            item(last, False)

        def split_ahead(split, eng, i, j, more):
            if j + MSPLIT < NU:
                split(eng, i, j + MSPLIT)
            elif more:
                split(eng, i + 1, j + MSPLIT - NU)

        def moe_sp(sp):
            def load(e, i, j):
                kind, g, part = order[j]
                if kind == "w2":
                    r0 = 512 * g + 256 * part
                    src = moe_w2[0][bass.ds(e, 1)][0, r0:r0 + 256, :] if e is not None else moe_w2[0, 0, r0:r0 + 256, :]
                else:
                    w = moe_w1 if kind == "w1" else moe_w3
                    rows, cols = slice(512 * part, 512 * part + 512), slice(512 * g, 512 * g + 512)
                    src = w[0][bass.ds(e, 1)][0, rows, cols] if e is not None else w[0, 0, rows, cols]
                if i is not None:
                    wait_lo(sp, i, j - MRING)
                    if order[j] == ("w2", 0, 0):
                        sp.sem_inc(sem("m_turn"), 1)
                sp.dma_start(moe_slot(j), src.rearrange("(k p) n -> p k n", p=P)) \
                  .then_inc(sem(f"slot{j % MRING}"), 16)

            sp.wait_ge(sem("out_mm"), KD * L)
            for j in range(MRING):
                load(None, None, j)
            sp.wait_ge(sem("items"), 1)
            last = sp.value_load(it_i[0:1, 2 * NI:2 * NI + 1], min_val=NE - 1, max_val=NI - 1)
            with sp.Fori(0, last) as i:
                e = sp.value_load(it_i[0:1, bass.ds(i, 1)], min_val=0, max_val=NE - 1)
                for j in range(MRING, NU):
                    load(e, i, j)
                e1_ = sp.value_load(it_i[0:1, bass.ds(i + 1, 1)], min_val=0, max_val=NE - 1)
                for j in range(MRING):
                    load(e1_, i + 1, j)
            e = sp.value_load(it_i[0:1, bass.ds(last, 1)], min_val=0, max_val=NE - 1)
            for j in range(MRING, NU):
                load(e, last, j)

        def moe_act(act, ln_act):
            for j in range(MSPLIT):
                moe_hi(act, None, j)
            for t in range(2):
                for h in range(2):
                    act.wait_ge(sem("xtkT"), 2 * t + h + 1)
                    act.activation(XTK[:, t, 512 * h:512 * h + 512], bank[1 + h][:], ACT.Copy).then_inc(sem("xtk"), 1)
            act.wait_ge(sem("gate_d"), 1)
            act.activation(gw[:, 1, :], gw[:, 0, :], ACT.Exp).then_inc(sem("gate_e"), 1)

            def gather(i):
                for r in range(2):
                    act.wait_ge(sem("m_ga"), 2 * i + r + 1)
                    act.activation(XGH[:, 4 * r:4 * r + 4, :], pk((7, 1)[r], 4, P), ACT.Copy).then_inc(sem("m_xh"), 1)

            def item(i, more):
                for j, (kind, s, part) in enumerate(order):
                    if (kind, part) == ("w1", 1):
                        act.wait_ge(sem("m_unit"), NU * i + j + 1)
                        act.wait_ge(sem("m_s"), NGM * i + max(s - 1, 0) + 1)
                        act.activation(SGM[:, s % 2], bank[s % 2][:], ACT.Sigmoid).then_inc(sem("m_sig"), 1)
                    split_ahead(moe_hi, act, i, j, more)
                    if (kind, part) == ("w3", 1) and s == 3:
                        act.wait_ge(sem("m_sgT"), i + 1 + 1)
                        act.activation(SGT, bank[7][:, 0:TL], ACT.Copy).then_inc(sem("m_sgt"), 1)
                    if (kind, s, part) == ("w2", NGM - 3, 1) and more:
                        gather(i + 1)
                    g = turned.get(j)
                    if g is not None:
                        act.wait_ge(sem("m_tr"), NGM * i + g + 1)
                        act.activation(GTH[g % 2], pk(4, 4, P), ACT.Copy).then_inc(sem("m_gh"), 1)
                act.wait_ge(sem("m_unit"), NU * i + NU)
                act.activation(YS[:, 0:512], bank[5][:], ACT.Copy)
                act.activation(YS[:, 512:1024], bank[6][:], ACT.Copy).then_inc(sem("m_ys"), 1)

            gather(0)
            act.wait_ge(sem("items"), 1)
            last = act.value_load(it_i[0:1, 2 * NI:2 * NI + 1], min_val=NE - 1, max_val=NI - 1)
            with act.Fori(0, last) as i:
                item(i, True)
            item(last, False)
            ln_act(3, slice(TC, T), 1, "ln2g", "ln2b")
            for t in range(2):
                for h in range(2):
                    n = 2 * t + h
                    act.wait_ge(sem("outT"), n + 1)
                    ins = act.activation(OUTT[:, t, 512 * h:512 * h + 512], bank[n][:], ACT.Copy)
            ins.then_inc(sem("fin"), 1)

        def moe_dve(dve, ln_dve, modulate, link):
            modulate(1, 3, 3, 4, (1,), ("ln_x", 2 * KD), False)
            tt, ts = nc.vector.tensor_tensor, nc.vector.tensor_scalar
            dve.wait_ge(sem("iota"), 1)
            link(nc.vector.tensor_copy(io, io_i))
            for j in range(MSPLIT):
                moe_lo(dve, None, j)
            nc.vector.memset(FA[:], 0.0).then_inc(sem("m_fa"), 1)
            nc.vector.memset(YS, 0.0).then_inc(sem("m_ys"), 1)
            nc.vector.memset(SGT, 0.0).then_inc(sem("m_sgt"), 1)
            dve.sem_inc(sem("m_s"), 1)
            dve.sem_inc(sem("m_g"), 1)
            dve.sem_inc(sem("m_gt"), 1)
            dve.wait_ge(sem("router_mm"), 1)
            dve.wait_ge(sem("router_load"), 32)
            link(tt(logit, pk(0, 2, NE), rb[:, None, :].to_broadcast([P, 2, NE]), ALU.add))
            for t in range(2):
                link(nc.vector.max(top_v[:, t], logit[:, t]))
                link(nc.vector.max_index(top_i[:, t], top_v[:, t], logit[:, t]))
            link(nc.vector.tensor_copy(top_f, top_i))
            tt(gw[:, 0, :], top_v[:, :, 1], top_v[:, :, 0], ALU.subtract).then_inc(sem("gate_d"), 1)
            for n in range(2):
                for t in range(2):
                    link(ts(one_hot[:, n, t], io[:, 0:NE], top_f[:, t, n:n + 1], None, ALU.is_equal))
            tt(chosen, one_hot[:, 0], one_hot[:, 1], ALU.add).then_inc(sem("chosen"), 1)
            dve.wait_ge(sem("rank_mm"), 1)
            dve.wait_ge(sem("chosen"), 1)
            stt = nc.vector.scalar_tensor_tensor
            ps = pk(3, 3, NE)
            link(stt(out=rank[:, 0], in0=ps[:, 0:2], scalar=1.0, in1=chosen, op0=ALU.add, op1=ALU.mult))
            link(ts(rank[:, 1], rank[:, 0], -1.0 - SLOTS, None, ALU.add))
            link(ts(rank[:, 0], rank[:, 0], -1.0, None, ALU.add))
            for t in range(2):
                ins = ts(SEL[:, t], io, rank[:, 0, t, 0:1], None, ALU.is_equal)
            ins.then_inc(sem("m_sel"), 1)
            dve.wait_ge(sem("gate_e"), 1)
            link(ts(gw[:, 2, :], gw[:, 1, :], 1.0, None, ALU.add))
            link(nc.vector.reciprocal(gw[:, 2, :], gw[:, 2, :]))
            link(tt(gw[:, 3, :], gw[:, 1, :], gw[:, 2, :], ALU.mult))
            link(tt(gate, one_hot[:, 0], gw[:, 2, :].unsqueeze(2).to_broadcast([P, 2, NE]), ALU.mult))
            link(tt(one_hot[:, 1], one_hot[:, 1], gw[:, 3, :].unsqueeze(2).to_broadcast([P, 2, NE]), ALU.mult))
            link(tt(gate, gate, one_hot[:, 1], ALU.add))
            link(ts(it_n[:, 0], ps[0:1, 2], float(SLOTS), 1.0, ALU.is_gt, ALU.add))
            link(nc.vector.tensor_tensor_scan(it_n[:, 1], ones_t[0:1, 0:NE], it_n[:, 0], 0.0, ALU.mult, ALU.add))
            link(tt(it_ge[:, 0], io[0:1, 0:NI].unsqueeze(2).to_broadcast([1, NI, NE]),
                    it_n[:, 1:2, :].to_broadcast([1, NI, NE]), ALU.is_ge))
            link(tt(it_ge[:, 1], it_ge[:, 0], it_n[:, 0:1, :].to_broadcast([1, NI, NE]), ALU.mult))
            link(nc.vector.tensor_reduce(out=it_f[:, 0], in_=it_ge[:, 0], axis=AX.X, op=ALU.add))
            link(nc.vector.tensor_reduce(out=it_f[:, 1], in_=it_ge[:, 1], axis=AX.X, op=ALU.add))
            link(ts(it_f[:, 0], it_f[:, 0], float(NE - 1), None, ALU.min))
            link(tt(it_f[:, 1], io[0:1, 0:NI], it_f[:, 1], ALU.subtract))
            link(ts(it_f[:, 1], it_f[:, 1], 1.0, None, ALU.min))
            link(stt(out=it_f[:, 2], in0=it_f[:, 1], scalar=float(2 * NE), in1=it_f[:, 0], op0=ALU.mult, op1=ALU.add))
            link(ts(it_f[:, 3], it_n[:, 1, NE - 1:NE].to_broadcast([1, NI]), -1.0, None, ALU.add))
            link(nc.vector.tensor_copy(it_i[:, 0:NI], it_f[:, 0]))
            link(nc.vector.tensor_copy(it_i[:, NI:2 * NI], it_f[:, 2]))
            nc.vector.tensor_copy(it_i[:, 2 * NI:3 * NI], it_f[:, 3]).then_inc(sem("items"), 1)
            dve.wait_ge(sem("items"), 1)
            dve.wait_ge(sem("xtk"), 4)
            rank_f = rank.rearrange("p b t e -> p (b t e)")
            gate_f = gate.rearrange("p t e -> p (t e)")

            def select(i):
                col = dve.value_load(it_i[0:1, bass.ds(i + NI, 1)], min_val=0, max_val=3 * NE - 1)
                for t in range(2):
                    ins = ts(SEL[:, t], io, rank_f[:, bass.ds(col + NE * t, 1)], None, ALU.is_equal)
                ins.then_inc(sem("m_sel"), 1)

            def weigh(i):
                e = dve.value_load(it_i[0:1, bass.ds(i, 1)], min_val=0, max_val=NE - 1)
                dve.wait_ge(sem("m_sel"), i + 1)
                for t in range(2):
                    ins = ts(SG[:, t], SEL[:, t], gate_f[:, bass.ds(e + NE * t, 1)], None, ALU.mult)
                ins.then_inc(sem("m_sg"), 1)

            def scatter_add(i):
                for r in range(4):
                    dve.wait_ge(sem("m_sc"), 4 * i + r + 1)
                    tt(FA[:, 2 * r:2 * r + 2], FA[:, 2 * r:2 * r + 2], pk((7, 4)[r % 2], 2, TL), ALU.add) \
                        .then_inc(sem("m_fa"), 1)

            def gather(i):
                for r in range(2):
                    dve.wait_ge(sem("m_xh"), 2 * i + r + 1)
                    tt(XGL[:, 4 * r:4 * r + 4, :], pk((7, 1)[r], 4, P), XGH[:, 4 * r:4 * r + 4, :], ALU.subtract) \
                        .then_inc(sem("m_xg"), 1)

            def item(i, more):
                dve.wait_ge(sem("m_sgT"), i + 1)
                weigh(i)
                for j, (kind, s, part) in enumerate(order):
                    if (kind, part) == ("w1", 1):
                        dve.wait_ge(sem("m_sig"), NGM * i + s + 1)
                        if s >= 2:
                            dve.wait_ge(sem("m_tr"), NGM * i + s - 1)
                        tt(GSM[:, s % 2], SGM[:, s % 2], bank[s % 2][:], ALU.mult).then_inc(sem("m_s"), 1)
                    if (kind, part) == ("w3", 1):
                        dve.wait_ge(sem("m_unit"), NU * i + j + 1)
                        dve.wait_ge(sem("m_s"), NGM * i + s + 1 + 1)
                        tt(GSM[:, s % 2], GSM[:, s % 2], bank[2 + s % 2][:], ALU.mult).then_inc(sem("m_g"), 1)
                    if (kind, s, part) == ("w3", 0, 1):
                        dve.wait_ge(sem("m_fa"), 4 * i + 1)
                        scatter_add(i)
                    split_ahead(moe_lo, dve, i, j, more)
                    if (kind, s, part) == ("w3", 4, 1) and more:
                        select(i + 1)
                    if (kind, s, part) == ("w2", NGM - 3, 1) and more:
                        gather(i + 1)
                    g = turned.get(j)
                    if g is not None:
                        dve.wait_ge(sem("m_gh"), NGM * i + g + 1)
                        tt(GTL[g % 2], pk(4, 4, P), GTH[g % 2], ALU.subtract).then_inc(sem("m_gt"), 1)

            gather(0)
            last = dve.value_load(it_i[0:1, 2 * NI:2 * NI + 1], min_val=NE - 1, max_val=NI - 1)
            with dve.Fori(0, last) as i:
                item(i, True)
            item(last, False)
            scatter_add(last + 1)
            dve.wait_ge(sem("m_fa"), 4 * last + 8 + 1)
            for m in range(KD):
                stt(out=X[:, m, TC:T], in0=FA[:, m], scalar=mc[:, 1, 1, 5 * KD + m:5 * KD + m + 1],
                    in1=X[:, m, TC:T], op0=ALU.mult, op1=ALU.add).then_inc(sem("z"), 1)
            ln_dve(3, slice(TC, T))

        def moe_pe(pe, ln_pe):
            mm = nc.tensor.matmul
            pe.wait_ge(sem("router_load"), 32)
            pe.wait_ge(sem("h_ready"), 4 * KD)
            for t in range(2):
                for k in range(KD):
                    ins = mm(pk(0, 2, NE)[:, t], HB[:, k, TC + P * t:TC + P * (t + 1)], rw[:, k, :], start=(k == 0),
                             stop=(k == KD - 1))
            ins.then_inc(sem("router_mm"), 1)
            for t in range(2):
                for h in range(2):
                    wait(pe, "xtk", 2 * t + h - 1)
                    for k in range(4):
                        ins = nc.tensor.transpose(bank[1 + h][:, k * P:(k + 1) * P],
                                                  HB[:, 4 * h + k, TC + P * t:TC + P * (t + 1)], ident)
                    ins.then_inc(sem("xtkT"), 1)
            pe.wait_ge(sem("chosen"), 1)
            ps = pk(3, 3, NE)
            mm(ps[:, 0], tri[:, 0, :], chosen[:, 0], start=True, stop=True)
            mm(ps[:, 1], tri[:, 0, :], chosen[:, 1], start=True, stop=False)
            mm(ps[:, 1], ones_t, chosen[:, 0], start=False, stop=True)
            mm(ps[:, 2], ones_t, chosen[:, 0], start=True, stop=False)
            mm(ps[:, 2], ones_t, chosen[:, 1], start=False, stop=True).then_inc(sem("rank_mm"), 1)
            pe.wait_ge(sem("xtk"), 4)
            pe.sem_inc(sem("m_sgT"), 1)

            def gather(i):
                pe.wait_ge(sem("m_sel"), i + 1)
                for r in range(2):
                    for k in range(4):
                        for t in range(2):
                            ins = mm(pk((7, 1)[r], 4, P)[:, k], XTK[:, t, (4 * r + k) * P:(4 * r + k + 1) * P],
                                     SEL[:, t], start=(t == 0), stop=(t == 1))
                    ins.then_inc(sem("m_ga"), 1)

            def scatter(i):
                pe.wait_ge(sem("m_ys"), i + 1)
                pe.wait_ge(sem("m_sgt"), i + 1)
                pe.wait_ge(sem("m_gt"), NGM * i + 1)
                for r in range(4):
                    if r >= 2:
                        pe.wait_ge(sem("m_fa"), 4 * i + r - 1 + 1)
                    for k in range(2):
                        ins = mm(pk((7, 4)[r % 2], 2, TL)[:, k], YS[:, (2 * r + k) * P:(2 * r + k + 1) * P], SGT,
                                 start=True, stop=True)
                    ins.then_inc(sem("m_sc"), 1)

            def hidden(i, g):
                if g < 2:
                    pe.wait_ge(sem("m_g"), NGM * i + 1)
                else:
                    pe.wait_ge(sem("m_g"), NGM * i + g - 1 + 1)
                for b, kind in ((0, "w1"), (2, "w3")):
                    for part in range(2):
                        j = place[kind, g, part]
                        wait_lo(pe, i, j)
                        wh, wl = moe_split(j)
                        three(bank[b + g % 2][:], [((XGH[:, 4 * part + k, :], XGL[:, 4 * part + k, :]),
                                                    (wh[:, k, :], wl[:, k, :])) for k in range(4)],
                              part == 0, part == 1).then_inc(sem("m_unit"), 1)

            def turn(i, g):
                pe.wait_ge(sem("m_g"), NGM * i + g + 1 + 1)
                if g:
                    pe.wait_ge(sem("m_gt"), NGM * i + g + 1)
                else:
                    pe.wait_ge(sem("m_fa"), 4 * i + 4 + 1)
                for f in range(4):
                    ins = nc.tensor.transpose(pk(4, 4, P)[:, f], GSM[:, g % 2, f * P:(f + 1) * P], ident)
                ins.then_inc(sem("m_tr"), 1)

            def down(i, g):
                pe.wait_ge(sem("m_gt"), NGM * i + g + 1 + 1)
                if g == 0:
                    pe.wait_ge(sem("m_ys"), i + 1)
                for part in range(2):
                    j = place["w2", g, part]
                    wait_lo(pe, i, j)
                    wh, wl = moe_split(j)
                    for h in range(2):
                        cols = slice(512 * h, 512 * h + 512)
                        ins = three(bank[5 + h][:], [((GTH[g % 2][:, 2 * part + f], GTL[g % 2][:, 2 * part + f]),
                                                      (wh[:, f, cols], wl[:, f, cols])) for f in range(2)],
                                    g + part == 0, g == NGM - 1 and part == 1)
                    ins.then_inc(sem("m_unit"), 1)

            def item(i, more):
                pe.wait_ge(sem("m_xg"), 2 * i + 2)
                for s in range(NGM + 2):
                    if s < NGM:
                        hidden(i, s)
                    if s == 0:
                        scatter(i)
                    if s == 3:
                        pe.wait_ge(sem("m_sg"), i + 1)
                        for t in range(2):
                            ins = nc.tensor.transpose(bank[7][:, t * P:(t + 1) * P], SG[:, t], ident)
                        ins.then_inc(sem("m_sgT"), 1)
                    if s == NGM and more:
                        pe.wait_ge(sem("m_g"), NGM * i + NGM - 1 + 1)
                        pe.wait_ge(sem("m_sgt"), i + 1 + 1)
                        gather(i + 1)
                    if 1 <= s <= NGM:
                        turn(i, s - 1)
                    if s >= 2:
                        down(i, s - 2)

            gather(0)
            pe.wait_ge(sem("items"), 1)
            last = pe.value_load(it_i[0:1, 2 * NI:2 * NI + 1], min_val=NE - 1, max_val=NI - 1)
            with pe.Fori(0, last) as i:
                item(i, True)
            item(last, False)
            scatter(last + 1)
            ln_pe(3, slice(TC, T))
            for t in range(2):
                for h in range(2):
                    n = 2 * t + h
                    for k in range(4):
                        if t == 0:
                            pe.wait_ge(sem("ln_x"), 3 * KD + 4 * h + k + 1)
                        ins = nc.tensor.transpose(bank[n][:, k * P:(k + 1) * P], X[:, 4 * h + k, TC + P * t:TC + P * (t + 1)],
                                                  ident)
                    ins.then_inc(sem("outT"), 1)

        block = es.enter_context(nc.Block())

        @block.sync
        def _(sp):
            for i, (src, nk, nm, _) in enumerate(units):
                if i >= RING:
                    for free in units[i - RING][3]:
                        wait(sp, *free)
                for l in range(L):
                    if i == index[("out", l, 0)]:
                        sp.wait_ge(sem("y_done"), YTOT[l])
                        sp.wait_ge(sem("state_done"), 16 * (l + 1))
                key = [k for k, v in index.items() if v == i][0]
                sp.dma_start(slot_view(key), src).then_inc(sem(f"slot{i % RING}"), 16)
            moe_sp(sp)
            sp.wait_ge(sem("fin"), 1)
            sp.dma_start(out[0].rearrange("(t p) d -> p t d", p=P), area(o_mix, 2, D)).then_inc(sem("out_dma"), 16)
            sp.wait_ge(sem("out_dma"), 16)

        @block.gpsimd
        def _(pool):
            pc = [0]

            def link(ins):
                pc[0] += 1
                ins.then_inc(sem("pool_chain"), 1)
                pool.wait_ge(sem("pool_chain"), pc[0])

            def blocks(b):
                n, w = P >> b, 1 << b
                v = same[:, b, :].rearrange("p (n w) -> p n w", w=w)
                link(nc.gpsimd.memset(same[:, b, :], 1.0))
                link(nc.gpsimd.affine_select(out=v, in_=v, compare_op=ALU.is_ge, fill=0.0, base=0,
                                             pattern=[[-w, n], [0, w]], channel_multiplier=1))
                link(nc.gpsimd.affine_select(out=v, in_=v, compare_op=ALU.is_ge, fill=0.0, base=w - 1,
                                             pattern=[[w, n], [0, w]], channel_multiplier=-1))

            blocks(0)
            link(nc.gpsimd.tensor_copy(keep[:, 0], same[:, 0, :]))
            link(nc.gpsimd.memset(cs[:], 0.0))
            nc.gpsimd.memset(cs[:, one:one + 1], 1.0).then_inc(sem("consts"), 1)
            link(nc.gpsimd.memset(mean_w[:], 1.0 / D))
            link(nc.gpsimd.memset(same[:, 7, :], 1.0))
            for b in range(1, 7):
                blocks(b)
            for b in range(7):
                link(nc.gpsimd.tensor_tensor(level[:, b, :], same[:, b + 1, :], same[:, b, :], ALU.subtract))
            for i, b in ((1, 6), (2, 7)):
                link(nc.gpsimd.tensor_copy(keep[:, i], same[:, b, :]))
            for i, (base, cm, st) in enumerate(((-1, -1, 1), (-1, 1, -1), (0, -1, 1), (0, 1, -1))):
                v = tri[:, i, :]
                link(nc.gpsimd.memset(v, 1.0))
                ins = nc.gpsimd.affine_select(out=v, in_=v, compare_op=ALU.is_ge, fill=0.0, base=base,
                                              pattern=[[st, P]], channel_multiplier=cm)
                if i < 3:
                    link(ins)
            ins.then_inc(sem("consts"), 1)

            for l in range(L):
                for u in range((NCT + 1) // 2):
                    split_lo(pool, split_of["in", l, u])
                wait(pool, "mod_mm", (8 + 2, 8 + 5)[l])
                wait(pool, *(("xT", KD) if l == 0 else ("mix_lo", KD * l)))
                nc.gpsimd.memset(w2z, 0.0).then_inc(sem("zeroed"), 1)
                pool.wait_ge(sem("q_in"), l + 1)
                nc.gpsimd.tensor_tensor(Qflat, Qflat, qm[:].unsqueeze(2).to_broadcast([P, 2 * NP * NT, P + 1]),
                                        ALU.subtract).then_inc(sem("q_done"), 1)
                for i in range(2 * NP):
                    k_ = KDIR[:, i // NP, i % NP]
                    pool.wait_ge(sem("kdir_f"), 2 * NP * l + i + 1)
                    nc.gpsimd.tensor_tensor(k_, k_, K[:, i % NP], ALU.mult).then_inc(sem("kdir"), 1)
                pool.wait_ge(sem("prep_done"), l + 1)
                nc.gpsimd.memset(ZR[:], 0.0).then_inc(sem("zeroed"), 1)
                def values(cn, tj):
                    wait(pool, "pe_m", 2 * cn)
                    pool.wait_ge(sem("vtok"), NT * (l + 1))
                    nc.gpsimd.tensor_copy(VS[:], VTK[:, tj]).then_inc(sem("vs"), 1)

                for st in range(8):
                    d, tj, cn = st // 4, TILE(st), 8 * l + st
                    values(cn, tj)
                    for k in range(6):
                        for q in range(2):
                            w = wk[q]
                            if k == 0:
                                pool.wait_ge(sem("dve_lt"), 2 * cn + q + 1)
                            if k >= 2:
                                wait(pool, "pe_x", (6 * cn + k - 2) * 2 + q + 1)
                            nc.gpsimd.tensor_tensor(w["LM"][:, k % 2], w["LT"],
                                                    level[:, k + 1:k + 2, :].to_broadcast([P, 4, P]), ALU.mult) \
                                .then_inc(sem("pool_lm"), 1)
                rtok = LTOK(l)
                pool.wait_ge(sem("bonus_in"), NP * (l + 1))
                for i, k in enumerate(list(range(NP, KD)) + list(range(NP))):
                    if i == NP:
                        split_lo(pool, split_of["out", l, 0])
                    pool.wait_ge(sem("mix_hi"), KD * l + i + 1)
                    nc.gpsimd.tensor_tensor(HL[k][:, rtok], MIX[:, k, rtok], HH[k][:, rtok], ALU.subtract) \
                        .then_inc(sem("mix_lo"), 1)
                for i in range(split_of["out", l, 0] + 1, split_of["in", 1, 0] if l == 0 else len(splits)):
                    split_lo(pool, i)
            pool.wait_ge(sem("mix"), NP * L)
            nc.gpsimd.iota(io_i, [[1, P]], base=0, channel_multiplier=0).then_inc(sem("iota"), 1)
            moe_pool(pool)



        @block.scalar
        def _(act):
            def load_params(l):
                if l:
                    wait(act, "par_T", l)
                srcs = [(b_mod[l], "b_mod"), (rk_w0[l], "w0"), (rk_a0[l], "a0"), (rk_kk[l], "kk"), (rk_ka[l], "ka"),
                        (rk_rk[l], "rk"), (rk_lnx_g[l], "lnxg"), (rk_lnx_b[l], "lnxb"), (conv_w[l], "conv"),
                        (ln1_g[l], "ln1g"), (ln1_b[l], "ln1b"), (ln2_g[l], "ln2g"), (ln2_b[l], "ln2b")]
                for s, nm in srcs:
                    if len(s.shape) == 2:
                        s = s.rearrange("a b -> (a b)")
                    n = s.shape[0] // P
                    act.dma_start(par_rows[COLS[nm]:COLS[nm] + n, :], s.rearrange("(n p) -> n p", p=P)) \
                       .then_inc(sem("par_load"), 16)

            act.dma_start(crow[0:KD, :], c_ctx.rearrange("(n p) -> n p", p=P)).then_inc(sem("c_load"), 16)
            act.dma_start(crow[KD:2 * KD, :], c[0].rearrange("(n p) -> n p", p=P)).then_inc(sem("c_load"), 16)
            load_params(0)
            act.dma_start(rw[:], router_w[0].rearrange("(k p) e -> p k e", p=P)).then_inc(sem("router_load"), 16)
            act.dma_start(rb[:], router_b[0].partition_broadcast(P)).then_inc(sem("router_load"), 16)
            act.dma_start(xrows[:, 0:TC // P, :], ctx[0].rearrange("(t p) d -> p t d", p=P)).then_inc(sem("x_load"), 16)
            act.dma_start(xrows[:, TC // P:NT, :], x[0].rearrange("(t p) d -> p t d", p=P)).then_inc(sem("x_load"), 16)
            load_params(1)
            act.wait_ge(sem("c_col"), 1)
            act.activation(csig[:], ccol[:], ACT.Sigmoid).then_inc(sem("c_sig"), 1)
            for k in range(KD):
                act.wait_ge(sem("xT"), k + 1)
                act.activation(X[:, k, :], bank[k % 4][:], ACT.Copy).then_inc(sem("xT_act"), 1)

            def mod_rows(m):
                wait(act, "mod_mm", 8 + m)
                wait(act, "mod_T", m)
                act.activation(mrow[:], bank[6][:], ACT.Copy).then_inc(sem("mod_rows"), 1)

            def ln_act(n, tok, l, g, b):
                for k in range(KD):
                    act.wait_ge(sem("ln_d"), KD * n + k + 1)
                    if k >= 2 or n:
                        wait(act, "ln_vmm", KD * n + k - 1)
                    act.activation(SQ[:, k % 2, tok], X[:, k, tok], ACT.Square).then_inc(sem("ln_sq"), 1)
                act.wait_ge(sem("ln_ve"), n + 1)
                act.activation(RSTD[:, tok], RSTD[:, tok], ACT.Sqrt).then_inc(sem("ln_std"), 1)
                for k in range(KD):
                    act.wait_ge(sem("ln_norm"), KD * n + k + 1)
                    act.activation(X[:, k, tok], X[:, k, tok], ACT.Identity, bias=pcol(l, b, k), scale=pcol(l, g, k)) \
                       .then_inc(sem("ln_x"), 1)

            def hi_parts(n):
                for k in range(KD):
                    act.wait_ge(sem("h_ready"), KD * n + k + 1)
                    act.activation(HH[k][:, :], HT[:, k % 2], ACT.Copy).then_inc(sem("h_hi"), 1)

            mod_rows(0)
            for l in range(L):
                dst = [R[:, i] for i in range(NP)] + [K[:, i] for i in range(NP)] + [V[:, i] for i in range(NP)] + \
                      [WD, AD, GD] + [CB[:, i] for i in range(NP)] + [CC[:, i] for i in range(NP)]
                s0 = split_of[("in", l, 0)]
                if l == 0:
                    split_hi(act, s0)
                    split_hi(act, s0 + 1)
                hi_parts(2 * l)
                for ct in range(NCT):
                    if ct < len(dst):
                        act.wait_ge(sem("proj_mm"), NCT * l + ct + 1)
                        f = {3 * NP: ACT.Tanh, 3 * NP + 2: ACT.Sigmoid}.get(ct, ACT.Copy)
                        tok = CTOK(l, ct)
                        act.activation(dst[ct][:, tok], bank[ct % 4][:, tok], f).then_inc(sem("proj_act"), 1)
                    if ct % 2 and s0 + ct // 2 + 2 <= split_of[("in", l, NCT // 2)]:
                        split_hi(act, s0 + ct // 2 + 2)
                    if l == 0 and ct == 11:
                        mod_rows(1)
                    if (ct - 9) % 3 == 0 and 0 <= (ct - 9) // 3 < NP:
                        j = (ct - 9) // 3
                        act.wait_ge(sem("kk_raw"), NP * l + j + 1)
                        wait(act, "kk_done", NP * l + j - 1)
                        act.activation(tmp_k(j), KKN[:, j], ACT.Square).then_inc(sem("kk_sq"), 1)
                    if (ct - 12) % 3 == 0 and 0 <= (ct - 12) // 3 < NP:
                        j = (ct - 12) // 3
                        act.wait_ge(sem("kk_ss"), NP * l + j + 1)
                        act.activation(tmp_k(j), tmp_k(j), ACT.Sqrt).then_inc(sem("kk_norm"), 1)
                if l == 0:
                    mod_rows(2)
                act.wait_ge(sem("zeroed"), 2 * l + 1)
                for kind, w in enumerate((rk_w2, rk_a2)):
                    for d in range(2):
                        act.dma_start(w2z[64 * d:64 * (d + 1), kind, d, :], w[l, d]).then_inc(sem("lora_load"), 16)
                act.wait_ge(sem("kk_done"), NP * (l + 1))
                for i in range(4 * NP):
                    n = 4 * NP * l + i
                    act.wait_ge(sem("lora_mm"), n + 1)
                    wait(act, "lora_use", n - 1)
                    kind, d, j = i // (2 * NP), i // NP % 2, i % NP
                    act.activation(tmp[:, i % 2], bank[i % 4][:], ACT.Sigmoid,
                                   bias=pcol(l, ("w0", "a0")[kind], d * NP + j)).then_inc(sem("lora_sig"), 1)
                act.wait_ge(sem("q_in"), l + 1)
                act.activation(e1[:].rearrange("p d j t -> p (d j t)"), qm[:], ACT.Exp, scale=-DECAY)
                act.activation(e2[:].rearrange("p d j t -> p (d j t)"), qt[:], ACT.Exp, scale=-DECAY) \
                   .then_inc(sem("e12"), 1)
                for t in range(NT):
                    act.wait_ge(sem("vT"), NT * l + t + 1)
                    if t == 0:
                        act.wait_ge(sem("kdir"), 2 * NP * (l + 1))
                    act.activation(VTK[:, t], pk(2 + t % 2, NP, P), ACT.Copy).then_inc(sem("vtok"), 1)
                act.wait_ge(sem("prep_done"), l + 1)
                act.dma_start(g2, rk_g2[l]).then_inc(sem("g2_load"), 16)

                def stage(cn, st):
                    d, tj = st // 4, TILE(st)
                    wait(act, "staged", cn)
                    incl, excl = (slice(1, P + 1), slice(0, P)) if d == 0 else (slice(0, P), slice(1, P + 1))
                    s = -DECAY if d == 0 else DECAY
                    act.activation(EX[:, 0], Q[:, d, :, tj, incl], ACT.Exp, scale=s)
                    act.activation(EX[:, 1], Q[:, d, :, tj, incl], ACT.Exp, scale=-s)
                    act.activation(EX[:, 2], Q[:, d, :, tj, excl], ACT.Exp, scale=s).then_inc(sem("ex"), 1)

                def masked(cn, st):
                    act.wait_ge(sem("staged"), cn + 1)
                    wait(act, "zeroed", 2 * l + 2)
                    wait(act, "pe_s2", 2 * cn)
                    for i, src in ((0, AS), (2, rt[:, st % 2])):
                        if i == 0 or reads_out(l, st):
                            act.activation(ZR[0:64, :, i, :], src[0:64], ACT.Copy)
                            ins = act.activation(ZR[64:128, :, i + 1, :], src[64:128], ACT.Copy)
                    ins.then_inc(sem("zr"), 1)

                act.wait_ge(sem("q_done"), l + 1)
                stage(8 * l, 0)
                masked(8 * l, 0)
                for st in range(8):
                    cn = 8 * l + st
                    for q in range(2):
                        w, b = wk[q], 4 * q
                        n = 2 * cn + q + 1
                        xa = w["XA"].rearrange("p (a h) n -> p a h n", h=2)
                        wait(act, "pe_tab", n)
                        src = pk(b, 4, P)
                        act.activation(xa[:, :, 0, 0:64], src[:, 0:2, 0:64], ACT.Copy)
                        act.activation(xa[:, :, 1, 64:128], src[:, 0:2, 64:128], ACT.Copy)
                        act.activation(w["BT"], src[:, 2:4, :], ACT.Copy).then_inc(sem("act_tab"), 1)
                        wait(act, "pe_tk", n)
                        act.activation(w["KT"], pk(b + 1, 2, P), ACT.Copy).then_inc(sem("act_tk"), 1)
                    for q in range(2):
                        w, b = wk[q], 4 * q
                        n = 2 * cn + q + 1
                        wait(act, "pe_t1", n)
                        act.activation(w["T"], pk(b + 2, 4, P), ACT.Copy).then_inc(sem("act_t1"), 1)
                    for q in range(2):
                        w, b = wk[q], 4 * q
                        n = 2 * cn + q + 1
                        xa = w["XA"].rearrange("p (a h) n -> p a h n", h=2)
                        wait(act, "pe_ax", n)
                        src = pk(b + 3, 2, 2, P)
                        act.activation(xa[:, :, 0, 64:128], src[:, :, 0, 0:64], ACT.Copy)
                        act.activation(xa[:, :, 1, 0:64], src[:, :, 1, 64:128], ACT.Copy).then_inc(sem("act_ax"), 1)
                    for k in range(6):
                        for q in range(2):
                            w, b = wk[q], 4 * q
                            act.wait_ge(sem("pe_x"), (6 * cn + k) * 2 + q + 1)
                            qr, qc = quadrant(st // 4) if k == 5 else (slice(0, P), slice(0, P))
                            act.activation(w["XS"][qr, :, qc], pk(b, 4, P)[qr, :, qc], ACT.Copy).then_inc(sem("act_xs"), 1)
                        if k == 1 and st < 7:
                            stage(cn + 1, st + 1)
                        if k == 3 and st < 7:
                            masked(cn + 1, st + 1)
                    for q in range(2):
                        w, b = wk[q], 4 * q
                        act.wait_ge(sem("pe_uw"), 2 * cn + q + 1)
                        act.activation(w["UW"], pk(b + 3, 4, P), ACT.Copy).then_inc(sem("act_uw"), 1)
                    for q in range(2):
                        w, b = wk[q], 4 * q
                        n = 2 * cn + q + 1
                        wait(act, "pe_gt", n)
                        act.activation(w["GT"], pk(b + 1, 2, HS), ACT.Copy).then_inc(sem("act_gt"), 1)
                        if not reads_out(l, st):
                            continue
                        act.wait_ge(sem("dve_yw"), 2 * ybefore[l, st] + q + 1)
                        yw = w["YW"].rearrange("p (a h) n -> p a h n", h=2)
                        src = pk(b, 2, 2, P)
                        act.activation(yw[64:128, :, 0, :], src[64:128, :, 0, :], ACT.Copy)
                        act.activation(yw[0:64, :, 1, :], src[0:64, :, 1, :], ACT.Copy).then_inc(sem("act_yw"), 1)
                rtok = LTOK(l)
                act.wait_ge(sem("state_done"), 16 * (l + 1))
                for k in range(NP, KD):
                    act.activation(HH[k][:, rtok], MIX[:, k, rtok], ACT.Copy).then_inc(sem("mix_hi"), 1)
                split_hi(act, split_of[("out", l, 0)])
                for j in range(NP):
                    act.wait_ge(sem("gn_d"), NP * l + j + 1)
                    act.activation(RSQ[:, j, rtok], Y[:, j, rtok], ACT.Square).then_inc(sem("gn_sq"), 1)
                for j in range(NP):
                    act.wait_ge(sem("gn_ve"), NP * l + j + 1)
                    act.activation(RRS[:, j, rtok], RRS[:, j, rtok], ACT.Sqrt).then_inc(sem("gn_std"), 1)
                for j in range(NP):
                    act.wait_ge(sem("gn_norm"), NP * l + j + 1)
                    act.activation(Y[:, j, rtok], Y[:, j, rtok], ACT.Identity, bias=pcol(l, "lnxb", j),
                                   scale=pcol(l, "lnxg", j)).then_inc(sem("gn_aff"), 1)
                for k in range(NP):
                    act.wait_ge(sem("mix"), NP * l + k + 1)
                    act.activation(HH[k][:, rtok], MIX[:, k, rtok], ACT.Copy).then_inc(sem("mix_hi"), 1)
                s0 = split_of[("out", l, 0)]
                for u in range(1, KD // 2):
                    split_hi(act, s0 + u)
                if l == 0:
                    s0 = split_of[("w1", 0, 0)]
                    split_hi(act, s0)
                    split_hi(act, s0 + 1)
                ln_act(2 * l, LTOK(l), l, "ln1g", "ln1b")
                if l == 0:
                    hi_parts(1)
                    NG = FF // 256

                    for j, ((kind, _, g), _) in enumerate(splits[s0:s0 + 3 * NG]):
                        if kind == "w1":
                            for f in (2 * g, 2 * g + 1):
                                act.wait_ge(sem("ffn_h1"), f + 1)
                                wait(act, "ffn_s", f - 1)
                                act.activation(FS[:, f % 2], bank[f % 2][:], ACT.Sigmoid).then_inc(sem("ffn_sig"), 1)
                            if g in reduce_at:
                                mod_rows(reduce_at[g])
                        elif kind == "w3":
                            for f in (2 * g, 2 * g + 1):
                                act.wait_ge(sem("ffn_g"), f + 1)
                                wait(act, "ffn_y", KD * (g - 1))
                                act.activation(GH[f % 4], FP[:, f % 2], ACT.Copy).then_inc(sem("ffn_ghi"), 1)
                        if j + 2 < 3 * NG:
                            split_hi(act, s0 + j + 2)
                    for u in range(2):
                        split_hi(act, split_of["in", 1, u])
                    ln_act(1, slice(0, T), 0, "ln2g", "ln2b")
            moe_act(act, ln_act)

        @block.vector
        def _(dve):
            ch = [0]

            def link(ins):
                ch[0] += 1
                ins.then_inc(sem("dve_chain"), 1)
                dve.wait_ge(sem("dve_chain"), ch[0])

            dve.wait_ge(sem("c_T"), 1)
            nc.vector.tensor_copy(ccol[:], bank[5][:, 0:2 * KD]).then_inc(sem("c_col"), 1)
            dve.wait_ge(sem("c_sig"), 1)
            dve.wait_ge(sem("consts"), 1)
            nc.vector.tensor_tensor(cs[:, 0:2 * KD].rearrange("p (k s) -> p k s", s=2), ccol[:].rearrange("p (s k) -> p k s", s=2),
                                    csig[:].rearrange("p (s k) -> p k s", s=2), ALU.mult).then_inc(sem("c_silu"), 1)

            def params(l):
                dve.wait_ge(sem("par_T"), l + 1)
                link(nc.vector.tensor_copy(par[:, l, :], bank[4][:, 0:P]))
                nc.vector.tensor_scalar(one_ka[:, l, :], par[:, l, COLS["ka"]:COLS["ka"] + NP], -1.0, 1.0,
                                        ALU.mult, ALU.add).then_inc(sem("par"), 1)
                dve.wait_ge(sem("par"), l + 1)

            params(0)
            params(1)

            def mod_cols(m):
                l, part = m // 3, m % 3
                dve.wait_ge(sem("mod_T"), m + 1)
                b = (7, 7, 5)[part]
                for i in range(4):
                    c0 = 16 * part + 8 * (i // 2) + i % 2
                    src = bank[b][:, i * P:(i + 1) * P].rearrange("p (q s) -> p q s", s=32)[:, :, 0:2]
                    bias = par[:, l, c0:c0 + 7:2].unsqueeze(2).to_broadcast([P, 4, 2])
                    dst = mc[:, l, :, c0:c0 + 7:2].rearrange("p s q -> p q s")
                    ins = nc.vector.tensor_tensor(dst, src, bias, ALU.add)
                    if part != 1 and i == 3:
                        link(ins)
                if part == 1:
                    ins.then_inc(sem("mod_cols"), 1)
                else:
                    c1 = KD if part == 0 else 4 * KD
                    nc.vector.tensor_scalar(mc[:, l, :, c1:c1 + KD], mc[:, l, :, c1:c1 + KD], 1.0, None, ALU.add) \
                      .then_inc(sem("mod_cols"), 1)

            def h_lo(n, k):
                dve.wait_ge(sem("h_hi"), KD * n + k + 1)
                nc.vector.tensor_tensor(HL[k][:, :], HT[:, k % 2], HH[k][:, :], ALU.subtract).then_inc(sem("h_lo"), 1)

            def modulate(l, n, shift, scale, streams, first, cut_):
                for k in range(KD):
                    dst = HT[:, k % 2] if cut_ else HB[:, k]
                    if cut_ and k >= 2:
                        wait(dve, "h_lo", KD * n + k - 1)
                    for s in streams:
                        tok = slice(TC, T) if s else slice(0, TC)
                        wait(dve, first[0], first[1] + k + 1)
                        ins = nc.vector.tensor_scalar(dst[:, tok], X[:, k, tok],
                                                      mc[:, l, s, scale * KD + k:scale * KD + k + 1],
                                                      mc[:, l, s, shift * KD + k:shift * KD + k + 1], ALU.mult, ALU.add)
                    ins.then_inc(sem("h_ready"), 1)
                    if cut_ and k:
                        h_lo(n, k - 1)
                if cut_:
                    h_lo(n, KD - 1)
                wait(dve, "h_ready", KD * (n + 1))
                tok = slice(TC if streams == (1,) else 0, T)
                nc.vector.tensor_scalar(X[:, :, tok], X[:, :, tok], ALPHA, None, ALU.mult).then_inc(sem("xa"), 1)

            def ln_dve(n, tok):
                dve.wait_ge(sem("ln_mean"), n + 1)
                for k in range(KD):
                    nc.vector.tensor_tensor(X[:, k, tok], X[:, k, tok], bank[4][:, tok], ALU.subtract) \
                      .then_inc(sem("ln_d"), 1)
                wait(dve, "ln_vmm", KD * (n + 1))
                nc.vector.tensor_scalar(RSTD[:, tok], bank[5][:, tok], LN_EPS, None, ALU.add).then_inc(sem("ln_ve"), 1)
                dve.wait_ge(sem("ln_std"), n + 1)
                link(nc.vector.reciprocal(RSTD[:, tok], RSTD[:, tok]))
                wait(dve, "ln_sq", KD * (n + 1))
                for k in range(KD):
                    nc.vector.tensor_tensor(X[:, k, tok], X[:, k, tok], RSTD[:, tok], ALU.mult).then_inc(sem("ln_norm"), 1)

            mod_cols(0)
            dve.wait_ge(sem("consts"), 2)
            for l in range(L):
                dve.wait_ge(sem("mod_cols"), 3 * l + 1)
                modulate(l, 2 * l, 0, 1, (0, 1), ("xT_act", 0) if l == 0 else ("ln_x", KD * (2 * l - 1)), True)
                s0 = split_of[("in", l, 0)]
                for u in range(2):
                    mod_sums(dve, ("in", l, u))
                for ct in range(NCT):
                    j = ct - (5 * NP + 3)
                    if j >= 0:
                        dve.wait_ge(sem("proj_mm"), NCT * l + ct + 1)
                        dve.wait_ge(sem("proj_act"), (5 * NP + 3) * l + 4 * NP + 3 + j + 1)
                        tok = CTOK(l, ct)
                        nc.vector.tensor_tensor(U[:, j, tok], CC[:, j, tok], bank[ct % 4][:, tok], ALU.mult) \
                          .then_inc(sem("proj_u"), 1)
                    if ct % 2 and s0 + ct // 2 + 2 <= split_of[("in", l, NCT // 2)]:
                        mod_sums(dve, ("in", l, ct // 2 + 2))
                    if l == 0 and ct == 17:
                        mod_cols(1)
                    if (ct - 8) % 3 == 0 and 0 <= (ct - 8) // 3 < NP:
                        j = (ct - 8) // 3
                        dve.wait_ge(sem("proj_act"), (5 * NP + 3) * l + NP + j + 1)
                        nc.vector.tensor_scalar(KKN[:, j], K[:, j], pcol(l, "kk", j), None, ALU.mult) \
                          .then_inc(sem("kk_raw"), 1)
                    if (ct - 11) % 3 == 0 and 0 <= (ct - 11) // 3 < NP:
                        j = (ct - 11) // 3
                        dve.wait_ge(sem("kk_mm"), NP * l + j + 1)
                        nc.vector.tensor_scalar(tmp_k(j), bank[4 + j % 2][:], 1e-24, None, ALU.max) \
                          .then_inc(sem("kk_ss"), 1)
                    if (ct - 13) % 3 == 0 and 0 <= (ct - 13) // 3 < NP:
                        j = (ct - 13) // 3
                        dve.wait_ge(sem("kk_norm"), NP * l + j + 1)
                        link(nc.vector.reciprocal(tmp_k(j), tmp_k(j)))
                        nc.vector.tensor_tensor(KKN[:, j], KKN[:, j], tmp_k(j), ALU.mult).then_inc(sem("kk_done"), 1)
                if l == 0:
                    wait(dve, "mod_mm", 8 + 2)
                dve.wait_ge(sem("proj_u"), NP * (l + 1))
                stt = nc.vector.scalar_tensor_tensor
                for j in range(NP):
                    m, ctok = MIX[:, NP + j], LTOK(l)
                    link(nc.vector.tensor_scalar(m[:, ctok], U[:, j, ctok], pcol(l, "conv", NP + j), None, ALU.mult))
                    rows = [(m[:, TC:T].rearrange("p (r w) -> p r w", w=GRID),
                             U[:, j, TC:T].rearrange("p (r w) -> p r w", w=GRID), GRID)]
                    if l < L - 1:
                        rows.append((m[:, None, 0:TC], U[:, j, None, 0:TC], TC))
                    for tap, dst, src in ((0, 1, 0), (2, 0, 1)):
                        for mr, ur, n in rows:
                            link(stt(out=mr[:, :, dst:n - 1 + dst], in0=ur[:, :, src:n - 1 + src],
                                     scalar=pcol(l, "conv", tap * NP + j), in1=mr[:, :, dst:n - 1 + dst],
                                     op0=ALU.mult, op1=ALU.add))
                    link(nc.vector.tensor_tensor(m[:, ctok], m[:, ctok], CB[:, j, ctok], ALU.mult))
                for i in range(2 * NP):
                    n = 4 * NP * l + i
                    d, j = i // NP, i % NP
                    dve.wait_ge(sem("lora_sig"), n + 1)
                    for t in range(NT):
                        ins = nc.vector.tensor_tensor_scan(Q[:, d, j, t, 1:P + 1], ones_t,
                                                           tmp[:, i % 2, t * P:(t + 1) * P], 0.0, ALU.mult, ALU.add)
                    ins.then_inc(sem("lora_use"), 1)
                link(nc.vector.memset(Qflat[:, :, 0:1], 0.0))
                wait(dve, "lora_use", 4 * NP * l + 2 * NP)
                link(nc.vector.tensor_copy(qm[:], Qflat[:, :, P // 2]))
                nc.vector.tensor_tensor(qt[:], Qflat[:, :, P], qm[:], ALU.subtract).then_inc(sem("q_in"), 1)
                for i in range(2 * NP):
                    n = 4 * NP * l + 2 * NP + i
                    d, j = i // NP, i % NP
                    dve.wait_ge(sem("lora_sig"), n + 1)
                    nc.vector.tensor_scalar(KDIR[:, d, j], tmp[:, i % 2], pcol(l, "ka", j), one_ka[:, l, j:j + 1],
                                            ALU.mult, ALU.add).then_inc(sem("kdir_f"), 1)
                    nc.vector.scalar_tensor_tensor(out=BV[:, d, j], in0=KKN[:, j], scalar=-1.0, in1=tmp[:, i % 2],
                                                   op0=ALU.mult, op1=ALU.mult).then_inc(sem("lora_use"), 1)
                dve.wait_ge(sem("lora_use"), 4 * NP * (l + 1))
                dve.wait_ge(sem("e12"), l + 1)
                for d in range(2):
                    for j in range(3):
                        a, b = TILE(4 * d + j), TILE(4 * d + j + 1)
                        post, pre = (e2, e1) if d == 0 else (e1, e2)
                        link(nc.vector.tensor_tensor(fac[:, d, :, j], post[:, d, :, a], pre[:, d, :, b], ALU.mult))
                link(nc.vector.memset(MC[:], 0.0))
                link(nc.vector.memset(MI[:], 0.0))
                mi = MI.rearrange("p (a h) n -> p a h n", h=2)
                link(nc.vector.tensor_copy(mi[64:128, :, 0, :], ident[64:128, None, 64:128].to_broadcast([64, NP, HS])))
                nc.vector.tensor_copy(mi[0:64, :, 1, :], ident[0:64, None, 0:64].to_broadcast([64, NP, HS])) \
                  .then_inc(sem("prep_done"), 1)
                if l == 0:
                    mod_cols(2)

                def stage(cn, st):
                    d, tj = st // 4, TILE(st)
                    tok = slice(tj * P, (tj + 1) * P)
                    dve.wait_ge(sem("ex"), cn + 1)
                    wait(dve, "pe_tk", 2 * cn)
                    wait(dve, "zr", cn)
                    nc.vector.tensor_tensor(BS, BV[:, d, :, tok], EX[:, 1], ALU.mult)
                    nc.vector.tensor_tensor(KS, KDIR[:, d, :, tok], EX[:, 1], ALU.mult)
                    ins = nc.vector.tensor_tensor(AS, KKN[:, :, tok], EX[:, 2], ALU.mult)
                    if reads_out(l, st):
                        ins = nc.vector.tensor_tensor(rt[:, st % 2], R[:, :, tok], EX[:, 0], ALU.mult)
                    ins.then_inc(sem("staged"), 1)

                dve.wait_ge(sem("prep_done"), l + 1)
                dve.wait_ge(sem("kdir"), 2 * NP * (l + 1))
                stage(8 * l, 0)
                for st in range(8):
                    d, tj, cn = st // 4, TILE(st), 8 * l + st
                    tok = slice(tj * P, (tj + 1) * P)
                    strict = tri[:, d:d + 1, :].to_broadcast([P, 2, P])
                    incl = tri[:, 2 + d:3 + d, :].to_broadcast([P, 2, P])
                    for q in range(2):
                        w, b = wk[q], 4 * q
                        n = 2 * cn + q + 1
                        wait(dve, "pe_s1", n)
                        for p in range(2):
                            ins = nc.vector.tensor_tensor(w["LT"][:, 2 * p:2 * p + 2], pk(b + p, 4, P)[:, 0:2], strict,
                                                          ALU.mult)
                        ins.then_inc(sem("dve_lt"), 1)
                        wait(dve, "dve_lt", n)
                        link(nc.vector.tensor_tensor(w["TT"], w["LT"], level[:, 0:1, :].to_broadcast([P, 4, P]),
                                                     ALU.mult))
                        nc.vector.tensor_tensor(w["TT"], w["TT"], ident[:, None, :].to_broadcast([P, 4, P]), ALU.add) \
                            .then_inc(sem("t0_done"), 1)
                        if reads_out(l, st):
                            for p in range(2):
                                ins = nc.vector.tensor_tensor(w["RB"][:, 2 * p:2 * p + 2], pk(b + p, 4, P)[:, 2:4],
                                                              incl, ALU.mult)
                            ins.then_inc(sem("dve_rb"), 1)
                    for q in range(2):
                        w, b = wk[q], 4 * q
                        n = 2 * cn + q + 1
                        wait(dve, "pe_s2", n)
                        for p in range(2):
                            ins = nc.vector.tensor_tensor(w["AK"][:, 2 * p:2 * p + 2], pk(b + 2 + p, 4, P)[:, 0:2],
                                                          strict, ALU.mult)
                            if reads_out(l, st):
                                ins = nc.vector.tensor_tensor(w["RK"][:, 2 * p:2 * p + 2], pk(b + 2 + p, 4, P)[:, 2:4],
                                                              incl, ALU.mult)
                        ins.then_inc(sem("dve_ak"), 1)
                    for k in range(6):
                        for q in range(2):
                            w, b = wk[q], 4 * q
                            if k < 5:
                                dve.wait_ge(sem("pe_u1"), (5 * cn + k) * 2 + q + 1)
                                dve.wait_ge(sem("act_t1"), 2 * cn + q + 1)
                                if k:
                                    wait(dve, "dve_t", (5 * cn + k - 1) * 2 + q + 1)
                                nc.vector.tensor_tensor(w["T"], w["T"], pk(b + 1, 4, P), ALU.add).then_inc(sem("dve_t"), 1)
                            dve.wait_ge(sem("pe_u2"), (6 * cn + k) * 2 + q + 1)
                            qr, qc = quadrant(d) if k == 5 else (slice(0, P), slice(0, P))
                            tt_ = w["TT"][qc, :, qr]
                            nc.vector.tensor_tensor(tt_, tt_, pk(b + 2, 4, P)[qc, :, qr], ALU.add).then_inc(sem("dve_tt"), 1)
                        if k == 2 and st < 7:
                            stage(cn + 1, st + 1)
                    if st >= 4:
                        j, rtok = st - 4, LTOK(l)
                        wait(dve, "staged", 8 * l + 4)
                        link(nc.vector.tensor_tensor(RTB[:, j, rtok], KDIR[:, 0, j, rtok], KDIR[:, 1, j, rtok], ALU.add))
                        nc.vector.scalar_tensor_tensor(out=RTB[:, j, rtok], in0=R[:, j, rtok], scalar=pcol(l, "rk", j),
                                                       in1=RTB[:, j, rtok], op0=ALU.mult, op1=ALU.mult) \
                          .then_inc(sem("bonus_in"), 1)
                    for q in range(2 if reads_out(l, st) else 0):
                        w, b = wk[q], 4 * q
                        n = 2 * ybefore[l, st] + q + 1
                        yw = w["YW"].rearrange("p (a h) n -> p a h n", h=2)
                        src = pk(b, 2, 2, P)
                        wait(dve, "pe_yw", n)
                        r_ = rt[:, st % 2, 2 * q:2 * q + 2]
                        nc.vector.tensor_tensor(yw[0:64, :, 0, :], src[0:64, :, 0, :], r_[0:64], ALU.add)
                        nc.vector.tensor_tensor(yw[64:128, :, 1, :], src[64:128, :, 1, :], r_[64:128], ALU.add) \
                          .then_inc(sem("dve_yw"), 1)
                    for q in range(2):
                        w, b = wk[q], 4 * q
                        n = 2 * cn + q + 1
                        dst = Y[:, 2 * q:2 * q + 2, tok]
                        if reads_out(l, st):
                            dve.wait_ge(sem("pe_y"), 2 * ybefore[l, st] + q + 1)
                        if not reads_out(l, st):
                            pass
                        elif d == 0:
                            nc.vector.tensor_copy(dst, pk(b + 2, 2, P)).then_inc(sem("y_done"), 1)
                        else:
                            nc.vector.tensor_tensor(dst, dst, pk(b + 2, 2, P), ALU.add).then_inc(sem("y_done"), 1)
                        mcq, mtq = MC[:, 2 * q:2 * q + 2], mt[:, 2 * q:2 * q + 2]
                        miq = MI.rearrange("p (a h) n -> p a h n", h=2)[:, 2 * q:2 * q + 2]
                        wait(dve, "pe_m", n)
                        if st % 4 == 3:
                            nc.vector.memset(mcq, 0.0)
                            nc.vector.memset(miq[0:64, :, 0, :], 0.0)
                            nc.vector.memset(miq[64:128, :, 1, :], 0.0).then_inc(sem("state_done"), 1)
                        else:
                            link(nc.vector.tensor_tensor(mtq, mcq, pk(b + 3, 2, HS), ALU.add))
                            link(nc.vector.tensor_tensor(mcq, mtq, fac[:, d, 2 * q:2 * q + 2, st % 4].unsqueeze(2)
                                                         .to_broadcast([P, 2, HS]), ALU.mult))
                            nc.vector.tensor_copy(miq[0:64, :, 0, :], mcq[0:64])
                            nc.vector.tensor_copy(miq[64:128, :, 1, :], mcq[64:128]).then_inc(sem("state_done"), 1)
                rtok = LTOK(l)
                dve.wait_ge(sem("y_done"), YTOT[l])
                for j in range(NP):
                    dve.wait_ge(sem("gn_mm"), NP * l + j + 1)
                    nc.vector.scalar_tensor_tensor(out=Y[:, j, rtok], in0=bank[j % 2][:, rtok], scalar=-1.0 / HS,
                                                   in1=Y[:, j, rtok], op0=ALU.mult, op1=ALU.add).then_inc(sem("gn_d"), 1)
                for j in range(NP):
                    dve.wait_ge(sem("gn_vmm"), NP * l + j + 1)
                    nc.vector.tensor_scalar(RRS[:, j, rtok], bank[2 + j % 2][:, rtok], 1.0 / HS, GN_EPS, ALU.mult, ALU.add) \
                      .then_inc(sem("gn_ve"), 1)
                for j in range(NP):
                    dve.wait_ge(sem("gn_std"), NP * l + j + 1)
                    link(nc.vector.reciprocal(RRS[:, j, rtok], RRS[:, j, rtok]))
                    dve.wait_ge(sem("gn_sq"), NP * l + j + 1)
                    nc.vector.tensor_tensor(Y[:, j, rtok], Y[:, j, rtok], RRS[:, j, rtok], ALU.mult) \
                      .then_inc(sem("gn_norm"), 1)
                for j in range(NP):
                    dve.wait_ge(sem("bonus_mm"), NP * l + j + 1)
                    link(nc.vector.tensor_tensor(RTB[:, j, rtok], V[:, j, rtok], bank[4 + j % 2][:, rtok], ALU.mult))
                    dve.wait_ge(sem("gn_aff"), NP * l + j + 1)
                    link(nc.vector.tensor_tensor(Y[:, j, rtok], Y[:, j, rtok], RTB[:, j, rtok], ALU.add))
                    dve.wait_ge(sem("gate_mm"), NP * (l + 1))
                    nc.vector.tensor_tensor(MIX[:, j, rtok], Y[:, j, rtok], bank[(6, 7, 0, 1)[j]][:, rtok], ALU.mult) \
                      .then_inc(sem("mix"), 1)
                wait(dve, "mod_cols", 3 * l + 3)
                for ct in range(KD):
                    dve.wait_ge(sem("out_mm"), KD * l + ct + 1)
                    for s in ((0, 1) if l < L - 1 else (1,)):
                        tok = slice(TC, T) if s else slice(0, TC)
                        ins = nc.vector.scalar_tensor_tensor(out=X[:, ct, tok], in0=bank[(ct + 2) % 4][:, tok],
                                                             scalar=mc[:, l, s, 2 * KD + ct:2 * KD + ct + 1],
                                                             in1=X[:, ct, tok], op0=ALU.mult, op1=ALU.add)
                    ins.then_inc(sem("z"), 1)
                ln_dve(2 * l, LTOK(l))
                if l == 0:
                    modulate(0, 1, 3, 4, (0, 1), ("ln_x", 0), True)
                    def acc(g):
                        for m in range(KD):
                            dve.wait_ge(sem("ffn_y"), KD * g + m + 1)
                            src = bank[4 + m % 4][:]
                            if g == 0:
                                nc.vector.tensor_copy(FACC[:, m], src).then_inc(sem("ffn_acc"), 1)
                            else:
                                if m == 0:
                                    wait(dve, "ffn_acc", KD * g)
                                nc.vector.tensor_tensor(FACC[:, m], FACC[:, m], src, ALU.add).then_inc(sem("ffn_acc"), 1)
                    NG = FF // 256
                    s0 = split_of[("w1", 0, 0)]
                    for key, _ in splits[s0:s0 + 2]:
                        mod_sums(dve, key)
                    for j, ((kind, _, g), _) in enumerate(splits[s0:s0 + 3 * NG]):
                        if kind == "w1":
                            for f in (2 * g, 2 * g + 1):
                                dve.wait_ge(sem("ffn_sig"), f + 1)
                                wait(dve, "ffn_glo", f - 1)
                                nc.vector.tensor_tensor(FP[:, f % 2], FS[:, f % 2], bank[f % 2][:], ALU.mult) \
                                  .then_inc(sem("ffn_s"), 1)
                        elif kind == "w3":
                            for f in (2 * g, 2 * g + 1):
                                dve.wait_ge(sem("ffn_h3"), f + 1)
                                dve.wait_ge(sem("ffn_s"), f + 1)
                                nc.vector.tensor_tensor(FP[:, f % 2], FP[:, f % 2], bank[2 + f % 2][:], ALU.mult) \
                                  .then_inc(sem("ffn_g"), 1)
                            for f in (2 * g, 2 * g + 1):
                                dve.wait_ge(sem("ffn_ghi"), f + 1)
                                nc.vector.tensor_tensor(GL[f % 4], FP[:, f % 2], GH[f % 4], ALU.subtract) \
                                  .then_inc(sem("ffn_glo"), 1)
                            if g in reduce_at:
                                mod_cols(reduce_at[g])
                        else:
                            acc(g)
                        if j + 2 < 3 * NG:
                            mod_sums(dve, splits[s0 + j + 2][0])
                    wait(dve, "ffn_acc", KD * (FF // 256))
                    for m in range(KD):
                        for s in (0, 1):
                            tok = slice(TC, T) if s else slice(0, TC)
                            ins = nc.vector.scalar_tensor_tensor(out=X[:, m, tok], in0=FACC[:, m, tok],
                                                                 scalar=mc[:, 0, s, 5 * KD + m:5 * KD + m + 1],
                                                                 in1=X[:, m, tok], op0=ALU.mult, op1=ALU.add)
                        ins.then_inc(sem("z"), 1)
                    ln_dve(1, slice(0, T))
            moe_dve(dve, ln_dve, modulate, link)

        @block.tensor
        def _(pe):
            mm = nc.tensor.matmul
            pe.wait_ge(sem("consts"), 1)
            pe.wait_ge(sem("c_load"), 32)
            nc.tensor.transpose(bank[5][:, 0:2 * KD], crow, ident[0:2 * KD, 0:2 * KD]).then_inc(sem("c_T"), 1)
            wait(pe, "par_load", 13 * 16)
            nc.tensor.transpose(bank[4][:, 0:P], par_rows, ident).then_inc(sem("par_T"), 1)
            pe.wait_ge(sem("x_load"), 32)
            for k in range(KD):
                wait(pe, "xT_act", k - 3)
                for t in range(NT):
                    ins = nc.tensor.transpose(bank[k % 4][:, t * P:(t + 1) * P], xrows[:, t, k * P:(k + 1) * P], ident)
                ins.then_inc(sem("xT"), 1)
            pe.wait_ge(sem("par"), 1)
            wait(pe, "par_load", 2 * 13 * 16)
            nc.tensor.transpose(bank[4][:, 0:P], par_rows, ident).then_inc(sem("par_T"), 1)

            def mod_first():
                pe.wait_ge(sem("c_silu"), 1)
                for u in range(8):
                    key = ("mod", 0, u)
                    wait_unit(pe, key)
                    wv = slot_view(key)
                    q, half = u % 4, u // 4
                    for k in range(KD):
                        ins = mm(bank[6][32 * q:32 * q + 32, 256 * half:256 * half + 256], cs[:, 2 * k:2 * k + 32], wv[:, k, :],
                                 start=(k == 0), stop=(k == KD - 1))
                    ins.then_inc(sem("mod_mm"), 1)

            def mod_reduce(m):
                wait(pe, "mod_acc", acc_count(m, KD - 1))
                wait(pe, "mod_rows", m)
                for u in range(8):
                    q, half = u % 4, u // 4
                    for s in range(2):
                        ins = mm(bank[6][32 * q:32 * q + 32, 256 * half:256 * half + 256], cs[:, one - s:one - s + 32],
                                 ACC[:, s, 256 * u:256 * (u + 1)], start=(s == 0), stop=(s == 1))
                ins.then_inc(sem("mod_mm"), 1)

            def mod_turn(m):
                pe.wait_ge(sem("mod_rows"), m + 1)
                pe.wait_ge(sem("par"), 2)
                for i in range(4):
                    ins = nc.tensor.transpose(bank[(7, 7, 5)[m % 3]][:, i * P:(i + 1) * P], mrow[:, i * P:(i + 1) * P],
                                              ident)
                ins.then_inc(sem("mod_T"), 1)

            def ln_pe(n, tok):
                for k in range(KD):
                    pe.wait_ge(sem("z"), KD * n + k + 1)
                    ins = mm(bank[4][:, tok], mean_w[:], X[:, k, tok], start=(k == 0), stop=(k == KD - 1))
                ins.then_inc(sem("ln_mean"), 1)
                for k in range(KD):
                    pe.wait_ge(sem("ln_sq"), KD * n + k + 1)
                    mm(bank[5][:, tok], mean_w[:], SQ[:, k % 2, tok], start=(k == 0), stop=(k == KD - 1)) \
                        .then_inc(sem("ln_vmm"), 1)

            mod_first()
            mod_turn(0)
            pe.wait_ge(sem("consts"), 2)
            for l in range(L):
                n_act = 5 * NP + 3
                for ct in range(NCT):
                    key = ("in", l, ct // 2)
                    wait_split(pe, key)
                    wh, wl = split_views(key)
                    tok, col = CTOK(l, ct), slice((ct % 2) * P, (ct % 2 + 1) * P)
                    if ct >= 4:
                        if ct - 4 < n_act:
                            wait(pe, "proj_act", n_act * l + ct - 3)
                        else:
                            wait(pe, "proj_u", NP * l + ct - 3 - n_act)
                    for k in range(KD):
                        if ct == 0:
                            pe.wait_ge(sem("h_lo"), KD * 2 * l + k + 1)
                        ins = three(bank[ct % 4][:, tok], [((wh[:, k, col], wl[:, k, col]), (HH[k][:, tok], HL[k][:, tok]))],
                                    k == 0, k == KD - 1)
                    ins.then_inc(sem("proj_mm"), 1)
                    if (ct - 10) % 3 == 0 and 0 <= (ct - 10) // 3 < NP:
                        j = (ct - 10) // 3
                        pe.wait_ge(sem("kk_sq"), NP * l + j + 1)
                        if j >= 2:
                            wait(pe, "kk_ss", NP * l + j - 1)
                        mm(bank[4 + j % 2][:], heads, tmp_k(j), start=True, stop=True).then_inc(sem("kk_mm"), 1)
                    if l == 0 and ct == 7:
                        mod_reduce(1)
                    if l == 0 and ct == 13:
                        pe.wait_ge(sem("mod_cols"), 1)
                        mod_turn(1)
                if l == 0:
                    mod_reduce(2)
                    pe.wait_ge(sem("mod_rows"), 3)
                pe.wait_ge(sem("lora_load"), 64 * (l + 1))
                pe.wait_ge(sem("proj_u"), NP * (l + 1))
                for i in range(4 * NP):
                    n = 4 * NP * l + i
                    kind, d, j = i // (2 * NP), i // NP % 2, i % NP
                    if i >= 4:
                        wait(pe, "lora_sig", n - 3)
                    mm(bank[i % 4][:], w2z[:, kind, d, j * P:(j + 1) * P], (WD, AD)[kind], start=True, stop=True) \
                        .then_inc(sem("lora_mm"), 1)
                pe.wait_ge(sem("kk_ss"), NP * (l + 1))
                if l == 0:
                    mod_turn(2)
                pe.wait_ge(sem("lora_sig"), 4 * NP * (l + 1))
                for t in range(NT):
                    wait(pe, "vtok", NT * l + t - 1)
                    wait(pe, "proj_act", n_act * l + 3 * NP)
                    for j in range(NP):
                        ins = nc.tensor.transpose(bank[2 + t % 2][:, j * P:(j + 1) * P], V[:, j, t * P:(t + 1) * P],
                                                  ident)
                    ins.then_inc(sem("vT"), 1)
                for st in range(8):
                    d, tj, cn = st // 4, TILE(st), 8 * l + st
                    tok = slice(tj * P, (tj + 1) * P)
                    pe.wait_ge(sem("staged"), cn + 1)
                    pe.wait_ge(sem("zr"), cn + 1)
                    if st == 0:
                        wait(pe, "mod_cols", 3 * l + 3)
                        pe.wait_ge(sem("vtok"), NT * (l + 1))
                    for q in range(2):
                        w, b = wk[q], 4 * q
                        n = 2 * cn + q + 1
                        ny = 2 * ybefore[l, st] + q - 1
                        cols = 4 * P if reads_out(l, st) else 2 * P
                        wait(pe, "dve_yw", ny)
                        wait(pe, "act_yw", ny)
                        wait(pe, "act_gt", n - 2)
                        for p in range(2):
                            ins = mm(bank[b + p][:, 0:cols], BS[:, 2 * q + p],
                                     ZR[:, 2 * q + p].rearrange("p a n -> p (a n)")[:, 0:cols], start=True, stop=True)
                        ins.then_inc(sem("pe_s1"), 1)
                        wait(pe, "y_done", ny)
                        wait(pe, "state_done", n - 2)
                        for p in range(2):
                            ins = mm(bank[b + 2 + p][:, 0:cols], KS[:, 2 * q + p],
                                     ZR[:, 2 * q + p].rearrange("p a n -> p (a n)")[:, 0:cols], start=True, stop=True)
                        ins.then_inc(sem("pe_s2"), 1)
                    for q in range(2):
                        w, b = wk[q], 4 * q
                        n = 2 * cn + q + 1
                        wait(pe, "dve_lt", n)
                        if reads_out(l, st):
                            pe.wait_ge(sem("dve_rb"), 2 * ybefore[l, st] + q + 1)
                        for i, s in enumerate((AS, AS, BS, BS)):
                            ins = nc.tensor.transpose(pk(b, 4, P)[:, i], s[:, 2 * q + i % 2], ident)
                        ins.then_inc(sem("pe_tab"), 1)
                        for i in range(2):
                            ins = nc.tensor.transpose(pk(b + 1, 4, P)[:, i], KS[:, 2 * q + i], ident)
                        ins.then_inc(sem("pe_tk"), 1)
                    for q in range(2):
                        w, b = wk[q], 4 * q
                        n = 2 * cn + q + 1
                        wait(pe, "dve_ak", n)
                        wait(pe, "t0_done", n)
                        for i in range(4):
                            ins = nc.tensor.transpose(pk(b + 2, 4, P)[:, i], w["TT"][:, i], ident)
                        ins.then_inc(sem("pe_t1"), 1)
                    for q in range(2):
                        w, b = wk[q], 4 * q
                        n = 2 * cn + q + 1
                        pe.wait_ge(sem("vs"), cn + 1)
                        for i in range(4):
                            ins = mm(pk(b + 3, 4, P)[:, i], w["AK"][:, i], VS[:, 2 * q + i // 2], start=True, stop=True)
                        ins.then_inc(sem("pe_ax"), 1)
                    qr, qc = quadrant(d)
                    for k in range(6):
                        for q in range(2):
                            w, b = wk[q], 4 * q
                            n = 2 * cn + q + 1
                            pe.wait_ge(sem("pool_lm"), (6 * cn + k) * 2 + q + 1)
                            if k == 0:
                                wait(pe, "act_tab", n)
                                wait(pe, "act_t1", n)
                            else:
                                wait(pe, "dve_t", (5 * cn + k - 1) * 2 + q + 1)
                            for i in range(4):
                                if k < 5:
                                    ins = mm(pk(b, 4, P)[:, i], w["LM"][:, k % 2, i], w["T"][:, i],
                                             start=True, stop=True)
                                else:
                                    ins = mm(pk(b, 4, P)[qr, i, qc], w["LM"][:, k % 2, i, qr], w["T"][:, i, qc],
                                             start=True, stop=True)
                            ins.then_inc(sem("pe_x"), 1)
                        for q in range(2):
                            w, b = wk[q], 4 * q
                            n = 2 * cn + q + 1
                            pe.wait_ge(sem("act_xs"), (6 * cn + k) * 2 + q + 1)
                            if k == 0:
                                wait(pe, "act_tk", n)
                            else:
                                wait(pe, "dve_tt", (6 * cn + k - 1) * 2 + q + 1)
                            if k < 5:
                                for i in range(4):
                                    ins = mm(pk(b + 1, 4, P)[:, i], w["TT"][:, i], w["XS"][:, i], start=True, stop=True)
                                ins.then_inc(sem("pe_u1"), 1)
                            for i in range(4):
                                if k < 5:
                                    ins = mm(pk(b + 2, 4, P)[:, i], w["XS"][:, i], w["TT"][:, i],
                                             start=True, stop=True)
                                else:
                                    ins = mm(pk(b + 2, 4, P)[qc, i, qr], w["XS"][:, i, qc], w["TT"][:, i, qr],
                                             start=True, stop=True)
                            ins.then_inc(sem("pe_u2"), 1)
                    for q in range(2):
                        w, b = wk[q], 4 * q
                        n = 2 * cn + q + 1
                        pe.wait_ge(sem("dve_tt"), (6 * cn + 5) * 2 + q + 1)
                        wait(pe, "act_ax", n)
                        for i in range(4):
                            ins = mm(pk(b + 3, 4, P)[:, i], w["TT"][:, i], w["XA"][:, i], start=True, stop=True)
                        ins.then_inc(sem("pe_uw"), 1)
                    for q in range(2):
                        w, b = wk[q], 4 * q
                        n = 2 * cn + q + 1
                        wait(pe, "act_uw", n)
                        wof, uof = (0, 64), (64, 0)
                        for i in range(4):
                            p, h = i // 2, i % 2
                            ins = mm(bank[b + 1][64 * h:64 * h + 64, HS * p:HS * p + HS],
                                     w["UW"][:, i, wof[h]:wof[h] + 64], w["BT"][:, p, 64 * h:64 * h + 64],
                                     start=True, stop=True)
                        ins.then_inc(sem("pe_gt"), 1)
                        for i in range(4 if reads_out(l, st) else 0):
                            p, h = i // 2, i % 2
                            mm(pk(b, 4, P)[:, i], w["UW"][:, i], w["RB"][:, i], start=True, stop=False,
                               skip_group_check=True)
                            ins = mm(pk(b, 4, P)[64 - 64 * h:128 - 64 * h, i], VS[:, 2 * q + p, 64 * h:64 * h + 64],
                                     w["RK"][:, i], start=False, stop=True, skip_group_check=True)
                        if reads_out(l, st):
                            ins.then_inc(sem("pe_yw"), 1)
                    for q in range(2):
                        w, b = wk[q], 4 * q
                        n = 2 * cn + q + 1
                        ny = 2 * ybefore[l, st] + q + 1
                        if reads_out(l, st):
                            wait(pe, "dve_yw", ny)
                            wait(pe, "act_yw", ny)
                        wait(pe, "state_done", n - 2)
                        for i in range(4 if reads_out(l, st) else 0):
                            p, h = i // 2, i % 2
                            ins = mm(bank[b + 2][64 * h:64 * h + 64, P * p:P * (p + 1)], MI[:, 4 * q + i], w["YW"][:, i],
                                     start=True, stop=True)
                        if reads_out(l, st):
                            ins.then_inc(sem("pe_y"), 1)
                        wait(pe, "act_gt", n)
                        for i in range(4):
                            p, h = i // 2, i % 2
                            o_ = bank[b + 3][64 * h:64 * h + 64, HS * p:HS * p + HS]
                            mm(o_, w["BT"][:, p, 64 * h:64 * h + 64], w["UW"][:, i, uof[h]:uof[h] + 64],
                               start=True, stop=False)
                            mm(o_, w["KT"][:, p, 64 * h:64 * h + 64], VS[:, 2 * q + p, 64 * h:64 * h + 64],
                               start=False, stop=False)
                            ins = mm(o_, w["GT"][64 * h:64 * h + 64, p], MC[64 * h:64 * h + 64, 2 * q + p],
                                     start=False, stop=True)
                        ins.then_inc(sem("pe_m"), 1)
                rtok = LTOK(l)
                pe.wait_ge(sem("y_done"), YTOT[l])
                pe.wait_ge(sem("state_done"), 16 * (l + 1))
                for j in range(NP):
                    if j >= 2:
                        wait(pe, "gn_d", NP * l + j - 1)
                    mm(bank[j % 2][:, rtok], heads, Y[:, j, rtok], start=True, stop=True).then_inc(sem("gn_mm"), 1)
                for j in range(NP):
                    pe.wait_ge(sem("gn_sq"), NP * l + j + 1)
                    if j >= 2:
                        wait(pe, "gn_ve", NP * l + j - 1)
                    mm(bank[2 + j % 2][:, rtok], heads, RSQ[:, j, rtok], start=True, stop=True).then_inc(sem("gn_vmm"), 1)
                pe.wait_ge(sem("g2_load"), 16 * (l + 1))
                pe.wait_ge(sem("gn_d"), NP * (l + 1))
                for j in range(NP):
                    mm(bank[(6, 7, 0, 1)[j]][:, rtok], g2[:, j * P:(j + 1) * P], GD[:, rtok], start=True, stop=True) \
                        .then_inc(sem("gate_mm"), 1)
                for j in range(NP):
                    pe.wait_ge(sem("bonus_in"), NP * l + j + 1)
                    if j >= 2:
                        wait(pe, "mix", NP * l + j - 1)
                    mm(bank[4 + j % 2][:, rtok], heads, RTB[:, j, rtok], start=True, stop=True) \
                        .then_inc(sem("bonus_mm"), 1)
                pe.wait_ge(sem("gn_ve"), NP * (l + 1))
                pe.wait_ge(sem("xa"), 2 * l + 1)
                for ct in range(KD):
                    key = ("out", l, ct // 2)
                    wait_split(pe, key)
                    wh, wl = split_views(key)
                    col = slice((ct % 2) * P, (ct % 2 + 1) * P)
                    if ct >= 4:
                        wait(pe, "z", 2 * KD * l + ct - 3)
                    for i in range(KD):
                        k = (NP + i) % KD
                        if ct == 0:
                            pe.wait_ge(sem("mix_lo"), KD * l + i + 1)
                        ins = three(bank[(ct + 2) % 4][:, rtok], [((wh[:, k, col], wl[:, k, col]), (HH[k][:, rtok], HL[k][:, rtok]))],
                                    i == 0, i == KD - 1)
                    ins.then_inc(sem("out_mm"), 1)
                ln_pe(2 * l, LTOK(l))
                if l == 0:
                    NG = FF // 256
                    s0 = split_of[("w1", 0, 0)]
                    for key, _ in splits[s0:s0 + 3 * NG]:
                        kind, _, g = key
                        wait_split(pe, key)
                        wh, wl = split_views(key)
                        if kind == "w2":
                            wait(pe, "ffn_glo", 2 * g + 2)
                            if g + 1 in reduce_at:
                                pe.wait_ge(sem("mod_cols"), reduce_at[g + 1] + 1)
                            for m in range(KD):
                                wait(pe, "ffn_acc", KD * g + m - 3)
                                col = slice(m * P, (m + 1) * P)
                                three(bank[4 + m % 4][:], [((wh[:, i, col], wl[:, i, col]),
                                                            (GH[(2 * g + i) % 4], GL[(2 * g + i) % 4]))
                                                           for i in range(2)]).then_inc(sem("ffn_y"), 1)
                            continue
                        b, done = (0, "ffn_h1") if kind == "w1" else (2, "ffn_h3")
                        for f in (2 * g, 2 * g + 1):
                            wait(pe, "ffn_s" if kind == "w1" else "ffn_g", f - 1)
                            col = slice((f % 2) * P, (f % 2 + 1) * P)
                            for k in range(KD):
                                if kind == "w1" and f == 0:
                                    pe.wait_ge(sem("h_lo"), KD + k + 1)
                                ins = three(bank[b + f % 2][:], [((wh[:, k, col], wl[:, k, col]), (HH[k], HL[k]))],
                                            k == 0, k == KD - 1)
                            ins.then_inc(sem(done), 1)
                        if g in reduce_at and kind == "w1":
                            wait(pe, "ffn_acc", KD * (g - 1))
                            mod_reduce(reduce_at[g])
                        elif g in reduce_at:
                            mod_turn(reduce_at[g])
                    ln_pe(1, slice(0, T))
            moe_pe(pe, ln_pe)


_INS = ["x", "c", "ctx", "c_ctx", "w_mod", "b_mod", "w_in", "rk_w0", "rk_w2", "rk_a0", "rk_a2", "rk_kk", "rk_ka", "rk_rk",
        "rk_g2", "rk_lnx_g", "rk_lnx_b", "conv_w", "w_out", "ln1_g", "ln1_b", "ln2_g", "ln2_b", "ffn_w1", "ffn_w3",
        "ffn_w2", "router_w", "router_b", "moe_w1", "moe_w3", "moe_w2"]


def kernel(**inputs):
    import numpy as _np
    import concourse.bacc as _bacc
    from concourse import mybir as _mybir
    from concourse.bass_utils import run_bass_kernel_spmd as _run

    nc = _bacc.Bacc("TRN2", target_bir_lowering=False, num_devices=1)
    arrays, args = {}, []
    for name in _INS:
        a = _np.ascontiguousarray(inputs[name])
        arrays[f"in_{name}_dram"] = a
        args.append(nc.dram_tensor(f"in_{name}_dram", a.shape, _mybir.dt.from_np(a.dtype), kind="ExternalInput").ap())
    shape = inputs["x"].shape
    args.append(nc.dram_tensor("out_dram", shape, _mybir.dt.float32, kind="ExternalOutput").ap())
    hybrid_kernel(nc, *args)
    r = _run(nc, [arrays], core_ids=[0])
    return r.results[0]["out_dram"]
```
